# Optimizing a Trainium2 kernel written in Bass

```python
import jax
import jax.numpy as jnp
from jax import lax
import numpy as np

D_MODEL = 1024
BATCH = 1
SEQ = 256
DEPTH = 2
DEC_BATCH = 8
DEC_SEQ = 16
PAST_LEN = 512

CHUNK = 64
N_MIXERS = 2
N_GLA = (DEPTH + 1) // 2
N_SGU = DEPTH // 2
GLA_HEADS = 4
GLA_KEY = D_MODEL // 2
GLA_VAL = D_MODEL
GLA_DK = GLA_KEY // GLA_HEADS
GLA_DV = GLA_VAL // GLA_HEADS
GLA_GATE_RANK = 16
GLA_TAU = 16.0
GLA_IN = 2 * GLA_KEY + 2 * GLA_VAL + GLA_GATE_RANK
SGU_CHUNK = 128
SGU_GROUPS = 4
SGU_HALF = 3 * D_MODEL
SGU_GROUP_DIM = SGU_HALF // SGU_GROUPS
D_FF = 4 * D_MODEL
NORM_EPS = 1e-6
LN_EPS = 1e-5

kernel_name = "gla_sgu_macaron_stream_step"

def rms_norm(x, g):
    xf = x.astype(jnp.float32)
    y = xf * lax.rsqrt(jnp.mean(xf * xf, axis=-1, keepdims=True) + NORM_EPS)
    return (y * g.astype(jnp.float32)).astype(x.dtype)

def layer_norm(x, g, b):
    xf = x.astype(jnp.float32)
    mu = jnp.mean(xf, axis=-1, keepdims=True)
    xc = xf - mu
    y = xc * lax.rsqrt(jnp.mean(xc * xc, axis=-1, keepdims=True) + LN_EPS)
    return (y * g.astype(jnp.float32) + b.astype(jnp.float32)).astype(x.dtype)

def swiglu_ffn(x, w_gate, w_up, w_down):
    return (jax.nn.silu(x @ w_gate) * (x @ w_up)) @ w_down

def gla_chunk(S, chunk):
    q, k, v, g = chunk
    b = jnp.cumsum(g, axis=1)
    b_last = b[:, -1]
    qf = q.astype(jnp.float32)
    kf = k.astype(jnp.float32)
    vf = v.astype(jnp.float32)
    qg = qf * jnp.exp(b)
    kg = kf * jnp.exp(-b)
    kd = kf * jnp.exp(b_last[:, None] - b)
    L = q.shape[1]
    mask = jnp.tril(jnp.ones((L, L), dtype=bool))
    A = jnp.where(mask, jnp.einsum('bthd,bshd->bhts', qg, kg), 0.0)
    o = jnp.einsum('bhts,bshv->bthv', A, vf) + jnp.einsum('bthd,bhdv->bthv', qg, S)
    S_new = jnp.exp(b_last)[..., None] * S + jnp.einsum('bshd,bshv->bhdv', kd, vf)
    return S_new, o

def gla_mixer(x, S0, w_in, w_gate2, b_gate, g_norm, w_out):
    B, T, _ = x.shape
    L = min(T, CHUNK)
    N = T // L
    h = x @ w_in
    q, k, v, r, zg = jnp.split(
        h, [GLA_KEY, 2 * GLA_KEY, 2 * GLA_KEY + GLA_VAL, 2 * GLA_KEY + 2 * GLA_VAL], axis=-1)
    g = jax.nn.log_sigmoid((zg @ w_gate2 + b_gate).astype(jnp.float32)) / GLA_TAU
    q = q * (GLA_DK ** -0.5)

    def heads(t, d):
        return jnp.moveaxis(t.reshape(B, N, L, GLA_HEADS, d), 1, 0)

    S, o = lax.scan(gla_chunk, S0.astype(jnp.float32),
                    (heads(q, GLA_DK), heads(k, GLA_DK), heads(v, GLA_DV), heads(g, GLA_DK)))
    o = jnp.moveaxis(o, 0, 1).reshape(B, T, GLA_HEADS, GLA_DV)
    o = rms_norm(o, g_norm).astype(x.dtype).reshape(B, T, GLA_VAL)
    y = (o * jax.nn.silu(r)) @ w_out
    return y, S

def sgu_mixer(x, w_in, b_in, ln_g, ln_b, w_s, b_s, w_out):
    B, T, _ = x.shape
    L = min(T, SGU_CHUNK)
    N = T // L
    z = jax.nn.gelu(x @ w_in + b_in, approximate=False)
    u, v = jnp.split(z, 2, axis=-1)
    v = layer_norm(v, ln_g, ln_b)
    w = jnp.tril(w_s[:, :L, :L])
    vg = v.reshape(B, N, L, SGU_GROUPS, SGU_GROUP_DIM)
    mixed = jnp.einsum('gts,bnsgc->bntgc', w, vg) + b_s[:, :L].T[:, :, None]
    y = (u * mixed.reshape(B, T, SGU_HALF)) @ w_out
    return y, v

def setup_inputs(seed: int = 0) -> dict:
    key = jax.random.key(seed)
    ks = jax.random.split(key, 24)
    D = D_MODEL

    def nrm(k, shape, scale):
        return jax.random.normal(k, shape, jnp.float32) * scale

    return {
        "x_prompt": nrm(ks[0], (BATCH, SEQ, D), 1.0),
        "x_sample": nrm(ks[1], (DEC_BATCH, DEC_SEQ, D), 1.0),
        "state_gla": nrm(ks[2], (N_GLA, DEC_BATCH, GLA_HEADS, GLA_DK, GLA_DV), 1.0),
        "norm_pre": 1.0 + nrm(ks[3], (DEPTH, 3, D), 0.05),
        "norm_post": 1.0 + nrm(ks[4], (DEPTH, 3, D), 0.05),
        "ffn_w_gate": nrm(ks[5], (DEPTH, 2, D, D_FF), D ** -0.5),
        "ffn_w_up": nrm(ks[6], (DEPTH, 2, D, D_FF), D ** -0.5),
        "ffn_w_down": nrm(ks[7], (DEPTH, 2, D_FF, D), D_FF ** -0.5),
        "gla_w_in": nrm(ks[8], (N_GLA, D, GLA_IN), D ** -0.5),
        "gla_w_gate2": nrm(ks[9], (N_GLA, GLA_GATE_RANK, GLA_KEY), GLA_GATE_RANK ** -0.5),
        "gla_b_gate": nrm(ks[10], (N_GLA, GLA_KEY), 0.1),
        "gla_norm": 1.0 + nrm(ks[11], (N_GLA, GLA_DV), 0.05),
        "gla_w_out": nrm(ks[12], (N_GLA, GLA_VAL, D), GLA_VAL ** -0.5),
        "sgu_w_in": nrm(ks[13], (N_SGU, D, 2 * SGU_HALF), D ** -0.5),
        "sgu_b_in": nrm(ks[14], (N_SGU, 2 * SGU_HALF), 0.02),
        "sgu_ln_g": 1.0 + nrm(ks[15], (N_SGU, SGU_HALF), 0.05),
        "sgu_ln_b": nrm(ks[16], (N_SGU, SGU_HALF), 0.02),
        "sgu_w_s": nrm(ks[17], (N_SGU, SGU_GROUPS, SGU_CHUNK, SGU_CHUNK), SGU_CHUNK ** -0.5),
        "sgu_b_s": 1.0 + nrm(ks[18], (N_SGU, SGU_GROUPS, SGU_CHUNK), 0.05),
        "sgu_w_out": nrm(ks[19], (N_SGU, SGU_HALF, D), SGU_HALF ** -0.5),
    }

def reference(x_prompt, x_sample, state_gla, norm_pre, norm_post, ffn_w_gate, ffn_w_up,
              ffn_w_down, gla_w_in, gla_w_gate2, gla_b_gate, gla_norm, gla_w_out,
              sgu_w_in, sgu_b_in, sgu_ln_g, sgu_ln_b, sgu_w_s, sgu_b_s, sgu_w_out):

    def block(x, s0, i):
        j = i // N_MIXERS
        h = swiglu_ffn(rms_norm(x, norm_pre[i, 0]), ffn_w_gate[i, 0], ffn_w_up[i, 0], ffn_w_down[i, 0])
        x = x + 0.5 * rms_norm(h, norm_post[i, 0])
        hn = rms_norm(x, norm_pre[i, 1])
        if i % N_MIXERS == 0:
            h, st = gla_mixer(hn, s0, gla_w_in[j], gla_w_gate2[j], gla_b_gate[j], gla_norm[j], gla_w_out[j])
        else:
            h, st = sgu_mixer(hn, sgu_w_in[j], sgu_b_in[j], sgu_ln_g[j], sgu_ln_b[j],
                              sgu_w_s[j], sgu_b_s[j], sgu_w_out[j])
        x = x + rms_norm(h, norm_post[i, 1])
        h = swiglu_ffn(rms_norm(x, norm_pre[i, 2]), ffn_w_gate[i, 1], ffn_w_up[i, 1], ffn_w_down[i, 1])
        x = x + 0.5 * rms_norm(h, norm_post[i, 2])
        return x, st

    xp, xs = x_prompt, x_sample
    gla_p, gla_s, sgu_s = [], [], []
    for i in range(DEPTH):
        j = i // N_MIXERS
        if i % N_MIXERS == 0:
            s0_p = jnp.zeros((xp.shape[0], GLA_HEADS, GLA_DK, GLA_DV), jnp.float32)
            xp, sp = block(xp, s0_p, i)
            xs, ss = block(xs, state_gla[j], i)
            gla_p.append(sp.astype(x_prompt.dtype))
            gla_s.append(ss.astype(x_sample.dtype))
        else:
            xp, _ = block(xp, None, i)
            xs, vs = block(xs, None, i)
            sgu_s.append(vs)

    gla_state_prompt = jnp.stack(gla_p)
    gla_state_sample = jnp.stack(gla_s)
    sgu_v_sample = jnp.stack(sgu_s)
    return (xp, xs, gla_state_prompt, gla_state_sample, sgu_v_sample)


_drawn_inputs = setup_inputs


def setup_inputs(seed=0):
    import zlib

    import numpy as np

    out = dict(_drawn_inputs(seed))
    spreads = {}
    factors = {'sgu_ln_b': 2.861, 'sgu_b_s': 2.933}
    for name, (base, spread) in spreads.items():
        noise = np.random.default_rng([zlib.crc32(name.encode()), seed]).standard_normal(out[name].shape)
        drawn = base * np.exp(spread * noise) if base else spread * noise
        out[name] = jnp.asarray(drawn.astype(out[name].dtype))
    for name, factor in factors.items():
        out[name] = (out[name] * factor).astype(out[name].dtype)
    return out
```

```python
from contextlib import ExitStack

import concourse.bass as bass
from concourse import mybir

F32 = mybir.dt.float32
F32R = mybir.dt.float32r
U32 = mybir.dt.uint32
ALU = mybir.AluOpType
ACT = mybir.ActivationFunctionType

P = 128
WIDE = 256
KT = 8
BANK = 512
RMS_EPS = 1e-6


def build_trunk(nc, a, outs, plan):
    seq, D = a["x_prompt"].shape[1:]
    dec_batch, dec_seq = a["x_sample"].shape[:2]
    NP = seq // P
    NT = NP + 1
    TOK = NT * P
    DK = D // P
    FF = a["ffn_w_gate"].shape[-1]
    FK = FF // P
    assert dec_batch * dec_seq == P and DK == KT and TOK <= BANK

    FFN_CHUNKS = 2 * FF // WIDE + FF // (P * KT) * (D // WIDE)
    DOWN_STEPS = FK // KT
    QUARTERS = D // WIDE

    HEADS, DH, DV = a["state_gla"].shape[2:]
    VT = DV // P
    RANK = a["gla_w_gate2"].shape[1]
    GLA_TAU = 16.0
    GCH = 64
    assert DH == P and DV == WIDE and HEADS * DV == D and dec_seq <= GCH
    Q_CHUNKS = HEADS * DH // WIDE
    V_TILE = 4 * Q_CHUNKS
    R_TILE = V_TILE + HEADS * NT
    R_AT = 2 * Q_CHUNKS + HEADS
    OUT_AT = R_AT + HEADS
    DEC_BANKS = (3, 7, 2, 3)
    GLA_CHUNKS = OUT_AT + QUARTERS

    HALF = a["sgu_ln_g"].shape[1]
    SPATIAL = a["sgu_w_s"].shape[1]
    LN_EPS = 1e-5
    V_CHUNKS = HALF // WIDE
    SGU_STEPS = HALF // (P * KT)
    SGU_CHUNKS = 2 * V_CHUNKS + SGU_STEPS * QUARTERS
    U_TILE = NT * V_CHUNKS
    SGU_OUT_TILE = U_TILE + HALF // P
    PER_SET = KT * P // WIDE
    assert a["sgu_w_s"].shape[2] == P

    chunk0, tile0, stat0, pre0, ff0 = [0], [0], [0], [0], [0]
    for kind, layer, which in plan:
        chunks, tiles, stats, kept, ff = {
            "ffn": (FFN_CHUNKS, 2 * FK + DK, 2, 1, FK),
            "sgu": (SGU_CHUNKS, SGU_OUT_TILE + DK, 2, 1, 0),
            "gla": (GLA_CHUNKS, 2 * HEADS * 2 + NT * HEADS + DK, 2 + HEADS, 1, 0),
        }[kind]
        for start, size in ((chunk0, chunks), (tile0, tiles), (stat0, stats), (pre0, kept), (ff0, ff)):
            start.append(start[-1] + size)
    CHUNKS = chunk0[-1]

    xp = a["x_prompt"].rearrange("b (t p) d -> p (b t) d", p=P)
    xs = a["x_sample"].rearrange("b l d -> (b l) d")
    yp = outs["y_prompt"].rearrange("b (t p) d -> p (b t) d", p=P)
    ys = outs["y_sample"].rearrange("b l d -> (b l) d")

    with ExitStack() as ctx:
        def sb(name, shape, dt=F32):
            return ctx.enter_context(nc.sbuf_tensor(name + "_sb", shape, dt))

        def shared(*wanted):
            with ExitStack() as scope:
                return [scope.enter_context(nc.sbuf_tensor(name + "_sb", shape, dt))
                        for name, shape, dt in wanted]

        def sem(name):
            return ctx.enter_context(nc.semaphore(name))

        ident_tri = sb("ident_tri", [P, 4, P])
        ident, tri_gla, tri_dec = ident_tri[:, 0, :], ident_tri[:, 2, :], ident_tri[:, 3, :]
        tri_tok = [tri_gla] * NP + [tri_dec]
        pair_mask = sb("pair_mask", [P, 2])
        ones = sb("ones", [P, P])
        g_pre = sb("g_pre", [P, 2 * 3 * DK])
        g_post = sb("g_post", [P, 2 * 3 * DK])
        g_head = sb("g_head", [P, VT])
        u_bias = sb("u_bias", [P, 2 * HALF // P])
        x = sb("x", [P, DK, TOK])
        xhi = sb("xhi", [P, DK, TOK], F32R)
        xlo = sb("xlo", [P, DK, TOK], F32R)
        yg = sb("yg", [P, DK, TOK])
        raw = sb("raw", [P, 2, KT, WIDE])
        whi = sb("whi", [P, 2, KT, WIDE], F32R)
        wlo = sb("wlo", [P, 2, KT, WIDE], F32R)
        sq = sb("sq", [P, 2, TOK])
        acc = sb("acc", [P, TOK])
        mean_sq = sb("mean_sq", [P, NT])
        rstd = sb("rstd", [P, 2, NT])
        minus_half = sb("minus_half", [P, NT])
        diag = acc
        r_pre = sb("r_pre", [P, TOK])

        hhi, hlo, h_gate, h_up = shared(
            ("hhi", [P, FK, TOK], F32R), ("hlo", [P, FK, TOK], F32R),
            ("h_gate", [P, 2, TOK], F32), ("h_up", [P, 2, TOK], F32))
        (qk, log_g, e_neg, e_pos, k_dec, v_rows, s0, olo, k_rows, scores, v_pair, s_prompt, ot, z_rows, z_cols,
         wz, w_gate2, wz_hi, wz_lo) = shared(
            ("qk", [P, HEADS, 2, TOK], F32), ("log_g", [P, HEADS * TOK], F32), ("e_neg", [P, HEADS, TOK], F32),
            ("e_pos", [P, HEADS, TOK], F32), ("k_dec", [P, HEADS, TOK], F32), ("v_rows", [P, NT, D], F32),
            ("s0", [P, 2, dec_batch, DV], F32), ("olo", [P, HEADS * VT, TOK], F32R), ("k_rows", [P, TOK], F32),
            ("scores", [P, TOK], F32), ("v_pair", [P, 2, DV], F32), ("s_prompt", [P, seq // GCH, DV], F32),
            ("ot", [P, VT, TOK], F32), ("z_rows", [P, NT, RANK], F32), ("z_cols", [32, TOK], F32),
            ("wz", [P, KT, RANK], F32), ("w_gate2", [RANK + 1, HEADS * DH], F32),
            ("wz_hi", [P, KT, RANK], F32R), ("wz_lo", [P, KT, RANK], F32R))
        log_g_rows = log_g[:, :].rearrange("p (t f) -> p t f", t=NT)
        b_cum = log_g[:, :].rearrange("p (h t) -> p h t", h=HEADS)
        ohi, r_silu = shared(("ohi", [P, HEADS * VT, TOK], F32R), ("r_silu", [P, HEADS * VT, TOK], F32))
        set_rows = [P, NT, KT * P]
        (v0, v1, v2, uhi0, uhi1, uhi2, ulo0, feat_rows, w_turned, b_spatial, u_tile, mixed, ln_stats, ln_mean_var,
         ln_var, ln_rstd) = shared(
            ("v0", set_rows, F32), ("v1", set_rows, F32), ("v2", set_rows, F32),
            ("uhi0", [P, KT, TOK], F32R), ("uhi1", [P, KT, TOK], F32R), ("uhi2", [P, KT, TOK], F32R),
            ("ulo0", [P, KT, TOK], F32R), ("feat_rows", [P, 2, 2, WIDE], F32),
            ("w_turned", [P, 2, SPATIAL, P], F32), ("b_spatial", [P, SPATIAL, P], F32), ("u_tile", [P, 2, TOK], F32),
            ("mixed", [P, 2, TOK], F32), ("ln_stats", [P, NT, V_CHUNKS, 6], F32), ("ln_mean_var", [P, NT, 2], F32),
            ("ln_var", [P, NT], F32), ("ln_rstd", [P, NT], F32))
        ulo1, ulo2, w_rows = shared(("ulo1", [P, KT, TOK], F32R), ("ulo2", [P, KT, TOK], F32R),
                                    ("w_rows", [P, 2, SPATIAL, P], F32))
        v_set, uhi, ulo = [v0, v1, v2], [uhi0, uhi1, uhi2], [ulo0, ulo1, ulo2]
        assert SGU_STEPS == len(v_set)
        y_rows, = shared(("y_rows", [P, NT, D], F32))
        x_rows = yg[:, :, :].rearrange("p k t -> p (k t)").rearrange("p (n d) -> p n d", n=NT)

        banks = [ctx.enter_context(nc.psum_tensor(f"bank{i}", [P, BANK], F32)) for i in range(8)]
        proj = banks[:4]
        NPROJ = len(proj)
        stat = banks[4]

        const_in = sem("const_in")
        x_in = sem("x_in")
        landed = [sem(f"landed{i}") for i in range(2)]
        w_hi = sem("w_hi")
        w_lo = sem("w_lo")
        w_used = sem("w_used")
        y_first = sem("y_first")
        tile_out = sem("tile_out")
        consts_ready = sem("consts_ready")
        xt_ready = sem("xt_ready")
        x_new = sem("x_new")
        x_hi = sem("x_hi")
        x_lo = sem("x_lo")
        x_sq = sem("x_sq")
        x_acc = sem("x_acc")
        y_sq = sem("y_sq")
        y_gain = sem("y_gain")
        y_acc = sem("y_acc")
        y_scaled = sem("y_scaled")
        sums_ready = sem("sums_ready")
        mean_ready = sem("mean_ready")
        rstd_ready = sem("rstd_ready")
        diag_ready = sem("diag_ready")
        factor_ready = sem("factor_ready")
        factor_read = sem("factor_read")
        silu_ready = sem("silu_ready")
        prod_ready = sem("prod_ready")
        h_hi = sem("h_hi")
        h_lo = sem("h_lo")
        gla_in = sem("gla_in")
        s0_in = [sem(f"s0_in{i}") for i in range(2)]
        s0_stored = [sem(f"s0_stored{i}") for i in range(2)]
        sp_stored = sem("sp_stored")
        wz_split = sem("wz_split")
        z_mm = sem("z_mm")
        z_evac = sem("z_evac")
        z_turned = sem("z_turned")
        g_abs = sem("g_abs")
        g_exp = sem("g_exp")
        g_log = sem("g_log")
        g_done = sem("g_done")
        b_copied = sem("b_copied")
        b_exp = sem("b_exp")
        b_diff = sem("b_diff")
        d_exp = sem("d_exp")
        k_decayed = sem("k_decayed")
        qk_ready = sem("qk_ready")
        qk_out = sem("qk_out")
        scores_mm = sem("scores_mm")
        k_turned = sem("k_turned")
        scores_out = sem("scores_out")
        k_out = sem("k_out")
        kv_mm = sem("kv_mm")
        s_done = sem("s_done")
        inter_mm = sem("inter_mm")
        o_mm = sem("o_mm")
        dec_mm = sem("dec_mm")
        dec_done = sem("dec_done")
        vp_done = sem("vp_done")
        o_sq = sem("o_sq")
        o_out = sem("o_out")
        o_acc = sem("o_acc")
        o_scaled = sem("o_scaled")
        o_gated = sem("o_gated")
        o_hi = sem("o_hi")
        o_lo = sem("o_lo")
        r_silu_done = sem("r_silu_done")
        ws_zero = sem("ws_zero")
        ws_in = sem("ws_in")
        ws_mm = sem("ws_mm")
        ws_done = sem("ws_done")
        rows_in = [sem(f"rows_in{i}") for i in range(2)]
        v_act = sem("v_act")
        v_stat = sem("v_stat")
        ln_aggr = sem("ln_aggr")
        ln_eps = sem("ln_eps")
        ln_pow = sem("ln_pow")
        ln_norm = sem("ln_norm")
        ln_gain = sem("ln_gain")
        ln_done = sem("ln_done")
        v_stored = sem("v_stored")
        mix_mm = sem("mix_mm")
        mix_out = sem("mix_out")
        u_act = sem("u_act")
        u_prod = sem("u_prod")
        u_hi = sem("u_hi")
        u_lo = sem("u_lo")
        yt_ready = sem("yt_ready")
        yt_out = sem("yt_out")
        stored = sem("stored")

        block = ctx.enter_context(nc.Block())

        def v_at(i, t):
            at = i % PER_SET * WIDE
            return v_set[i // PER_SET][:, t, at:at + WIDE]

        def gain(g, b, k):
            kind, layer, which = plan[b]
            return g[:, bass.ds((layer * 3 + which) * DK + k, 1)]

        def pairs_of_groups(eng, group, unroll):
            if unroll:
                for q in range(QUARTERS):
                    group(q, q % 2)
                return
            with eng.Fori(0, QUARTERS // 2) as it:
                for parity in range(2):
                    group(2 * it + parity, parity)

        @block.sync
        def _(sp):
            sp.dma_start(x_rows[:, 0:NP, :], xp).then_inc(x_in, 16)
            sp.dma_start(x_rows[:, NP, :], xs).then_inc(x_in, 16)
            sp.dma_start(ident_tri[:, :, :], a["ident_tri"]).then_inc(const_in, 16)
            sp.dma_start(pair_mask[:, :], a["pair_mask"]).then_inc(const_in, 16)
            sp.dma_start(g_pre[:, :], a["gain_pre"]).then_inc(const_in, 16)
            sp.dma_start(g_post[:, :], a["gain_post"]).then_inc(const_in, 16)
            sp.dma_start(g_head[:, :], a["gain_head"]).then_inc(const_in, 16)
            sp.dma_start(u_bias[:, :], a["u_bias"]).then_inc(const_in, 16)

            def load(n, src, slot, first=False):
                if not first:
                    sp.wait_ge(w_lo, n - 1)
                sp.dma_start(raw[:, slot], src).then_inc(landed[slot], 16)

            def by_k(w):
                return w.rearrange("(k p) c -> p k c", p=P)

            for b, (kind, layer, which) in enumerate(plan):
                n0 = chunk0[b]
                if kind == "ffn":
                    i = which // 2
                    gate, up = by_k(a["ffn_w_gate"][layer, i]), by_k(a["ffn_w_up"][layer, i])
                    down = by_k(a["ffn_w_down"][layer, i])
                    load(n0, gate[:, :, 0:WIDE], 0, b == 0)
                    load(n0 + 1, up[:, :, 0:WIDE], 1, b == 0)
                    with sp.Fori(1, FF // WIDE) as it:
                        load(n0 + 2 * it, gate[:, :, bass.ds(it * WIDE, WIDE)], 0)
                        load(n0 + 2 * it + 1, up[:, :, bass.ds(it * WIDE, WIDE)], 1)
                    with sp.Fori(0, QUARTERS) as q:
                        for step in range(DOWN_STEPS):
                            load(n0 + 2 * FF // WIDE + DOWN_STEPS * q + step,
                                 down[:, KT * step:KT * step + KT, bass.ds(q * WIDE, WIDE)], step % 2)
                if kind == "gla":
                    w_in, w_out = by_k(a["gla_w_in"][layer // 2]), by_k(a["gla_w_out"][layer // 2])
                    with sp.Fori(0, OUT_AT // 2) as it:
                        for slot in range(2):
                            load(n0 + 2 * it + slot, w_in[:, :, bass.ds((2 * it + slot) * WIDE, WIDE)], slot)
                    with sp.Fori(0, QUARTERS // 2) as it:
                        for slot in range(2):
                            load(n0 + OUT_AT + 2 * it + slot, w_out[:, :, bass.ds((2 * it + slot) * WIDE, WIDE)], slot)
                if kind == "sgu":
                    w_in, w_out = by_k(a["sgu_w_in"][layer // 2]), by_k(a["sgu_w_out"][layer // 2])
                    for at, start in ((0, HALF), (V_CHUNKS, 0)):
                        with sp.Fori(0, V_CHUNKS // 2) as it:
                            for slot in range(2):
                                load(n0 + at + 2 * it + slot,
                                     w_in[:, :, bass.ds((2 * it + slot) * WIDE + start, WIDE)], slot)
                    with sp.Fori(0, QUARTERS // 2) as it:
                        for c in range(2 * SGU_STEPS):
                            q, step = 2 * it + c // SGU_STEPS, c % SGU_STEPS
                            load(n0 + 2 * V_CHUNKS + 2 * SGU_STEPS * it + c,
                                 w_out[:, KT * step:KT * step + KT, bass.ds(q * WIDE, WIDE)], c % 2)
            for half in range(2):
                for t in range(NT):
                    g = half * NT + t
                    sp.wait_ge(yt_out, g + 1)
                    dst = (yp[:, t, :] if t < NP else ys)[:, half * BANK:(half + 1) * BANK]
                    sp.dma_start(dst, y_rows[:, t, half * BANK:(half + 1) * BANK]).then_inc(stored, 16)
            sp.wait_ge(stored, 16 * 2 * NT)

        @block.scalar
        def _(act):
            def round_chunk(n, slot, first=False):
                act.wait_ge(landed[slot], 8 * (n - slot) + 16)
                if not first:
                    act.wait_ge(w_used, n - 1)
                act.activation(whi[:, slot], raw[:, slot], ACT.Copy).then_inc(w_hi, 1)

            def split_x(b):
                for k in range(DK):
                    act.wait_ge(x_new, DK * b + k + 1)
                    act.activation(xhi[:, k, :], x[:, k, :], ACT.Copy, scale=gain(g_pre, b, k)).then_inc(x_hi, 1)
                    if k >= 2:
                        act.wait_ge(x_acc, DK * b + k - 1)
                    act.activation(sq[:, k % 2, :], x[:, k, :], ACT.Square).then_inc(x_sq, 1)

            def pre_factor(b):
                act.wait_ge(factor_ready, stat0[b] + 1)
                act.activation(r_pre[:, :], stat[:, 0:TOK], ACT.Copy).then_inc(factor_read, 1)

            def output(b, n1, steps, started=False):
                def group(q, parity):
                    for step in range(steps):
                        n = n1 + q * steps + step
                        if isinstance(n, int) and (n + 1 >= CHUNKS or started and n == n1):
                            continue
                        round_chunk(n + 1, (steps * parity + step + 1) % 2)
                    for j in range(2):
                        m = 2 * q + j
                        if j == 0:
                            act.wait_ge(y_first, QUARTERS * b + q + 1)
                        else:
                            act.wait_ge(w_used, n1 + (q + 1) * steps)
                        act.wait_ge(y_acc, (DK + 2) * b + 1 + m)
                        psum = proj[2 * parity + j][:, 0:TOK]
                        act.activation(sq[:, j, :], psum, ACT.Square).then_inc(y_sq, 1)
                        act.activation(yg[:, bass.ds(m, 1), :], psum, ACT.Copy,
                                       scale=gain(g_post, b, m)).then_inc(tile_out, 1)
                pairs_of_groups(act, group, started or b == len(plan) - 1)

            act.wait_ge(const_in, 96)
            round_chunk(0, 0, True)
            for b, (kind, layer, which) in enumerate(plan):
                n0 = chunk0[b]
                split_x(b)
                if kind == "ffn":
                    f0 = ff0[b]

                    def silu(it):
                        for j in range(2):
                            act.wait_ge(tile_out, tile0[b] + 4 * it + j + 1)
                            act.activation(h_gate[:, j, :], h_gate[:, j, :], ACT.Silu).then_inc(silu_ready, 1)

                    def round_h(it):
                        for j in range(2):
                            act.wait_ge(prod_ready, f0 + 2 * it + j + 1)
                            act.activation(hhi[:, bass.ds(2 * it + j, 1), :], h_up[:, j:j + 1, :], ACT.Copy)\
                               .then_inc(h_hi, 1)

                    round_chunk(n0 + 1, 1, b == 0)
                    round_chunk(n0 + 2, 0)
                    pre_factor(b)
                    silu(0)
                    with act.Fori(1, FF // WIDE) as it:
                        round_chunk(n0 + 2 * it + 1, 1)
                        round_h(it - 1)
                        round_chunk(n0 + 2 * it + 2, 0)
                        silu(it)
                    round_h(FF // WIDE - 1)
                    output(b, n0 + 2 * FF // WIDE, DOWN_STEPS)
                if kind == "gla":
                    def tile_cols(buf, t):
                        return buf[:, :, t * P:(t + 1) * P]

                    act.wait_ge(gla_in, 48)
                    act.activation(wz_hi[:, :, :], wz[:, :, :], ACT.Copy).then_inc(wz_split, 1)
                    round_chunk(n0 + 1, 1)
                    round_chunk(n0 + 2, 0)
                    pre_factor(b)
                    act.wait_ge(z_mm, 2)
                    act.wait_ge(z_turned, 1)
                    act.activation(z_cols[0:RANK, :], banks[6][0:RANK, 0:TOK], ACT.Copy).then_inc(z_turned, 1)
                    round_chunk(n0 + 3, 1)
                    act.wait_ge(z_mm, 3)
                    for t in range(NT):
                        act.activation(log_g_rows[:, t, :], banks[5 + t][:, :], ACT.Abs).then_inc(g_abs, 1)
                    round_chunk(n0 + 4, 0)
                    for t in range(NT):
                        act.wait_ge(g_abs, t + 1)
                        act.activation(log_g_rows[:, t, :], log_g_rows[:, t, :], ACT.Exp, scale=-1.0)\
                           .then_inc(g_exp, 1)
                    for t in range(NT):
                        act.wait_ge(g_exp, t + 1)
                        act.activation(log_g_rows[:, t, :], log_g_rows[:, t, :], ACT.Ln, bias=ones[:, 0:1])\
                           .then_inc(g_log, 1)
                    round_chunk(n0 + 5, 1)
                    for t in range(NT):
                        act.wait_ge(b_copied, t + 1)
                        act.activation(tile_cols(e_pos, t), tile_cols(b_cum, t), ACT.Exp, scale=1 / GLA_TAU)\
                           .then_inc(b_exp, 1)
                        act.activation(tile_cols(e_neg, t), tile_cols(b_cum, t), ACT.Exp, scale=-1 / GLA_TAU)\
                           .then_inc(b_exp, 1)
                    round_chunk(n0 + 6, 0)
                    act.wait_ge(b_diff, 2)
                    act.activation(k_dec[:, :, :], k_dec[:, :, :], ACT.Exp, scale=1 / GLA_TAU).then_inc(d_exp, 1)
                    round_chunk(n0 + 7, 1)
                    round_chunk(n0 + 8, 0)

                    def round_o(h):
                        for i in range(VT):
                            act.wait_ge(o_gated, VT * h + i + 1)
                            act.activation(ohi[:, VT * h + i, :], ot[:, i, :], ACT.Copy).then_inc(o_hi, 1)

                    for h in range(HEADS):
                        act.wait_ge(k_turned, h + 1)
                        act.activation(k_rows[:, :], banks[3][:, 0:TOK], ACT.Copy).then_inc(k_out, 1)
                        round_chunk(n0 + R_AT + h + 1, (h + 1) % 2)
                        if h > 0:
                            round_o(h - 1)
                        act.wait_ge(o_mm, h + 1)
                        if h > 0:
                            act.wait_ge(o_acc, h)
                            act.wait_ge(o_lo, VT * h)
                        for i in range(VT):
                            act.activation(sq[:, i, :], banks[5 + i][:, 0:TOK], ACT.Square).then_inc(o_sq, 1)
                        for i in range(VT):
                            act.activation(ot[:, i, :], banks[5 + i][:, 0:TOK], ACT.Copy,
                                           scale=g_head[:, i:i + 1]).then_inc(o_out, 1)
                        for i in range(VT):
                            act.wait_ge(tile_out, tile0[b] + R_TILE + VT * h + i + 1)
                            act.activation(r_silu[:, VT * h + i, :], r_silu[:, VT * h + i, :], ACT.Silu)\
                               .then_inc(r_silu_done, 1)
                    round_chunk(n0 + OUT_AT + 1, 1)
                    round_o(HEADS - 1)
                    output(b, n0 + OUT_AT, 1, started=True)
                if kind == "sgu":
                    def v_gelu(i):
                        for t in range(NT):
                            act.wait_ge(tile_out, tile0[b] + NT * i + t + 1)
                            act.activation(v_at(i, t), v_at(i, t), ACT.Gelu).then_inc(v_act, 1)

                    def round_u(i):
                        for j in range(2):
                            c = 2 * i + j
                            act.wait_ge(u_prod, c + 1)
                            act.activation(uhi[c // KT][:, c % KT, :], u_tile[:, j, :], ACT.Copy).then_inc(u_hi, 1)

                    round_chunk(n0 + 1, 1)
                    round_chunk(n0 + 2, 0)
                    v_gelu(0)
                    pre_factor(b)
                    for i in range(1, V_CHUNKS):
                        if i > 1:
                            round_chunk(n0 + i + 1, (i + 1) % 2)
                        v_gelu(i)
                    for i in range(V_CHUNKS):
                        round_chunk(n0 + V_CHUNKS + i + 1, (i + 1) % 2)
                        if i > 0:
                            round_u(i - 1)
                        for j in range(2):
                            c = 2 * i + j
                            act.wait_ge(tile_out, tile0[b] + U_TILE + c + 1)
                            act.activation(u_tile[:, j, :], u_tile[:, j, :], ACT.Gelu, bias=u_bias[:, c:c + 1])\
                               .then_inc(u_act, 1)
                    round_u(V_CHUNKS - 1)
                    output(b, n0 + 2 * V_CHUNKS, SGU_STEPS)
            for g in range(2 * NT):
                half, t = divmod(g, NT)
                act.wait_ge(yt_ready, g + 1)
                act.activation(y_rows[:, t, half * BANK:(half + 1) * BANK], proj[g % NPROJ][:, :], ACT.Copy)\
                   .then_inc(yt_out, 1)

        @block.vector
        def _(dve):
            def split_chunk(n, slot):
                dve.wait_ge(w_hi, n + 1)
                dve.tensor_tensor(wlo[:, slot], raw[:, slot], whi[:, slot].bitcast(F32), ALU.subtract)\
                   .then_inc(w_lo, 1)

            def lo_x(b, k):
                dve.wait_ge(x_hi, DK * b + k + 1)
                dve.scalar_tensor_tensor(xlo[:, k, :], x[:, k, :], gain(g_pre, b, k), xhi[:, k, :].bitcast(F32),
                                         ALU.mult, ALU.subtract).then_inc(x_lo, 1)

            def mean(s, features):
                dve.wait_ge(sums_ready, s + 1)
                dve.tensor_scalar(mean_sq[:, :], stat[:, TOK:TOK + NT], 1.0 / features, RMS_EPS, ALU.mult, ALU.add)\
                   .then_inc(mean_ready, 1)

            def spread(s, buf, scale):
                dve.wait_ge(rstd_ready, s + 1)
                for t in range(NT):
                    last = dve.tensor_scalar(diag[:, t * P:(t + 1) * P], ident, rstd[:, buf, t:t + 1], scale,
                                             ALU.mult, ALU.mult)
                last.then_inc(diag_ready, 1)

            def output(b, n1, steps, started=False):
                dve.wait_ge(factor_ready, stat0[b + 1] - 1)
                dve.memset(acc[:, :], 0.0).then_inc(y_acc, 2)

                def group(q, parity):
                    for step in range(steps):
                        n = n1 + q * steps + step
                        if isinstance(n, int) and (n + 1 >= CHUNKS or started and n == n1):
                            continue
                        split_chunk(n + 1, (steps * parity + step + 1) % 2)
                    for j in range(2):
                        m = 2 * q + j
                        dve.wait_ge(y_sq, DK * b + m + 1)
                        dve.wait_ge(y_acc, (DK + 2) * b + 2 + m)
                        dve.tensor_tensor(acc[:, :], acc[:, :], sq[:, j, :], ALU.add).then_inc(y_acc, 1)
                pairs_of_groups(dve, group, started or b == len(plan) - 1)

            dve.memset(ones[:, :], 1.0).then_inc(consts_ready, 1)
            dve.wait_ge(const_in, 96)
            for k in range(DK):
                dve.wait_ge(xt_ready, k + 1)
                dve.tensor_copy(x[:, k, :], proj[k % NPROJ][:, 0:TOK]).then_inc(x_new, 1)
                if k > 0:
                    if k == 1:
                        dve.wait_ge(x_new, k)
                    lo_x(0, k - 1)
            lo_x(0, DK - 1)
            split_chunk(0, 0)
            for b, (kind, layer, which) in enumerate(plan):
                n0, T0, last = chunk0[b], tile0[b], b == len(plan) - 1
                if kind == "ffn":
                    f0 = ff0[b]

                    def gate(it, first):
                        dve.wait_ge(w_used, n0 + 2 * it + 1)
                        for j in range(2):
                            if not first:
                                dve.wait_ge(prod_ready, f0 + 2 * it + j - 1)
                            dve.tensor_tensor(h_gate[:, j, :], proj[j][:, 0:TOK], r_pre[:, :], ALU.mult)\
                               .then_inc(tile_out, 1)

                    def product(it, first):
                        T, f = T0 + 4 * it + 2, f0 + 2 * it
                        dve.wait_ge(w_used, n0 + 2 * it + 2)
                        for j in range(2):
                            if not first:
                                dve.wait_ge(h_lo, f + j - 1)
                            dve.tensor_tensor(h_up[:, j, :], proj[2 + j][:, 0:TOK], r_pre[:, :], ALU.mult)\
                               .then_inc(tile_out, 1)
                        for j in range(2):
                            dve.wait_ge(tile_out, T + j + 1)
                            dve.wait_ge(silu_ready, f + j + 1)
                            dve.tensor_tensor(h_up[:, j, :], h_up[:, j, :], h_gate[:, j, :], ALU.mult)\
                               .then_inc(prod_ready, 1)

                    split_chunk(n0 + 1, 1)
                    mean(stat0[b], D)
                    spread(stat0[b], 0, 1.0)
                    split_chunk(n0 + 2, 0)
                    dve.wait_ge(factor_read, pre0[b] + 1)
                    gate(0, b == 0)
                    product(0, b == 0)
                    split_chunk(n0 + 3, 1)
                    gate(1, False)
                    split_chunk(n0 + 4, 0)
                    with dve.Fori(2, FF // WIDE) as it:
                        product(it - 1, False)
                        split_chunk(n0 + 2 * it + 1, 1)
                        gate(it, False)
                        split_chunk(n0 + 2 * it + 2, 0)
                    product(FF // WIDE - 1, False)
                    output(b, n0 + 2 * FF // WIDE, DOWN_STEPS)
                if kind == "gla":
                    dve.memset(scores[:, :], 0.0).then_inc(scores_out, 1)
                    dve.wait_ge(wz_split, 1)
                    dve.tensor_tensor(wz_lo[:, :, :], wz[:, :, :], wz_hi[:, :, :].bitcast(F32), ALU.subtract)\
                       .then_inc(wz_split, 1)
                    split_chunk(n0 + 1, 1)
                    mean(stat0[b], D)
                    spread(stat0[b], 0, 1.0)
                    dve.wait_ge(z_mm, 1)
                    for t in range(NT):
                        dve.tensor_scalar(z_rows[:, t, :], banks[7][:, t * RANK:(t + 1) * RANK], rstd[:, 0, t:t + 1],
                                          None, ALU.mult).then_inc(z_evac, 1)
                    split_chunk(n0 + 2, 0)
                    dve.wait_ge(factor_read, pre0[b] + 1)

                    def evac_qk(i):
                        dve.wait_ge(w_used, n0 + i + 1)
                        which_qk, at = divmod(i, Q_CHUNKS)
                        for j in range(2):
                            dve.scalar_tensor_tensor(qk[:, 2 * at + j, which_qk, :], proj[2 * (i % 2) + j][:, 0:TOK],
                                                     (DH ** -0.5, 1.0)[which_qk], r_pre[:, :], ALU.mult, ALU.mult)\
                               .then_inc(tile_out, 1)

                    def evac_v(h):
                        dve.wait_ge(w_used, n0 + 2 * Q_CHUNKS + h + 1)
                        for t in range(NT):
                            dve.tensor_scalar(v_rows[:, t, h * DV:(h + 1) * DV], proj[(NT * h + t) % NPROJ][:, 0:DV],
                                              rstd[:, 0, t:t + 1], None, ALU.mult).then_inc(tile_out, 1)

                    evac_qk(0)
                    split_chunk(n0 + 3, 1)
                    evac_qk(1)
                    split_chunk(n0 + 4, 0)
                    evac_qk(2)
                    for t in range(NT):
                        dve.wait_ge(g_log, t + 1)
                        dve.scalar_tensor_tensor(log_g_rows[:, t, :], banks[5 + t][:, :], 0.0, log_g_rows[:, t, :],
                                                 ALU.min, ALU.subtract).then_inc(g_done, 1)
                    split_chunk(n0 + 5, 1)
                    evac_qk(3)
                    dve.wait_ge(z_mm, 4)
                    for t in range(NT):
                        dve.tensor_copy(b_cum[:, :, t * P:(t + 1) * P],
                                        banks[5 + t][:, :].rearrange("p (h t) -> p h t", h=HEADS))\
                           .then_inc(b_copied, 1)
                    dve.wait_ge(b_copied, NT)
                    for at, size, span in ((0, seq, GCH), (seq, P, dec_seq)):
                        cut = lambda buf: buf[:, :, at:at + size].rearrange("p h (c l) -> p h c l", l=span)
                        dve.tensor_tensor(cut(k_dec), cut(b_cum)[:, :, :, span - 1:span].to_broadcast(
                                              [P, HEADS, size // span, span]), cut(b_cum), ALU.subtract)\
                           .then_inc(b_diff, 1)
                    evac_v(0)
                    split_chunk(n0 + 6, 0)
                    evac_v(1)
                    dve.wait_ge(d_exp, 1)
                    for h in range(HEADS):
                        dve.tensor_tensor(k_dec[:, h, :], k_dec[:, h, :], qk[:, h, 1, :], ALU.mult)\
                           .then_inc(k_decayed, 1)
                    split_chunk(n0 + 7, 1)
                    evac_v(2)
                    dve.wait_ge(b_exp, 2 * NT)
                    for h in range(HEADS):
                        dve.tensor_tensor(qk[:, h, 0, :], qk[:, h, 0, :], e_pos[:, h, :], ALU.mult)
                        dve.tensor_tensor(qk[:, h, 1, :], qk[:, h, 1, :], e_neg[:, h, :], ALU.mult)\
                           .then_inc(qk_ready, 1)
                    split_chunk(n0 + 8, 0)
                    evac_v(3)

                    def gate_o(h):
                        dve.wait_ge(factor_ready, stat0[b] + 2 + h)
                        dve.wait_ge(o_out, VT * (h + 1))
                        dve.wait_ge(r_silu_done, VT * (h + 1))
                        for i in range(VT):
                            dve.tensor_tensor(ot[:, i, :], ot[:, i, :], stat[:, 0:TOK], ALU.mult)\
                               .then_inc(o_scaled, 1)
                        for i in range(VT):
                            dve.wait_ge(o_scaled, VT * h + i + 1)
                            dve.tensor_tensor(ot[:, i, :], ot[:, i, :], r_silu[:, VT * h + i, :], ALU.mult)\
                               .then_inc(o_gated, 1)
                        for i in range(VT):
                            dve.wait_ge(o_hi, VT * h + i + 1)
                            dve.tensor_tensor(olo[:, VT * h + i, :], ot[:, i, :], ohi[:, VT * h + i, :].bitcast(F32),
                                              ALU.subtract).then_inc(o_lo, 1)

                    for h in range(HEADS):
                        s = stat0[b] + 1 + h
                        dve.wait_ge(scores_mm, h + 1)
                        if h == 0:
                            dve.wait_ge(scores_out, 1)
                        for t in range(NT):
                            cols = slice(t * P, (t + 1) * P)
                            dve.copy_predicated(scores[:, cols], tri_tok[t].bitcast(U32), banks[2][:, cols])\
                               .then_inc(scores_out, 1)
                        dve.wait_ge(tile_out, T0 + R_TILE)
                        for i in range(2):
                            dve.tensor_scalar(v_pair[:, i, :], v_rows[:, NP, h * DV:(h + 1) * DV],
                                              pair_mask[:, i:i + 1], None, ALU.mult).then_inc(vp_done, 1)
                        for c in range(seq // GCH):
                            product = banks[7 if c % 2 == 0 else 2][:, c // 2 * DV:(c // 2 + 1) * DV]
                            dve.wait_ge(kv_mm, 2 * h + 1 + c % 2)
                            if c == 0:
                                if h > 0:
                                    dve.wait_ge(sp_stored, 16 * h)
                                dve.tensor_copy(s_prompt[:, 0, :], product).then_inc(s_done, 1)
                            else:
                                dve.wait_ge(s_done, seq // GCH * h + c)
                                dve.scalar_tensor_tensor(s_prompt[:, c, :], s_prompt[:, c - 1, :],
                                                         e_pos[:, h, (c + 1) * GCH - 1:(c + 1) * GCH], product,
                                                         ALU.mult, ALU.add).then_inc(s_done, 1)
                        split_chunk(n0 + R_AT + h + 1, (h + 1) % 2)
                        if h > 0:
                            spread(s - 1, 1, 1.0)
                            gate_o(h - 1)
                        for c in range(dec_batch):
                            dve.wait_ge(dec_mm, dec_batch // 2 * h + c // 2 + 1)
                            last_token = seq + (c + 1) * dec_seq - 1
                            state = s0[:, h % 2, c, :]
                            dve.scalar_tensor_tensor(state, state, e_pos[:, h, last_token:last_token + 1],
                                                     banks[DEC_BANKS[c // 2]][:, c % 2 * DV:(c % 2 + 1) * DV],
                                                     ALU.mult, ALU.add).then_inc(dec_done, 1)
                        dve.wait_ge(w_used, n0 + R_AT + h + 1)
                        for i in range(VT):
                            dve.tensor_tensor(r_silu[:, VT * h + i, :], proj[i][:, 0:TOK], r_pre[:, :], ALU.mult)\
                               .then_inc(tile_out, 1)
                        dve.wait_ge(o_sq, VT * (h + 1))
                        dve.tensor_tensor(acc[:, :], sq[:, 0, :], sq[:, 1, :], ALU.add).then_inc(o_acc, 1)
                        mean(s, DV)
                    split_chunk(n0 + OUT_AT + 1, 1)
                    spread(stat0[b] + HEADS, 1, 1.0)
                    gate_o(HEADS - 1)
                    output(b, n0 + OUT_AT, 1, started=True)
                if kind == "sgu":
                    def v_evac(i):
                        dve.wait_ge(rows_in[i % 2], 16 * (i // 2 + 1))
                        dve.wait_ge(w_used, n0 + i + 1)
                        for t in range(NT):
                            dve.scalar_tensor_tensor(v_at(i, t), proj[(NT * i + t) % NPROJ][:, 0:WIDE],
                                                     rstd[:, 0, t:t + 1], feat_rows[:, i % 2, 0, :],
                                                     ALU.mult, ALU.add).then_inc(tile_out, 1)

                    def v_stats(i):
                        for t in range(NT):
                            dve.wait_ge(v_act, NT * i + t + 1)
                            dve.bn_stats(ln_stats[:, t, i, :], v_at(i, t)).then_inc(v_stat, 1)

                    def normalise(i):
                        for t in range(NT):
                            dve.tensor_scalar(v_at(i, t), v_at(i, t), ln_mean_var[:, t, 0:1], ln_rstd[:, t:t + 1],
                                              ALU.subtract, ALU.mult).then_inc(ln_norm, 1)

                    def u_product(i):
                        for j in range(2):
                            dve.wait_ge(u_act, 2 * i + j + 1)
                            dve.wait_ge(mix_out, 4 * i + 2 * j + 2)
                            dve.tensor_tensor(u_tile[:, j, :], u_tile[:, j, :], mixed[:, j, :], ALU.mult)\
                               .then_inc(u_prod, 1)

                    split_chunk(n0 + 1, 1)
                    mean(stat0[b], D)
                    spread(stat0[b], 0, 1.0)
                    split_chunk(n0 + 2, 0)
                    v_evac(0)
                    dve.wait_ge(ws_mm, 1)
                    for i, mask in enumerate((ident_tri[:, 1:2, :], ident_tri[:, 3:4, :])):
                        dve.tensor_tensor(w_turned[:, i], banks[5 + i][:, :].rearrange("p (g t) -> p g t", g=SPATIAL),
                                          mask.to_broadcast([P, SPATIAL, P]), ALU.mult).then_inc(ws_done, 1)
                    for i in range(1, V_CHUNKS):
                        if i > 1:
                            split_chunk(n0 + i + 1, (i + 1) % 2)
                        v_evac(i)
                        v_stats(i - 1)
                    v_stats(V_CHUNKS - 1)
                    dve.wait_ge(v_stat, NT * V_CHUNKS)
                    for t in range(NT):
                        dve.bn_aggr(ln_mean_var[:, t, :], ln_stats[:, t].rearrange("p c s -> p (c s)"))\
                           .then_inc(ln_aggr, 1)
                    dve.wait_ge(ln_aggr, NT)
                    dve.tensor_scalar(ln_var[:, :], ln_mean_var[:, :, 1], LN_EPS, None, ALU.add).then_inc(ln_eps, 1)
                    dve.wait_ge(ln_pow, 1)
                    normalise(0)
                    dve.wait_ge(ws_in, 16 * (dec_batch + 2))
                    for i in range(V_CHUNKS):
                        if i > 0:
                            u_product(i - 1)
                        split_chunk(n0 + V_CHUNKS + i + 1, (i + 1) % 2)
                        if i + 1 < V_CHUNKS:
                            normalise(i + 1)
                        dve.wait_ge(mix_mm, i + 1)
                        if i > 0:
                            dve.wait_ge(u_prod, 2 * i)
                        for j in range(2):
                            g = (2 * i + j) * SPATIAL // (HALF // P)
                            for at, size, span in ((0, seq, P), (seq, P, dec_seq)):
                                cut = lambda buf: buf.rearrange("p (c l) -> p c l", l=span)
                                dve.tensor_tensor(cut(mixed[:, j, at:at + size]), cut(banks[5 + j][:, at:at + size]),
                                                  b_spatial[:, g:g + 1, 0:span].to_broadcast([P, size // span, span]),
                                                  ALU.add).then_inc(mix_out, 1)
                        dve.wait_ge(w_used, n0 + V_CHUNKS + i + 1)
                        for j in range(2):
                            if i > 0:
                                dve.wait_ge(u_lo, 2 * i + j - 1)
                            dve.tensor_tensor(u_tile[:, j, :], proj[2 * (i % 2) + j][:, 0:TOK], r_pre[:, :], ALU.mult)\
                               .then_inc(tile_out, 1)
                    u_product(V_CHUNKS - 1)
                    output(b, n0 + 2 * V_CHUNKS, SGU_STEPS)
                s = stat0[b + 1] - 1
                mean(s, D)
                spread(s, 1, 0.5 if kind == "ffn" else 1.0)
                dve.wait_ge(factor_ready, s + 1)
                dve.wait_ge(tile_out, tile0[b + 1])
                for k in range(DK):
                    dve.tensor_tensor(yg[:, k, :], yg[:, k, :], stat[:, 0:TOK], ALU.mult).then_inc(y_scaled, 1)
                    if k > 0 and not last:
                        lo_x(b + 1, k - 1)
                    dve.wait_ge(y_scaled, DK * b + k + 1)
                    dve.tensor_tensor(x[:, k, :], x[:, k, :], yg[:, k, :], ALU.add).then_inc(x_new, 1)
                if not last:
                    lo_x(b + 1, DK - 1)

        @block.gpsimd
        def _(pool):
            def power(s, buf):
                pool.wait_ge(mean_ready, s + 1)
                pool.tensor_tensor(rstd[:, buf, :], mean_sq[:, :], minus_half[:, :], ALU.pow).then_inc(rstd_ready, 1)

            pool.memset(minus_half[:, :], -0.5).then_inc(consts_ready, 1)
            pool.wait_ge(consts_ready, 2)
            for b, (kind, layer, which) in enumerate(plan):
                if b > 0:
                    pool.wait_ge(factor_ready, stat0[b])
                if kind == "gla":
                    def load_s0(h):
                        pool.dma_start(s0[:, h % 2], a["state_gla"][layer // 2, :, h].rearrange("b p v -> p b v"))\
                            .then_inc(s0_in[h % 2], 16)

                    j = layer // 2
                    pool.wait_ge(x_new, DK * b + 1)
                    with nc.allow_non_contiguous_dma(reason="16 columns of w_in"):
                        pool.dma_start(wz[:, :, :], a["gla_w_in"][j].rearrange("(k p) c -> p k c", p=P)[
                            :, :, OUT_AT * WIDE:OUT_AT * WIDE + RANK]).then_inc(gla_in, 16)
                    pool.dma_start(w_gate2[0:RANK, :], a["gla_w_gate2"][j]).then_inc(gla_in, 16)
                    pool.dma_start(w_gate2[RANK:RANK + 1, :], a["gla_b_gate"][j:j + 1]).then_inc(gla_in, 16)
                    load_s0(0)
                    load_s0(1)
                    pool.memset(z_cols[:, :], 1.0).then_inc(z_turned, 1)
                if kind == "sgu":
                    j = layer // 2

                    def load_bias(i):
                        pool.dma_start(feat_rows[:, i % 2, 0, :], a["sgu_b_in"][j:j + 1, HALF + i * WIDE:
                                       HALF + (i + 1) * WIDE].to_broadcast([P, WIDE])).then_inc(rows_in[i % 2], 16)

                    pool.wait_ge(x_new, DK * b + 1)
                    pool.memset(w_rows[:, 1], 0.0).then_inc(ws_zero, 1)
                    pool.dma_start(w_rows[:, 0], a["sgu_w_s"][j].rearrange("g t s -> t g s")).then_inc(ws_in, 16)
                    pool.dma_start(b_spatial[:, :, :].rearrange("p g t -> p (g t)"), a["sgu_b_s"][j:j + 1].rearrange(
                        "a g t -> a (g t)").to_broadcast([P, SPATIAL * P])).then_inc(ws_in, 16)
                    load_bias(0)
                    load_bias(1)
                    pool.wait_ge(ws_zero, 1)
                    for c in range(dec_batch):
                        at = slice(c * dec_seq, (c + 1) * dec_seq)
                        pool.dma_start(w_rows[at, 1, :, at], a["sgu_w_s"][j, :, 0:dec_seq, 0:dec_seq].rearrange(
                            "g t s -> t g s")).then_inc(ws_in, 16)
                for k in range(DK):
                    pool.wait_ge(x_sq, DK * b + k + 1)
                    if k == 0:
                        pool.tensor_copy(acc[:, :], sq[:, 0, :]).then_inc(x_acc, 1)
                    else:
                        pool.wait_ge(x_acc, DK * b + k)
                        pool.tensor_tensor(acc[:, :], acc[:, :], sq[:, k % 2, :], ALU.add).then_inc(x_acc, 1)
                power(stat0[b], 0)
                if kind == "ffn":
                    with pool.Fori(0, FF // WIDE) as it:
                        for j in range(2):
                            pool.wait_ge(h_hi, ff0[b] + 2 * it + j + 1)
                            at = bass.ds(2 * it + j, 1)
                            pool.tensor_tensor(hlo[:, at, :], h_up[:, j:j + 1, :], hhi[:, at, :].bitcast(F32),
                                               ALU.subtract).then_inc(h_lo, 1)
                if kind == "gla":
                    for h in range(HEADS):
                        pool.wait_ge(dec_done, dec_batch * (h + 1))
                        pool.wait_ge(s_done, seq // GCH * (h + 1))
                        pool.dma_start(outs["gla_state_prompt"][layer // 2, 0, h], s_prompt[:, seq // GCH - 1, :])\
                            .then_inc(sp_stored, 16)
                        pool.dma_start(outs["gla_state_sample"][layer // 2, :, h].rearrange("b p v -> p b v"),
                                       s0[:, h % 2]).then_inc(s0_stored[h % 2], 16)
                        if h + 2 < HEADS:
                            pool.wait_ge(s0_stored[h % 2], 16)
                            load_s0(h + 2)
                        power(stat0[b] + 1 + h, 1)
                    pool.wait_ge(sp_stored, 16 * HEADS)
                    for i in range(2):
                        pool.wait_ge(s0_stored[i], 16 * HEADS // 2)
                if kind == "sgu":
                    def load_ln(i):
                        for which_row, name in enumerate(("sgu_ln_g", "sgu_ln_b")):
                            pool.dma_start(feat_rows[:, i % 2, which_row, :], a[name][j:j + 1, i * WIDE:(i + 1) * WIDE]
                                           .to_broadcast([P, WIDE])).then_inc(rows_in[i % 2], 16)

                    def affine(i):
                        at = i % PER_SET * WIDE
                        v = v_set[i // PER_SET][:, :, at:at + WIDE]
                        pool.wait_ge(rows_in[i % 2], 16 * (V_CHUNKS // 2 + 2 * (i // 2 + 1)))
                        pool.wait_ge(ln_norm, NT * (i + 1))
                        pool.tensor_tensor(v, v, feat_rows[:, i % 2, 0:1, :].to_broadcast([P, NT, WIDE]), ALU.mult)\
                            .then_inc(ln_gain, 1)
                        pool.wait_ge(ln_gain, i + 1)
                        pool.tensor_tensor(v, v, feat_rows[:, i % 2, 1:2, :].to_broadcast([P, NT, WIDE]), ALU.add)\
                            .then_inc(ln_done, 1)
                        pool.wait_ge(ln_done, i + 1)
                        if i + 2 < V_CHUNKS:
                            load_ln(i + 2)
                        if i % PER_SET == PER_SET - 1:
                            at = i // PER_SET * KT * P
                            pool.dma_start(outs["sgu_v_sample"][j].rearrange("b l c -> (b l) c")[:, at:at + KT * P],
                                           v_set[i // PER_SET][:, NP, :]).then_inc(v_stored, 16)

                    for i in range(2, V_CHUNKS):
                        pool.wait_ge(tile_out, tile0[b] + NT * (i - 1))
                        load_bias(i)
                    for i in range(2):
                        pool.wait_ge(tile_out, tile0[b] + NT * (V_CHUNKS - 1 + i))
                        load_ln(i)
                    pool.wait_ge(ln_eps, 1)
                    pool.tensor_tensor(ln_rstd[:, :], ln_var[:, :], minus_half[:, :], ALU.pow).then_inc(ln_pow, 1)
                    affine(0)
                    for i in range(V_CHUNKS):
                        if i + 1 < V_CHUNKS:
                            affine(i + 1)
                        for c in (2 * i, 2 * i + 1):
                            if c == KT:
                                pool.wait_ge(mix_mm, PER_SET)
                                pool.wait_ge(v_stored, 16)
                            if c == 2 * KT:
                                pool.wait_ge(mix_mm, 2 * PER_SET)
                                pool.wait_ge(v_stored, 32)
                            pool.wait_ge(u_hi, c + 1)
                            pool.tensor_tensor(ulo[c // KT][:, c % KT, :], u_tile[:, c % 2, :],
                                               uhi[c // KT][:, c % KT, :].bitcast(F32), ALU.subtract)\
                                .then_inc(u_lo, 1)
                    pool.wait_ge(v_stored, 48)
                power(stat0[b + 1] - 1, 1)

        @block.tensor
        def _(pe):
            def multiply(out, slot, k, j, rhs_hi, rhs_lo, start, stop):
                cols = slice(j * P, (j + 1) * P)
                pe.matmul(out, whi[:, slot, k, cols], rhs_hi, start=start, stop=False)
                pe.matmul(out, whi[:, slot, k, cols], rhs_lo, start=False, stop=False)
                return pe.matmul(out, wlo[:, slot, k, cols], rhs_hi, start=False, stop=stop)

            def sums(s):
                for t in range(NT):
                    last = pe.matmul(stat[:, TOK + t:TOK + t + 1], acc[:, t * P:(t + 1) * P], ones[:, 0:1],
                                     start=True, stop=True)
                last.then_inc(sums_ready, 1)

            def factors(s):
                pe.wait_ge(diag_ready, s + 1)
                pe.matmul(stat[:, 0:TOK], ones[:, :], diag[:, :], start=True, stop=True).then_inc(factor_ready, 1)

            def multiply_rows(out, slot, k, t, start, stop):
                cols = slice(t * P, (t + 1) * P)
                pe.matmul(out, xhi[:, k, cols], whi[:, slot, k, :], start=start, stop=False)
                pe.matmul(out, xhi[:, k, cols], wlo[:, slot, k, :], start=False, stop=False)
                return pe.matmul(out, xlo[:, k, cols], whi[:, slot, k, :], start=False, stop=stop)

            def first_chunk(b):
                pe.wait_ge(w_lo, chunk0[b] + 1)
                if b > 0:
                    pe.wait_ge(tile_out, tile0[b])
                for k in range(KT):
                    pe.wait_ge(x_lo, DK * b + k + 1)
                    if plan[b][0] == "sgu":
                        for t in range(NT):
                            mm = multiply_rows(proj[t][:, 0:WIDE], 0, k, t, k == 0, k == KT - 1)
                        continue
                    for j in range(2):
                        mm = multiply(proj[j][:, 0:TOK], 0, k, j, xhi[:, k, :], xlo[:, k, :], k == 0, k == KT - 1)
                mm.then_inc(w_used, 1)

            def pre_sums(b):
                pe.wait_ge(x_acc, DK * (b + 1))
                if b > 0:
                    pe.wait_ge(y_scaled, DK * b)
                sums(stat0[b])

            def tile(bank, slot, j):
                for k in range(KT):
                    mm = multiply(proj[bank][:, 0:TOK], slot, k, j, xhi[:, k, :], xlo[:, k, :], k == 0, k == KT - 1)
                return mm

            def output(b, n1, T1, steps, rhs, in_order=False):
                def group(q, parity):
                    if in_order and q == 0:
                        pe.wait_ge(tile_out, T1)
                        pe.wait_ge(w_lo, n1 + 1)
                        for k in range(KT):
                            pe.wait_ge(rhs(0)[2], k + 1)
                            for j in range(2):
                                mm = multiply(proj[j][:, 0:TOK], 0, k, j, rhs(0)[0][:, k, :], rhs(0)[1][:, k, :],
                                              k == 0, k == KT - 1)
                                if k == KT - 1:
                                    mm.then_inc((y_first, w_used)[j], 1)
                        return
                    pe.wait_ge(tile_out, T1 + 2 * q - 2)
                    for step in range(steps):
                        n = n1 + q * steps + step
                        pe.wait_ge(w_lo, n + 1)
                        ready, count = rhs(step)[2:]
                        if not in_order:
                            pe.wait_ge(ready, count)
                        for j in range(2):
                            for k in range(KT):
                                hi, lo = rhs(step)[:2]
                                mm = multiply(proj[2 * parity + j][:, 0:TOK], (steps * parity + step) % 2, k, j,
                                              hi[:, k, :], lo[:, k, :], step == k == 0,
                                              step == steps - 1 and k == KT - 1)
                            if j == 0 and step == steps - 1:
                                mm.then_inc(y_first, 1)
                        mm.then_inc(w_used, 1)
                pairs_of_groups(pe, group, in_order)
                s = stat0[b + 1] - 1
                pe.wait_ge(y_acc, (DK + 2) * (b + 1))
                pe.wait_ge(factor_read, pre0[b + 1])
                if kind == "gla":
                    pe.wait_ge(o_scaled, HEADS * VT)
                sums(s)
                factors(s)

            pe.wait_ge(const_in, 96)
            pe.wait_ge(x_in, 32)
            pe.wait_ge(consts_ready, 2)
            for k in range(DK):
                if k >= NPROJ:
                    pe.wait_ge(x_new, k - NPROJ + 1)
                for t in range(NT):
                    last = pe.transpose(proj[k % NPROJ][:, t * P:(t + 1) * P], x_rows[:, t, k * P:(k + 1) * P],
                                        ident)
                last.then_inc(xt_ready, 1)
            for b, (kind, layer, which) in enumerate(plan):
                n0, T0 = chunk0[b], tile0[b]
                first_chunk(b)
                pre_sums(b)
                if kind == "ffn":
                    pe.wait_ge(w_lo, n0 + 2)
                    tile(2, 1, 0)
                    factors(stat0[b])
                    tile(3, 1, 1).then_inc(w_used, 1)
                    with pe.Fori(1, FF // WIDE) as it:
                        for slot in range(2):
                            pe.wait_ge(w_lo, n0 + 2 * it + slot + 1)
                            pe.wait_ge(tile_out, T0 + 4 * it + 2 * slot - 2)
                            tile(2 * slot, slot, 0)
                            tile(2 * slot + 1, slot, 1).then_inc(w_used, 1)
                    output(b, n0 + 2 * FF // WIDE, T0 + 2 * FK, DOWN_STEPS,
                           lambda step: (hhi[:, KT * step:KT * (step + 1), :], hlo[:, KT * step:KT * (step + 1), :],
                                         h_lo, ff0[b] + KT * (step + 1)))
                if kind == "gla":
                    pe.wait_ge(wz_split, 2)
                    for t in range(NT):
                        cols = slice(t * P, (t + 1) * P)
                        z = banks[7][:, t * RANK:(t + 1) * RANK]
                        for k in range(KT):
                            pe.matmul(z, xhi[:, k, cols], wz_hi[:, k, :], start=k == 0, stop=False)
                            pe.matmul(z, xhi[:, k, cols], wz_lo[:, k, :], start=False, stop=False)
                            mm = pe.matmul(z, xlo[:, k, cols], wz_hi[:, k, :], start=False, stop=k == KT - 1)
                    mm.then_inc(z_mm, 1)

                    def x_tile(i, j):
                        return tile(2 * (i % 2 if i < 2 * Q_CHUNKS else 0) + j, i % 2, j)

                    def v_chunk(h):
                        i = 2 * Q_CHUNKS + h
                        pe.wait_ge(w_lo, n0 + i + 1)
                        for t in range(NT):
                            T = T0 + V_TILE + NT * h + t
                            pe.wait_ge(tile_out, T - NPROJ + 1)
                            out = proj[(NT * h + t) % NPROJ][:, 0:DV]
                            for k in range(KT):
                                mm = multiply_rows(out, i % 2, k, t, k == 0, k == KT - 1)
                        mm.then_inc(w_used, 1)

                    pe.wait_ge(w_lo, n0 + 2)
                    x_tile(1, 0)
                    factors(stat0[b])
                    x_tile(1, 1).then_inc(w_used, 1)
                    pe.wait_ge(z_evac, NT)
                    for t in range(NT):
                        mm = pe.matmul(banks[6][0:RANK, t * P:(t + 1) * P], z_rows[:, t, :], ident,
                                       start=True, stop=True)
                    mm.then_inc(z_mm, 1)
                    pe.wait_ge(w_lo, n0 + 3)
                    pe.wait_ge(tile_out, T0 + 2)
                    x_tile(2, 0)
                    pe.wait_ge(z_turned, 2)
                    pe.wait_ge(gla_in, 48)
                    for t in range(NT):
                        mm = pe.matmul(banks[5 + t][:, :], z_cols[0:RANK + 1, t * P:(t + 1) * P],
                                       w_gate2[:, :], start=True, stop=True)
                    mm.then_inc(z_mm, 1)
                    x_tile(2, 1).then_inc(w_used, 1)
                    pe.wait_ge(w_lo, n0 + 4)
                    pe.wait_ge(tile_out, T0 + 4)
                    x_tile(3, 0)
                    x_tile(3, 1).then_inc(w_used, 1)
                    v_chunk(0)
                    pe.wait_ge(g_done, NT)
                    for t in range(NT):
                        for h in range(HEADS):
                            mm = pe.matmul(banks[5 + t][:, h * P:(h + 1) * P], log_g_rows[:, t, h * P:(h + 1) * P],
                                           tri_tok[t], start=True, stop=True)
                    mm.then_inc(z_mm, 1)
                    for h in range(1, HEADS):
                        v_chunk(h)
                    pe.wait_ge(tile_out, T0 + R_TILE)
                    pe.wait_ge(b_copied, NT)
                    for h in range(HEADS):
                        s = stat0[b] + 1 + h
                        q_h, k_h, v_h = qk[:, h, 0, :], qk[:, h, 1, :], v_rows[:, :, h * DV:(h + 1) * DV]
                        pe.wait_ge(qk_ready, h + 1)
                        if h > 0:
                            pe.wait_ge(dec_done, dec_batch * h)
                        for t in range(NT):
                            cols = slice(t * P, (t + 1) * P)
                            mm = pe.matmul(banks[2][:, cols], k_h[:, cols], q_h[:, cols], start=True, stop=True)
                        mm.then_inc(scores_mm, 1)
                        pe.wait_ge(k_decayed, h + 1)
                        for t in range(NT):
                            mm = pe.transpose(banks[3][:, t * P:(t + 1) * P], k_dec[:, h, t * P:(t + 1) * P], ident)
                        mm.then_inc(k_turned, 1)
                        pe.wait_ge(w_lo, n0 + R_AT + h + 1)
                        pe.wait_ge(tile_out, T0 + R_TILE + VT * h)
                        x_tile(R_AT + h, 0)
                        if h > 0:
                            pe.wait_ge(o_acc, h)
                            if h > 1:
                                pe.wait_ge(o_scaled, VT * (h - 1))
                            sums(s - 1)
                        pe.wait_ge(k_out, h + 1)
                        pe.wait_ge(scores_out, 1 + NT * (h + 1))
                        for c in (0, 2, 1, 3):
                            rows, t = slice(c % 2 * GCH, (c % 2 + 1) * GCH), c // 2
                            mm = pe.matmul(banks[7 if c % 2 == 0 else 2][:, t * DV:(t + 1) * DV],
                                           k_rows[rows, t * P:(t + 1) * P], v_h[rows, t, :], start=True, stop=True)
                            if t == 1:
                                mm.then_inc(kv_mm, 1)
                        if h > 0:
                            pe.wait_ge(o_out, VT * h)
                        pe.wait_ge(s0_in[h % 2], 16 * (h // 2 + 1))
                        for i in range(VT):
                            o, vals = banks[5 + i], slice(i * P, (i + 1) * P)
                            for t in range(NT):
                                cols = slice(t * P, (t + 1) * P)
                                pe.matmul(o[:, cols], v_h[:, t, vals], scores[:, cols], start=t == 0, stop=False,
                                          skip_group_check=True)
                            for c in range(dec_batch):
                                cols = slice(seq + c * dec_seq, seq + (c + 1) * dec_seq)
                                mm = pe.matmul(o[:, cols], s0[:, h % 2, c, vals], q_h[:, cols], start=False,
                                               stop=False, skip_group_check=True)
                        mm.then_inc(inter_mm, 1)
                        x_tile(R_AT + h, 1).then_inc(w_used, 1)
                        if h > 0:
                            factors(s - 1)
                        for c in range(1, seq // GCH):
                            cols = slice(c * GCH, (c + 1) * GCH)
                            pe.wait_ge(s_done, seq // GCH * h + c)
                            for i in range(VT):
                                mm = pe.matmul(banks[5 + i][:, cols], s_prompt[:, c - 1, i * P:(i + 1) * P],
                                               q_h[:, cols], start=False, stop=c == seq // GCH - 1,
                                               skip_group_check=True)
                        mm.then_inc(o_mm, 1)
                        pe.wait_ge(vp_done, 2 * (h + 1))
                        pe.wait_ge(s_done, seq // GCH * (h + 1))
                        for j in range(dec_batch // 2):
                            rows = slice(j * 2 * dec_seq, (j + 1) * 2 * dec_seq)
                            if j == dec_batch // 2 - 1:
                                pe.wait_ge(dec_done, dec_batch * h + 2)
                            pe.matmul(banks[DEC_BANKS[j]][:, :], k_rows[rows, NP * P:TOK],
                                      v_pair[rows, :, :].rearrange("p i v -> p (i v)"), start=True, stop=True)\
                              .then_inc(dec_mm, 1)
                    s = stat0[b] + HEADS
                    pe.wait_ge(o_acc, HEADS)
                    pe.wait_ge(o_scaled, VT * (HEADS - 1))
                    sums(s)
                    pe.wait_ge(w_lo, n0 + OUT_AT + 1)
                    factors(s)
                    output(b, n0 + OUT_AT, T0 + R_TILE + HEADS * VT, 1, lambda step: (ohi, olo, o_lo, 0), True)
                if kind == "sgu":
                    def v_tile(i, parity4, t):
                        pe.wait_ge(tile_out, NT * i + (T0 + t - NPROJ + 1))
                        for k in range(KT):
                            mm = multiply_rows(proj[(NT * parity4 + t) % NPROJ][:, 0:WIDE], parity4 % 2, k, t,
                                               k == 0, k == KT - 1)
                        return mm

                    for i in range(1, 4):
                        pe.wait_ge(w_lo, n0 + i + 1)
                        for t in range(NT):
                            mm = v_tile(i, i, t)
                            if i == 1 and t == 0:
                                factors(stat0[b])
                        mm.then_inc(w_used, 1)
                        if i == 1:
                            pe.wait_ge(ws_in, 16 * (dec_batch + 2))
                            for which_w in range(2):
                                for g in range(SPATIAL):
                                    mm = pe.transpose(banks[5 + which_w][:, g * P:(g + 1) * P],
                                                      w_rows[:, which_w, g, :], ident)
                            mm.then_inc(ws_mm, 1)
                    with pe.Fori(1, V_CHUNKS // 4) as it:
                        for c in range(4):
                            pe.wait_ge(w_lo, n0 + 4 * it + c + 1)
                            for t in range(NT):
                                mm = v_tile(4 * it + c, c, t)
                            mm.then_inc(w_used, 1)
                    pe.wait_ge(ws_done, 2)
                    for i in range(V_CHUNKS):
                        pe.wait_ge(w_lo, n0 + V_CHUNKS + i + 1)
                        pe.wait_ge(tile_out, T0 + U_TILE + 2 * i - 2)
                        tile(2 * (i % 2), i % 2, 0)
                        pe.wait_ge(ln_done, i + 1)
                        if i > 0:
                            pe.wait_ge(mix_out, 4 * i)
                        for j in range(2):
                            c = 2 * i + j
                            g = c * SPATIAL // (HALF // P)
                            for t in range(NT):
                                mm = pe.matmul(banks[5 + j][:, t * P:(t + 1) * P],
                                               v_at(i, t)[:, j * P:(j + 1) * P], w_turned[:, t // NP, g, :],
                                               start=True, stop=True)
                        mm.then_inc(mix_mm, 1)
                        tile(2 * (i % 2) + 1, i % 2, 1).then_inc(w_used, 1)
                    output(b, n0 + 2 * V_CHUNKS, T0 + SGU_OUT_TILE, SGU_STEPS,
                           lambda step: (uhi[step], ulo[step], u_lo, KT * (step + 1)))
            for g in range(2 * NT):
                half, t = divmod(g, NT)
                pe.wait_ge(x_new, DK * len(plan) + (half + 1) * DK // 2)
                if g >= NPROJ:
                    pe.wait_ge(yt_out, g - NPROJ + 1)
                for k in range(DK // 2):
                    last = pe.transpose(proj[g % NPROJ][:, k * P:(k + 1) * P],
                                        x[:, half * DK // 2 + k, t * P:(t + 1) * P], ident)
                last.then_inc(yt_ready, 1)


def constants():
    import numpy as np

    s, t = np.arange(P)[:, None], np.arange(P)[None, :]
    upto = s <= t
    tri = np.stack([s == t, upto, upto & (s // 64 == t // 64), upto & (s // 16 == t // 16)], axis=1)
    odd = np.arange(P) // 16 % 2
    return {"ident_tri": tri.astype(np.float32), "pair_mask": np.stack([1 - odd, odd], axis=1).astype(np.float32)}


def laid_out(inputs):
    import numpy as np

    def columns(g):
        return np.ascontiguousarray(g.reshape(-1, P).T)

    return {"gain_pre": columns(inputs["norm_pre"]), "gain_post": columns(inputs["norm_post"]),
            "gain_head": columns(inputs["gla_norm"]), "u_bias": columns(inputs["sgu_b_in"])}


PLAN = [("ffn", 0, 0), ("gla", 0, 1), ("ffn", 0, 2), ("ffn", 1, 0), ("sgu", 1, 1), ("ffn", 1, 2)]


def kernel(**inputs):
    import numpy as np
    import concourse.bacc as bacc
    from concourse.bass_utils import run_bass_kernel_spmd

    nc = bacc.Bacc("TRN2", target_bir_lowering=False, num_devices=1)
    arrays = {name: np.ascontiguousarray(value) for name, value in inputs.items()}
    arrays.update(constants(), **laid_out(arrays))
    a = {name: nc.dram_tensor(name, value.shape, mybir.dt.from_np(value.dtype), kind="ExternalInput").ap()
         for name, value in arrays.items()}
    n_gla, dec_batch, heads, dk, dv = inputs["state_gla"].shape
    n_sgu, half = inputs["sgu_ln_g"].shape
    shapes = {"y_prompt": inputs["x_prompt"].shape, "y_sample": inputs["x_sample"].shape,
              "gla_state_prompt": (n_gla, inputs["x_prompt"].shape[0], heads, dk, dv),
              "gla_state_sample": inputs["state_gla"].shape,
              "sgu_v_sample": (n_sgu,) + inputs["x_sample"].shape[:2] + (half,)}
    outs = {name: nc.dram_tensor(name, shape, F32, kind="ExternalOutput").ap() for name, shape in shapes.items()}
    build_trunk(nc, a, outs, PLAN)
    result = run_bass_kernel_spmd(nc, [arrays], core_ids=[0])
    return tuple(result.results[0][name] for name in shapes)
```

```python
from contextlib import ExitStack

import concourse.bass as bass
from concourse import mybir

F32 = mybir.dt.float32
F32R = mybir.dt.float32r
U32 = mybir.dt.uint32
ALU = mybir.AluOpType
ACT = mybir.ActivationFunctionType

P = 128
WIDE = 256
KT = 8
BANK = 512
RMS_EPS = 1e-6


def build_trunk(nc, a, outs, plan):
    seq, D = a["x_prompt"].shape[1:]
    dec_batch, dec_seq = a["x_sample"].shape[:2]
    NP = seq // P
    NT = NP + 1
    TOK = NT * P
    DK = D // P
    FF = a["ffn_w_gate"].shape[-1]
    FK = FF // P
    assert dec_batch * dec_seq == P and DK == KT and TOK <= BANK

    FFN_CHUNKS = 2 * FF // WIDE + FF // (P * KT) * (D // WIDE)
    DOWN_STEPS = FK // KT
    QUARTERS = D // WIDE

    HEADS, DH, DV = a["state_gla"].shape[2:]
    VT = DV // P
    RANK = a["gla_w_gate2"].shape[1]
    GLA_TAU = 16.0
    GCH = 64
    assert DH == P and DV == WIDE and HEADS * DV == D and dec_seq <= GCH
    Q_CHUNKS = HEADS * DH // WIDE
    V_TILE = 4 * Q_CHUNKS
    R_TILE = V_TILE + HEADS * NT
    R_AT = 2 * Q_CHUNKS + HEADS
    OUT_AT = R_AT + HEADS
    DEC_BANKS = (3, 7, 2, 3)
    GLA_CHUNKS = OUT_AT + QUARTERS

    HALF = a["sgu_ln_g"].shape[1]
    SPATIAL = a["sgu_w_s"].shape[1]
    LN_EPS = 1e-5
    V_CHUNKS = HALF // WIDE
    SGU_STEPS = HALF // (P * KT)
    SGU_CHUNKS = 2 * V_CHUNKS + SGU_STEPS * QUARTERS
    U_TILE = NT * V_CHUNKS
    SGU_OUT_TILE = U_TILE + HALF // P
    PER_SET = KT * P // WIDE
    assert a["sgu_w_s"].shape[2] == P

    chunk0, tile0, stat0, ff0 = [0], [0], [0], [0]
    for kind, layer, which in plan:
        chunks, tiles, stats, ff = {
            "ffn": (FFN_CHUNKS, 2 * FK + DK, 2, FK),
            "sgu": (SGU_CHUNKS, SGU_OUT_TILE + DK, 2, 0),
            "gla": (GLA_CHUNKS, 2 * HEADS * 2 + NT * HEADS + DK, 2 + HEADS, 0),
        }[kind]
        for start, size in ((chunk0, chunks), (tile0, tiles), (stat0, stats), (ff0, ff)):
            start.append(start[-1] + size)
    CHUNKS = chunk0[-1]

    xp = a["x_prompt"].rearrange("b (t p) d -> p (b t) d", p=P)
    xs = a["x_sample"].rearrange("b l d -> (b l) d")
    yp = outs["y_prompt"].rearrange("b (t p) d -> p (b t) d", p=P)
    ys = outs["y_sample"].rearrange("b l d -> (b l) d")

    with ExitStack() as ctx:
        def sb(name, shape, dt=F32):
            return ctx.enter_context(nc.sbuf_tensor(name + "_sb", shape, dt))

        def shared(*wanted):
            with ExitStack() as scope:
                return [scope.enter_context(nc.sbuf_tensor(name + "_sb", shape, dt))
                        for name, shape, dt in wanted]

        def sem(name):
            return ctx.enter_context(nc.semaphore(name))

        ident_tri = sb("ident_tri", [P, 4, P])
        ident, tri_gla, tri_dec = ident_tri[:, 0, :], ident_tri[:, 2, :], ident_tri[:, 3, :]
        tri_tok = [tri_gla] * NP + [tri_dec]
        pair_mask = sb("pair_mask", [P, 2])
        ones = sb("ones", [P, P])
        g_pre = sb("g_pre", [P, 2 * 3 * DK])
        g_post = sb("g_post", [P, 2 * 3 * DK])
        g_head = sb("g_head", [P, VT])
        u_bias = sb("u_bias", [P, 2 * HALF // P])
        x = sb("x", [P, DK, TOK])
        xhi = sb("xhi", [P, DK, TOK], F32R)
        xlo = sb("xlo", [P, DK, TOK], F32R)
        yg = sb("yg", [P, DK, TOK])
        raw = sb("raw", [P, 2, KT, WIDE])
        whi = sb("whi", [P, 2, KT, WIDE], F32R)
        wlo = sb("wlo", [P, 2, KT, WIDE], F32R)
        sq = sb("sq", [P, 2, TOK])
        acc = sb("acc", [P, TOK])
        diag = acc
        r_pre = sb("r_pre", [P, TOK])
        minus_half = sb("minus_half", [P, 1])
        mean_sq = sb("mean_sq", [P, NT])
        rstd = sb("rstd", [P, 2, NT])

        hhi, hlo, h_gate, h_up = shared(
            ("hhi", [P, FK, TOK], F32R), ("hlo", [P, FK, TOK], F32R),
            ("h_gate", [P, 2, TOK], F32), ("h_up", [P, 2, TOK], F32))
        (v_rows, qk, k_dec, s0, v_pair, log_g, e_neg, e_pos, olo, k_rows, scores, s_prompt, ot, z_rows, z_cols,
         wz, w_gate2, wz_hi, wz_lo) = shared(
            ("v_rows", [P, NT, D], F32), ("qk", [P, HEADS, 2, TOK], F32), ("k_dec", [P, HEADS, TOK], F32),
            ("s0", [P, 2, dec_batch, DV], F32), ("v_pair", [P, 2, DV], F32),
            ("log_g", [P, HEADS * TOK], F32), ("e_neg", [P, HEADS, TOK], F32), ("e_pos", [P, HEADS, TOK], F32),
            ("olo", [P, HEADS * VT, TOK], F32R), ("k_rows", [P, TOK], F32),
            ("scores", [P, TOK], F32), ("s_prompt", [P, seq // GCH, DV], F32),
            ("ot", [P, VT, TOK], F32), ("z_rows", [P, NT, RANK], F32), ("z_cols", [32, TOK], F32),
            ("wz", [P, KT, RANK], F32), ("w_gate2", [RANK + 1, HEADS * DH], F32),
            ("wz_hi", [P, KT, RANK], F32R), ("wz_lo", [P, KT, RANK], F32R))
        log_g_rows = log_g[:, :].rearrange("p (t f) -> p t f", t=NT)
        b_cum = log_g[:, :].rearrange("p (h t) -> p h t", h=HEADS)
        _, ohi, _, r_silu = shared(
            ("under_v_rows", [P, NT, D], F32), ("ohi", [P, HEADS * VT, TOK], F32R),
            ("under_k_dec_s0_v_pair", [P, HEADS * TOK + 2 * (dec_batch + 1) * DV], F32),
            ("r_silu", [P, HEADS * VT, TOK], F32))
        set_rows = [P, NT, KT * P]
        (uhi0, v0, v1, v2, ulo0, uhi1, uhi2, feat_rows, w_turned, b_spatial, u_tile, mixed, ln_stats, ln_mean_var,
         ln_var, ln_rstd) = shared(
            ("uhi0", [P, KT, TOK], F32R), ("v0", set_rows, F32), ("v1", set_rows, F32), ("v2", set_rows, F32),
            ("ulo0", [P, KT, TOK], F32R), ("uhi1", [P, KT, TOK], F32R), ("uhi2", [P, KT, TOK], F32R),
            ("feat_rows", [P, 2, 2, WIDE], F32),
            ("w_turned", [P, 2, SPATIAL, P], F32), ("b_spatial", [P, SPATIAL, P], F32), ("u_tile", [P, 2, TOK], F32),
            ("mixed", [P, 2, TOK], F32), ("ln_stats", [P, NT, V_CHUNKS, 6], F32), ("ln_mean_var", [P, NT, 2], F32),
            ("ln_var", [P, NT], F32), ("ln_rstd", [P, NT], F32))
        _, ulo1, ulo2, w_rows = shared(("under_uhi0", [P, KT, TOK], F32), ("ulo1", [P, KT, TOK], F32R),
                                       ("ulo2", [P, KT, TOK], F32R), ("w_rows", [P, 2, SPATIAL, P], F32))
        v_set, uhi, ulo = [v0, v1, v2], [uhi0, uhi1, uhi2], [ulo0, ulo1, ulo2]
        assert SGU_STEPS == len(v_set)
        next_hi, _, next_lo = shared(
            ("next_hi", [P, KT, WIDE], F32R), ("next_between", [P, FK * TOK - KT * WIDE], F32),
            ("next_lo", [P, KT, WIDE], F32R))
        weights = [(whi[:, 0], wlo[:, 0]), (whi[:, 1], wlo[:, 1]), (next_hi, next_lo)]
        NEXT = 2
        y_rows, = shared(("y_rows", [P, NT, D], F32))
        x_rows = yg[:, :, :].rearrange("p k t -> p (k t)").rearrange("p (n d) -> p n d", n=NT)

        banks = [ctx.enter_context(nc.psum_tensor(f"bank{i}", [P, BANK], F32)) for i in range(8)]
        proj = banks[:4]
        NPROJ = len(proj)
        stat = banks[4]

        const_in = sem("const_in")
        x_in = sem("x_in")
        landed = [sem(f"landed{i}") for i in range(2)]
        w_hi = sem("w_hi")
        w_lo = sem("w_lo")
        w_used = sem("w_used")
        y_first = sem("y_first")
        tile_out = sem("tile_out")
        consts_ready = sem("consts_ready")
        xt_ready = sem("xt_ready")
        x_new = sem("x_new")
        x_hi = sem("x_hi")
        x_lo = sem("x_lo")
        x_sq = sem("x_sq")
        x_acc = sem("x_acc")
        x_acc_pool = sem("x_acc_pool")
        y_sq = sem("y_sq")
        y_gain = sem("y_gain")
        y_acc = sem("y_acc")
        y_scaled = sem("y_scaled")
        y_scaled_pool = sem("y_scaled_pool")
        sums_ready = sem("sums_ready")
        mean_ready = sem("mean_ready")
        rstd_ready = sem("rstd_ready")
        diag_ready = sem("diag_ready")
        factor_ready = sem("factor_ready")
        pre_read = sem("pre_read")
        post_read = sem("post_read")
        silu_ready = sem("silu_ready")
        prod_ready = sem("prod_ready")
        h_hi = sem("h_hi")
        h_lo = sem("h_lo")
        gla_in = sem("gla_in")
        s0_in = [sem(f"s0_in{i}") for i in range(2)]
        s0_stored = [sem(f"s0_stored{i}") for i in range(2)]
        sp_stored = sem("sp_stored")
        wz_split = sem("wz_split")
        z_mm = sem("z_mm")
        z_evac = sem("z_evac")
        z_turned = sem("z_turned")
        g_abs = sem("g_abs")
        g_exp = sem("g_exp")
        g_log = sem("g_log")
        g_done = sem("g_done")
        b_copied = sem("b_copied")
        b_exp = sem("b_exp")
        b_diff = sem("b_diff")
        d_exp = sem("d_exp")
        k_decayed = sem("k_decayed")
        qk_ready = sem("qk_ready")
        qk_out = sem("qk_out")
        scores_mm = sem("scores_mm")
        k_turned = sem("k_turned")
        scores_out = sem("scores_out")
        k_out = sem("k_out")
        kv_mm = sem("kv_mm")
        s_done = sem("s_done")
        inter_mm = sem("inter_mm")
        o_mm = sem("o_mm")
        dec_mm = sem("dec_mm")
        dec_done = sem("dec_done")
        vp_done = sem("vp_done")
        o_sq = sem("o_sq")
        o_out = sem("o_out")
        o_acc = sem("o_acc")
        o_scaled = sem("o_scaled")
        o_gated = sem("o_gated")
        o_hi = sem("o_hi")
        o_lo = sem("o_lo")
        r_silu_done = sem("r_silu_done")
        ws_zero = sem("ws_zero")
        ws_in = sem("ws_in")
        ws_mm = sem("ws_mm")
        ws_done = sem("ws_done")
        rows_in = [sem(f"rows_in{i}") for i in range(2)]
        v_act = sem("v_act")
        v_stat = sem("v_stat")
        ln_aggr = sem("ln_aggr")
        ln_eps = sem("ln_eps")
        ln_pow = sem("ln_pow")
        ln_norm = sem("ln_norm")
        ln_gain = sem("ln_gain")
        ln_done = sem("ln_done")
        v_stored = sem("v_stored")
        mix_mm = sem("mix_mm")
        mix_out = sem("mix_out")
        u_act = sem("u_act")
        u_prod = sem("u_prod")
        u_hi = sem("u_hi")
        u_lo = sem("u_lo")
        yt_ready = sem("yt_ready")
        yt_out = sem("yt_out")
        stored = sem("stored")

        block = ctx.enter_context(nc.Block())

        def v_at(i, t):
            at = i % PER_SET * WIDE
            return v_set[i // PER_SET][:, t, at:at + WIDE]

        def gain(g, b, k):
            kind, layer, which = plan[b]
            return g[:, bass.ds((layer * 3 + which) * DK + k, 1)]

        def pairs_of_groups(eng, group, unroll):
            if unroll:
                for q in range(QUARTERS):
                    group(q, q % 2)
                return
            with eng.Fori(0, QUARTERS // 2) as it:
                for parity in range(2):
                    group(2 * it + parity, parity)

        @block.sync
        def _(sp):
            sp.dma_start(x_rows[:, 0:NP, :], xp).then_inc(x_in, 16)
            sp.dma_start(x_rows[:, NP, :], xs).then_inc(x_in, 16)
            sp.dma_start(ident_tri[:, :, :], a["ident_tri"]).then_inc(const_in, 16)
            sp.dma_start(pair_mask[:, :], a["pair_mask"]).then_inc(const_in, 16)
            sp.dma_start(g_pre[:, :], a["gain_pre"]).then_inc(const_in, 16)
            sp.dma_start(g_post[:, :], a["gain_post"]).then_inc(const_in, 16)
            sp.dma_start(g_head[:, :], a["gain_head"]).then_inc(const_in, 16)
            sp.dma_start(u_bias[:, :], a["u_bias"]).then_inc(const_in, 16)

            def load(n, src, slot, first=False):
                if not first:
                    sp.wait_ge(w_lo, n - 1)
                sp.dma_start(raw[:, slot], src).then_inc(landed[slot], 16)

            def by_k(w):
                return w.rearrange("(k p) c -> p k c", p=P)

            for b, (kind, layer, which) in enumerate(plan):
                n0 = chunk0[b]
                if kind == "ffn":
                    i = which // 2
                    gate, up = by_k(a["ffn_w_gate"][layer, i]), by_k(a["ffn_w_up"][layer, i])
                    down = by_k(a["ffn_w_down"][layer, i])
                    load(n0, gate[:, :, 0:WIDE], 0, b == 0)
                    load(n0 + 1, up[:, :, 0:WIDE], 1, b == 0)
                    with sp.Fori(1, FF // WIDE) as it:
                        load(n0 + 2 * it, gate[:, :, bass.ds(it * WIDE, WIDE)], 0)
                        load(n0 + 2 * it + 1, up[:, :, bass.ds(it * WIDE, WIDE)], 1)
                    with sp.Fori(0, QUARTERS) as q:
                        for step in range(DOWN_STEPS):
                            load(n0 + 2 * FF // WIDE + DOWN_STEPS * q + step,
                                 down[:, KT * step:KT * step + KT, bass.ds(q * WIDE, WIDE)], step % 2)
                if kind == "gla":
                    w_in, w_out = by_k(a["gla_w_in"][layer // 2]), by_k(a["gla_w_out"][layer // 2])
                    with sp.Fori(0, OUT_AT // 2) as it:
                        for slot in range(2):
                            load(n0 + 2 * it + slot, w_in[:, :, bass.ds((2 * it + slot) * WIDE, WIDE)], slot)
                    with sp.Fori(0, QUARTERS // 2) as it:
                        for slot in range(2):
                            load(n0 + OUT_AT + 2 * it + slot, w_out[:, :, bass.ds((2 * it + slot) * WIDE, WIDE)], slot)
                if kind == "sgu":
                    w_in, w_out = by_k(a["sgu_w_in"][layer // 2]), by_k(a["sgu_w_out"][layer // 2])
                    for at, start in ((0, HALF), (V_CHUNKS, 0)):
                        with sp.Fori(0, V_CHUNKS // 2) as it:
                            for slot in range(2):
                                load(n0 + at + 2 * it + slot,
                                     w_in[:, :, bass.ds((2 * it + slot) * WIDE + start, WIDE)], slot)
                    with sp.Fori(0, QUARTERS // 2) as it:
                        for c in range(2 * SGU_STEPS):
                            q, step = 2 * it + c // SGU_STEPS, c % SGU_STEPS
                            load(n0 + 2 * V_CHUNKS + 2 * SGU_STEPS * it + c,
                                 w_out[:, KT * step:KT * step + KT, bass.ds(q * WIDE, WIDE)], c % 2)
            for half in range(2):
                for t in range(NT):
                    g = half * NT + t
                    sp.wait_ge(yt_out, g + 1)
                    dst = (yp[:, t, :] if t < NP else ys)[:, half * BANK:(half + 1) * BANK]
                    sp.dma_start(dst, y_rows[:, t, half * BANK:(half + 1) * BANK]).then_inc(stored, 16)
            sp.wait_ge(stored, 16 * 2 * NT)

        @block.scalar
        def _(act):
            def round_chunk(n, slot, first=False):
                act.wait_ge(landed[slot], 8 * (n - slot) + 16)
                if not first:
                    act.wait_ge(w_used, n - 1)
                act.activation(whi[:, slot], raw[:, slot], ACT.Copy).then_inc(w_hi, 1)

            def round_next(n):
                act.wait_ge(landed[1], 8 * (n - 1) + 16)
                act.activation(next_hi[:, :, :], raw[:, 1], ACT.Copy).then_inc(w_hi, 1)

            def hi_x(b, k):
                act.wait_ge(x_new, DK * b + k + 1)
                act.activation(xhi[:, k, :], x[:, k, :], ACT.Copy, scale=gain(g_pre, b, k)).then_inc(x_hi, 1)

            def square_x(k):
                act.activation(yg[:, k, :], x[:, k, :], ACT.Square).then_inc(x_sq, 1)

            def pre_factor(b):
                act.wait_ge(factor_ready, stat0[b] + 1)
                act.activation(r_pre[:, :], stat[:, 0:TOK], ACT.Copy).then_inc(pre_read, 1)

            def output(b, n1, steps, started=False):
                def group(q, parity):
                    for step in range(steps):
                        n = n1 + q * steps + step
                        if n + 1 >= CHUNKS or started and n == n1:
                            continue
                        round_chunk(n + 1, (steps * parity + step + 1) % 2)
                        if n + 1 == chunk0[b + 1]:
                            round_next(n + 2)
                    for j in range(2):
                        m = 2 * q + j
                        if j == 0:
                            act.wait_ge(y_first, QUARTERS * b + q + 1)
                        else:
                            act.wait_ge(w_used, n1 + (q + 1) * steps)
                        act.wait_ge(y_acc, DK * b + max(m, 1))
                        psum = proj[2 * parity + j][:, 0:TOK]
                        act.activation(sq[:, j, :], psum, ACT.Square).then_inc(y_sq, 1)
                        act.activation(yg[:, bass.ds(m, 1), :], psum, ACT.Copy,
                                       scale=gain(g_post, b, m)).then_inc(tile_out, 1)
                for q in range(QUARTERS):
                    group(q, q % 2)
                act.wait_ge(factor_ready, stat0[b + 1])
                act.wait_ge(y_scaled, b + 1)
                act.activation(acc[:, :], stat[:, 0:TOK], ACT.Copy).then_inc(post_read, 1)

            act.wait_ge(const_in, 96)
            hi_x(0, 0)
            hi_x(0, 1)
            round_chunk(0, 0, True)
            for k in range(2, DK):
                hi_x(0, k)
            round_next(1)
            act.wait_ge(xt_ready, DK)
            for k in range(DK):
                square_x(k)
            for b, (kind, layer, which) in enumerate(plan):
                n0 = chunk0[b]
                if b > 0:
                    for k in range(DK):
                        hi_x(b, k)
                        square_x(k)
                if kind == "ffn":
                    f0 = ff0[b]

                    def silu(it):
                        for j in range(2):
                            act.wait_ge(tile_out, tile0[b] + 4 * it + j + 1)
                            act.activation(h_gate[:, j, :], h_gate[:, j, :], ACT.Silu).then_inc(silu_ready, 1)

                    def round_h(it):
                        for j in range(2):
                            act.wait_ge(prod_ready, f0 + 2 * it + j + 1)
                            act.activation(hhi[:, bass.ds(2 * it + j, 1), :], h_up[:, j:j + 1, :], ACT.Copy)\
                               .then_inc(h_hi, 1)

                    round_chunk(n0 + 2, 0)
                    pre_factor(b)
                    silu(0)
                    with act.Fori(1, FF // WIDE) as it:
                        round_chunk(n0 + 2 * it + 1, 1)
                        round_h(it - 1)
                        round_chunk(n0 + 2 * it + 2, 0)
                        silu(it)
                    round_h(FF // WIDE - 1)
                    output(b, n0 + 2 * FF // WIDE, DOWN_STEPS)
                if kind == "gla":
                    def tile_cols(buf, t):
                        return buf[:, :, t * P:(t + 1) * P]

                    act.wait_ge(gla_in, 48)
                    act.activation(wz_hi[:, :, :], wz[:, :, :], ACT.Copy).then_inc(wz_split, 1)
                    round_chunk(n0 + 2, 0)
                    pre_factor(b)
                    act.wait_ge(z_mm, 2)
                    act.wait_ge(z_turned, 1)
                    act.activation(z_cols[0:RANK, :], banks[6][0:RANK, 0:TOK], ACT.Copy).then_inc(z_turned, 1)
                    round_chunk(n0 + 3, 1)
                    act.wait_ge(z_mm, 3)
                    for t in range(NT):
                        act.activation(log_g_rows[:, t, :], banks[5 + t][:, :], ACT.Abs).then_inc(g_abs, 1)
                    round_chunk(n0 + 4, 0)
                    for t in range(NT):
                        act.wait_ge(g_abs, t + 1)
                        act.activation(log_g_rows[:, t, :], log_g_rows[:, t, :], ACT.Exp, scale=-1.0)\
                           .then_inc(g_exp, 1)
                    for t in range(NT):
                        act.wait_ge(g_exp, t + 1)
                        act.activation(log_g_rows[:, t, :], log_g_rows[:, t, :], ACT.Ln, bias=ones[:, 0:1])\
                           .then_inc(g_log, 1)
                    round_chunk(n0 + 5, 1)
                    for t in range(NT):
                        act.wait_ge(b_copied, t + 1)
                        act.activation(tile_cols(e_pos, t), tile_cols(b_cum, t), ACT.Exp, scale=1 / GLA_TAU)\
                           .then_inc(b_exp, 1)
                        act.activation(tile_cols(e_neg, t), tile_cols(b_cum, t), ACT.Exp, scale=-1 / GLA_TAU)\
                           .then_inc(b_exp, 1)
                    round_chunk(n0 + 6, 0)
                    act.wait_ge(b_diff, 2)
                    act.activation(k_dec[:, :, :], k_dec[:, :, :], ACT.Exp, scale=1 / GLA_TAU).then_inc(d_exp, 1)
                    round_chunk(n0 + 7, 1)
                    round_chunk(n0 + 8, 0)

                    def round_o(h):
                        for i in range(VT):
                            act.wait_ge(o_gated, VT * h + i + 1)
                            act.activation(ohi[:, VT * h + i, :], ot[:, i, :], ACT.Copy).then_inc(o_hi, 1)

                    for h in range(HEADS):
                        act.wait_ge(k_turned, h + 1)
                        act.activation(k_rows[:, :], banks[3][:, 0:TOK], ACT.Copy).then_inc(k_out, 1)
                        round_chunk(n0 + R_AT + h + 1, (h + 1) % 2)
                        if h > 0:
                            round_o(h - 1)
                        act.wait_ge(o_mm, h + 1)
                        if h > 0:
                            act.wait_ge(o_acc, h)
                            act.wait_ge(o_lo, VT * h)
                        for i in range(VT):
                            act.activation(sq[:, i, :], banks[5 + i][:, 0:TOK], ACT.Square).then_inc(o_sq, 1)
                        for i in range(VT):
                            act.activation(ot[:, i, :], banks[5 + i][:, 0:TOK], ACT.Copy,
                                           scale=g_head[:, i:i + 1]).then_inc(o_out, 1)
                        for i in range(VT):
                            act.wait_ge(tile_out, tile0[b] + R_TILE + VT * h + i + 1)
                            act.activation(r_silu[:, VT * h + i, :], r_silu[:, VT * h + i, :], ACT.Silu)\
                               .then_inc(r_silu_done, 1)
                    round_chunk(n0 + OUT_AT + 1, 1)
                    round_o(HEADS - 1)
                    output(b, n0 + OUT_AT, 1, started=True)
                if kind == "sgu":
                    def v_gelu(i):
                        for t in range(NT):
                            act.wait_ge(tile_out, tile0[b] + NT * i + t + 1)
                            act.activation(v_at(i, t), v_at(i, t), ACT.Gelu).then_inc(v_act, 1)

                    def round_u(i):
                        for j in range(2):
                            c = 2 * i + j
                            act.wait_ge(u_prod, c + 1)
                            act.activation(uhi[c // KT][:, c % KT, :], u_tile[:, j, :], ACT.Copy).then_inc(u_hi, 1)

                    round_chunk(n0 + 2, 0)
                    v_gelu(0)
                    pre_factor(b)
                    for i in range(1, V_CHUNKS):
                        if i > 1:
                            round_chunk(n0 + i + 1, (i + 1) % 2)
                        v_gelu(i)
                    for i in range(V_CHUNKS):
                        round_chunk(n0 + V_CHUNKS + i + 1, (i + 1) % 2)
                        if i > 0:
                            round_u(i - 1)
                        for j in range(2):
                            c = 2 * i + j
                            act.wait_ge(tile_out, tile0[b] + U_TILE + c + 1)
                            act.activation(u_tile[:, j, :], u_tile[:, j, :], ACT.Gelu, bias=u_bias[:, c:c + 1])\
                               .then_inc(u_act, 1)
                    round_u(V_CHUNKS - 1)
                    output(b, n0 + 2 * V_CHUNKS, SGU_STEPS)
            for g in range(2 * NT):
                half, t = divmod(g, NT)
                act.wait_ge(yt_ready, g + 1)
                act.activation(y_rows[:, t, half * BANK:(half + 1) * BANK], proj[g % NPROJ][:, :], ACT.Copy)\
                   .then_inc(yt_out, 1)

        @block.vector
        def _(dve):
            def split_chunk(n, slot):
                dve.wait_ge(w_hi, n + 1)
                dve.tensor_tensor(wlo[:, slot], raw[:, slot], whi[:, slot].bitcast(F32), ALU.subtract)\
                   .then_inc(w_lo, 1)

            def lo_x(b, k):
                dve.wait_ge(x_hi, DK * b + k + 1)
                dve.scalar_tensor_tensor(xlo[:, k, :], x[:, k, :], gain(g_pre, b, k), xhi[:, k, :].bitcast(F32),
                                         ALU.mult, ALU.subtract).then_inc(x_lo, 1)

            def split_next(n):
                dve.wait_ge(w_hi, n + 1)
                dve.tensor_tensor(next_lo[:, :, :], raw[:, 1], next_hi[:, :, :].bitcast(F32), ALU.subtract)\
                   .then_inc(w_lo, 1)

            def mean(s, features):
                dve.wait_ge(sums_ready, s + 1)
                dve.tensor_scalar(mean_sq[:, :], stat[:, TOK:TOK + NT], 1.0 / features, RMS_EPS, ALU.mult, ALU.add)\
                   .then_inc(mean_ready, 1)

            def spread(s, buf, scale=1.0):
                dve.wait_ge(rstd_ready, s + 1)
                for t in range(NT):
                    last = dve.tensor_scalar(diag[:, t * P:(t + 1) * P], ident, rstd[:, buf, t:t + 1], scale,
                                             ALU.mult, ALU.mult)
                last.then_inc(diag_ready, 1)

            def pre_acc(b):
                dve.wait_ge(x_sq, DK * (b + 1))
                dve.tensor_tensor(yg[:, 4:6, :], yg[:, 4:6, :], yg[:, 6:8, :], ALU.add).then_inc(x_acc, 1)
                dve.wait_ge(x_acc_pool, 2 * (b + 1))
                dve.wait_ge(x_acc, 3 * b + 1)
                dve.tensor_tensor(yg[:, 4:6, :], yg[:, 4:6, :], yg[:, 0:3:2, :], ALU.add).then_inc(x_acc, 1)
                dve.wait_ge(x_acc, 3 * b + 2)
                dve.tensor_tensor(yg[:, 4, :], yg[:, 4, :], yg[:, 5, :], ALU.add).then_inc(x_acc, 1)

            def output(b, n1, steps, started=False):
                if b > 0:
                    dve.wait_ge(y_scaled_pool, (DK - 1) * b)
                dve.memset(acc[:, :], 0.0).then_inc(y_acc, 1)
                for q in range(QUARTERS):
                    for step in range(steps):
                        n = n1 + q * steps + step
                        if n + 1 >= CHUNKS or started and n == n1:
                            continue
                        split_chunk(n + 1, (n + 1) % 2)
                        if n + 1 == chunk0[b + 1]:
                            split_next(n + 2)
                    for j in range(2):
                        m = 2 * q + j
                        if m == DK - 1:
                            continue
                        dve.wait_ge(y_sq, DK * b + m + 1)
                        dve.wait_ge(y_acc, DK * b + 1 + m)
                        dve.tensor_tensor(acc[:, :], acc[:, :], sq[:, j, :], ALU.add).then_inc(y_acc, 1)

            dve.memset(ones[:, :], 1.0).then_inc(consts_ready, 1)
            dve.wait_ge(const_in, 96)
            for k in range(DK):
                dve.wait_ge(xt_ready, k + 1)
                dve.tensor_copy(x[:, k, :], proj[k % NPROJ][:, 0:TOK]).then_inc(x_new, 1)
            split_chunk(0, 0)
            for k in range(DK):
                lo_x(0, k)
            split_next(1)
            for b, (kind, layer, which) in enumerate(plan):
                n0, T0, last = chunk0[b], tile0[b], b == len(plan) - 1
                if kind == "ffn":
                    f0 = ff0[b]

                    def gate(it, first):
                        dve.wait_ge(w_used, n0 + 2 * it + 1)
                        for j in range(2):
                            if not first:
                                dve.wait_ge(prod_ready, f0 + 2 * it + j - 1)
                            dve.tensor_tensor(h_gate[:, j, :], proj[j][:, 0:TOK], r_pre[:, :], ALU.mult)\
                               .then_inc(tile_out, 1)

                    def product(it, first):
                        T, f = T0 + 4 * it + 2, f0 + 2 * it
                        dve.wait_ge(w_used, n0 + 2 * it + 2)
                        for j in range(2):
                            if not first:
                                dve.wait_ge(h_lo, f + j - 1)
                            dve.tensor_tensor(h_up[:, j, :], proj[2 + j][:, 0:TOK], r_pre[:, :], ALU.mult)\
                               .then_inc(tile_out, 1)
                        for j in range(2):
                            dve.wait_ge(tile_out, T + j + 1)
                            dve.wait_ge(silu_ready, f + j + 1)
                            dve.tensor_tensor(h_up[:, j, :], h_up[:, j, :], h_gate[:, j, :], ALU.mult)\
                               .then_inc(prod_ready, 1)

                    pre_acc(b)
                    mean(stat0[b], D)
                    spread(stat0[b], 0)
                    split_chunk(n0 + 2, 0)
                    dve.wait_ge(pre_read, b + 1)
                    gate(0, b == 0)
                    product(0, b == 0)
                    split_chunk(n0 + 3, 1)
                    gate(1, False)
                    split_chunk(n0 + 4, 0)
                    with dve.Fori(2, FF // WIDE) as it:
                        product(it - 1, False)
                        split_chunk(n0 + 2 * it + 1, 1)
                        gate(it, False)
                        split_chunk(n0 + 2 * it + 2, 0)
                    product(FF // WIDE - 1, False)
                    output(b, n0 + 2 * FF // WIDE, DOWN_STEPS)
                if kind == "gla":
                    dve.memset(scores[:, :], 0.0).then_inc(scores_out, 1)
                    dve.wait_ge(wz_split, 1)
                    dve.tensor_tensor(wz_lo[:, :, :], wz[:, :, :], wz_hi[:, :, :].bitcast(F32), ALU.subtract)\
                       .then_inc(wz_split, 1)
                    pre_acc(b)
                    mean(stat0[b], D)
                    spread(stat0[b], 0)
                    dve.wait_ge(z_mm, 1)
                    for t in range(NT):
                        dve.tensor_scalar(z_rows[:, t, :], banks[7][:, t * RANK:(t + 1) * RANK], rstd[:, 0, t:t + 1],
                                          None, ALU.mult).then_inc(z_evac, 1)
                    split_chunk(n0 + 2, 0)
                    dve.wait_ge(pre_read, b + 1)

                    def evac_qk(i):
                        dve.wait_ge(w_used, n0 + i + 1)
                        which_qk, at = divmod(i, Q_CHUNKS)
                        for j in range(2):
                            dve.scalar_tensor_tensor(qk[:, 2 * at + j, which_qk, :], proj[2 * (i % 2) + j][:, 0:TOK],
                                                     (DH ** -0.5, 1.0)[which_qk], r_pre[:, :], ALU.mult, ALU.mult)\
                               .then_inc(tile_out, 1)

                    def evac_v(h):
                        dve.wait_ge(w_used, n0 + 2 * Q_CHUNKS + h + 1)
                        for t in range(NT):
                            dve.tensor_scalar(v_rows[:, t, h * DV:(h + 1) * DV], proj[(NT * h + t) % NPROJ][:, 0:DV],
                                              rstd[:, 0, t:t + 1], None, ALU.mult).then_inc(tile_out, 1)

                    evac_qk(0)
                    split_chunk(n0 + 3, 1)
                    evac_qk(1)
                    split_chunk(n0 + 4, 0)
                    evac_qk(2)
                    for t in range(NT):
                        dve.wait_ge(g_log, t + 1)
                        dve.scalar_tensor_tensor(log_g_rows[:, t, :], banks[5 + t][:, :], 0.0, log_g_rows[:, t, :],
                                                 ALU.min, ALU.subtract).then_inc(g_done, 1)
                    split_chunk(n0 + 5, 1)
                    evac_qk(3)
                    dve.wait_ge(z_mm, 4)
                    for t in range(NT):
                        dve.tensor_copy(b_cum[:, :, t * P:(t + 1) * P],
                                        banks[5 + t][:, :].rearrange("p (h t) -> p h t", h=HEADS))\
                           .then_inc(b_copied, 1)
                    dve.wait_ge(b_copied, NT)
                    for at, size, span in ((0, seq, GCH), (seq, P, dec_seq)):
                        cut = lambda buf: buf[:, :, at:at + size].rearrange("p h (c l) -> p h c l", l=span)
                        dve.tensor_tensor(cut(k_dec), cut(b_cum)[:, :, :, span - 1:span].to_broadcast(
                                              [P, HEADS, size // span, span]), cut(b_cum), ALU.subtract)\
                           .then_inc(b_diff, 1)
                    evac_v(0)
                    split_chunk(n0 + 6, 0)
                    evac_v(1)
                    dve.wait_ge(d_exp, 1)
                    for h in range(HEADS):
                        dve.tensor_tensor(k_dec[:, h, :], k_dec[:, h, :], qk[:, h, 1, :], ALU.mult)\
                           .then_inc(k_decayed, 1)
                    split_chunk(n0 + 7, 1)
                    evac_v(2)
                    dve.wait_ge(b_exp, 2 * NT)
                    for h in range(HEADS):
                        dve.tensor_tensor(qk[:, h, 0, :], qk[:, h, 0, :], e_pos[:, h, :], ALU.mult)
                        dve.tensor_tensor(qk[:, h, 1, :], qk[:, h, 1, :], e_neg[:, h, :], ALU.mult)\
                           .then_inc(qk_ready, 1)
                    split_chunk(n0 + 8, 0)
                    evac_v(3)

                    def gate_o(h):
                        dve.wait_ge(factor_ready, stat0[b] + 2 + h)
                        dve.wait_ge(o_out, VT * (h + 1))
                        dve.wait_ge(r_silu_done, VT * (h + 1))
                        for i in range(VT):
                            dve.tensor_tensor(ot[:, i, :], ot[:, i, :], stat[:, 0:TOK], ALU.mult)\
                               .then_inc(o_scaled, 1)
                        for i in range(VT):
                            dve.wait_ge(o_scaled, VT * h + i + 1)
                            dve.tensor_tensor(ot[:, i, :], ot[:, i, :], r_silu[:, VT * h + i, :], ALU.mult)\
                               .then_inc(o_gated, 1)
                        for i in range(VT):
                            dve.wait_ge(o_hi, VT * h + i + 1)
                            dve.tensor_tensor(olo[:, VT * h + i, :], ot[:, i, :], ohi[:, VT * h + i, :].bitcast(F32),
                                              ALU.subtract).then_inc(o_lo, 1)

                    for h in range(HEADS):
                        dve.wait_ge(scores_mm, h + 1)
                        if h == 0:
                            dve.wait_ge(scores_out, 1)
                        for t in range(NT):
                            cols = slice(t * P, (t + 1) * P)
                            dve.copy_predicated(scores[:, cols], tri_tok[t].bitcast(U32), banks[2][:, cols])\
                               .then_inc(scores_out, 1)
                        dve.wait_ge(tile_out, T0 + R_TILE)
                        for i in range(2):
                            dve.tensor_scalar(v_pair[:, i, :], v_rows[:, NP, h * DV:(h + 1) * DV],
                                              pair_mask[:, i:i + 1], None, ALU.mult).then_inc(vp_done, 1)
                        for c in range(seq // GCH):
                            product = banks[7 if c % 2 == 0 else 2][:, c // 2 * DV:(c // 2 + 1) * DV]
                            dve.wait_ge(kv_mm, 2 * h + 1 + c % 2)
                            if c == 0:
                                if h > 0:
                                    dve.wait_ge(sp_stored, 16 * h)
                                dve.tensor_copy(s_prompt[:, 0, :], product).then_inc(s_done, 1)
                            else:
                                dve.wait_ge(s_done, seq // GCH * h + c)
                                dve.scalar_tensor_tensor(s_prompt[:, c, :], s_prompt[:, c - 1, :],
                                                         e_pos[:, h, (c + 1) * GCH - 1:(c + 1) * GCH], product,
                                                         ALU.mult, ALU.add).then_inc(s_done, 1)
                        if h > 0:
                            mean(stat0[b] + h, DV)
                        split_chunk(n0 + R_AT + h + 1, (h + 1) % 2)
                        if h > 0:
                            spread(stat0[b] + h, 1)
                            gate_o(h - 1)
                        for c in range(dec_batch):
                            dve.wait_ge(dec_mm, dec_batch // 2 * h + c // 2 + 1)
                            last_token = seq + (c + 1) * dec_seq - 1
                            state = s0[:, h % 2, c, :]
                            dve.scalar_tensor_tensor(state, state, e_pos[:, h, last_token:last_token + 1],
                                                     banks[DEC_BANKS[c // 2]][:, c % 2 * DV:(c % 2 + 1) * DV],
                                                     ALU.mult, ALU.add).then_inc(dec_done, 1)
                        dve.wait_ge(w_used, n0 + R_AT + h + 1)
                        for i in range(VT):
                            dve.tensor_tensor(r_silu[:, VT * h + i, :], proj[i][:, 0:TOK], r_pre[:, :], ALU.mult)\
                               .then_inc(tile_out, 1)
                        dve.wait_ge(o_sq, VT * (h + 1))
                        dve.tensor_tensor(acc[:, :], sq[:, 0, :], sq[:, 1, :], ALU.add).then_inc(o_acc, 1)
                    split_chunk(n0 + OUT_AT + 1, 1)
                    mean(stat0[b] + HEADS, DV)
                    spread(stat0[b] + HEADS, 1)
                    gate_o(HEADS - 1)
                    output(b, n0 + OUT_AT, 1, started=True)
                if kind == "sgu":
                    def v_evac(i):
                        dve.wait_ge(rows_in[i % 2], 16 * (i // 2 + 1))
                        dve.wait_ge(w_used, n0 + i + 1)
                        for t in range(NT):
                            bank = banks[4 + t] if i == 1 and t > 0 else proj[(NT * i + t) % NPROJ]
                            dve.scalar_tensor_tensor(v_at(i, t), bank[:, 0:WIDE],
                                                     rstd[:, 0, t:t + 1], feat_rows[:, i % 2, 0, :],
                                                     ALU.mult, ALU.add).then_inc(tile_out, 1)

                    def v_stats(i):
                        for t in range(NT):
                            dve.wait_ge(v_act, NT * i + t + 1)
                            dve.bn_stats(ln_stats[:, t, i, :], v_at(i, t)).then_inc(v_stat, 1)

                    def normalise(i):
                        for t in range(NT):
                            dve.tensor_scalar(v_at(i, t), v_at(i, t), ln_mean_var[:, t, 0:1], ln_rstd[:, t:t + 1],
                                              ALU.subtract, ALU.mult).then_inc(ln_norm, 1)

                    def u_product(i):
                        for j in range(2):
                            dve.wait_ge(u_act, 2 * i + j + 1)
                            dve.wait_ge(mix_out, 4 * i + 2 * j + 2)
                            dve.tensor_tensor(u_tile[:, j, :], u_tile[:, j, :], mixed[:, j, :], ALU.mult)\
                               .then_inc(u_prod, 1)

                    pre_acc(b)
                    split_chunk(n0 + 2, 0)
                    mean(stat0[b], D)
                    spread(stat0[b], 0)
                    v_evac(0)
                    for i in range(1, V_CHUNKS):
                        if i > 1:
                            split_chunk(n0 + i + 1, (i + 1) % 2)
                        v_evac(i)
                        if i == 2:
                            dve.wait_ge(ws_mm, 1)
                            for w, mask in enumerate((ident_tri[:, 1:2, :], ident_tri[:, 3:4, :])):
                                dve.tensor_tensor(w_turned[:, w], banks[5 + w][:, :].rearrange("p (g t) -> p g t", g=SPATIAL),
                                                  mask.to_broadcast([P, SPATIAL, P]), ALU.mult).then_inc(ws_done, 1)
                        v_stats(i - 1)
                    v_stats(V_CHUNKS - 1)
                    dve.wait_ge(v_stat, NT * V_CHUNKS)
                    for t in range(NT):
                        dve.bn_aggr(ln_mean_var[:, t, :], ln_stats[:, t].rearrange("p c s -> p (c s)"))\
                           .then_inc(ln_aggr, 1)
                    dve.wait_ge(ln_aggr, NT)
                    dve.tensor_scalar(ln_var[:, :], ln_mean_var[:, :, 1], LN_EPS, None, ALU.add).then_inc(ln_eps, 1)
                    dve.wait_ge(ln_pow, 1)
                    normalise(0)
                    dve.wait_ge(ws_in, 16 * (dec_batch + 2))
                    for i in range(V_CHUNKS):
                        if i > 0:
                            u_product(i - 1)
                        split_chunk(n0 + V_CHUNKS + i + 1, (i + 1) % 2)
                        if i + 1 < V_CHUNKS:
                            normalise(i + 1)
                        dve.wait_ge(mix_mm, i + 1)
                        if i > 0:
                            dve.wait_ge(u_prod, 2 * i)
                        for j in range(2):
                            g = (2 * i + j) * SPATIAL // (HALF // P)
                            for at, size, span in ((0, seq, P), (seq, P, dec_seq)):
                                cut = lambda buf: buf.rearrange("p (c l) -> p c l", l=span)
                                dve.tensor_tensor(cut(mixed[:, j, at:at + size]), cut(banks[5 + j][:, at:at + size]),
                                                  b_spatial[:, g:g + 1, 0:span].to_broadcast([P, size // span, span]),
                                                  ALU.add).then_inc(mix_out, 1)
                        dve.wait_ge(w_used, n0 + V_CHUNKS + i + 1)
                        for j in range(2):
                            if i > 0:
                                dve.wait_ge(u_lo, 2 * i + j - 1)
                            dve.tensor_tensor(u_tile[:, j, :], proj[2 * (i % 2) + j][:, 0:TOK], r_pre[:, :], ALU.mult)\
                               .then_inc(tile_out, 1)
                    u_product(V_CHUNKS - 1)
                    output(b, n0 + 2 * V_CHUNKS, SGU_STEPS)
                s = stat0[b + 1] - 1
                mean(s, D)
                spread(s, 1, 0.5 if kind == "ffn" else 1.0)
                dve.wait_ge(factor_ready, s + 1)
                dve.tensor_tensor(yg[:, 0, :], yg[:, 0, :], stat[:, 0:TOK], ALU.mult).then_inc(y_scaled, 1)
                for k in range(DK):
                    if k == 0:
                        dve.wait_ge(y_scaled, b + 1)
                    else:
                        dve.wait_ge(y_scaled_pool, (DK - 1) * b + k)
                    dve.tensor_tensor(x[:, k, :], x[:, k, :], yg[:, k, :], ALU.add).then_inc(x_new, 1)
                    if k > 0 and not last:
                        lo_x(b + 1, k - 1)
                if not last:
                    lo_x(b + 1, DK - 1)

        @block.gpsimd
        def _(pool):
            def power(s, buf):
                pool.wait_ge(mean_ready, s + 1)
                pool.tensor_tensor(rstd[:, buf, :], mean_sq[:, :], minus_half[:, :].to_broadcast([P, NT]), ALU.pow)\
                    .then_inc(rstd_ready, 1)

            def pre_acc(b):
                for k in (0, 2):
                    pool.wait_ge(x_sq, DK * b + k + 2)
                    pool.tensor_tensor(yg[:, k, :], yg[:, k, :], yg[:, k + 1, :], ALU.add).then_inc(x_acc_pool, 1)
                power(stat0[b], 0)

            pool.memset(minus_half[:, :], -0.5).then_inc(consts_ready, 1)
            pool.wait_ge(consts_ready, 2)

            for b, (kind, layer, which) in enumerate(plan):
                if kind == "gla":
                    def load_s0(h):
                        pool.dma_start(s0[:, h % 2], a["state_gla"][layer // 2, :, h].rearrange("b p v -> p b v"))\
                            .then_inc(s0_in[h % 2], 16)

                    j = layer // 2
                    pool.wait_ge(x_new, DK * b + 1)
                    with nc.allow_non_contiguous_dma(reason="16 columns of w_in"):
                        pool.dma_start(wz[:, :, :], a["gla_w_in"][j].rearrange("(k p) c -> p k c", p=P)[
                            :, :, OUT_AT * WIDE:OUT_AT * WIDE + RANK]).then_inc(gla_in, 16)
                    pool.dma_start(w_gate2[0:RANK, :], a["gla_w_gate2"][j]).then_inc(gla_in, 16)
                    pool.dma_start(w_gate2[RANK:RANK + 1, :], a["gla_b_gate"][j:j + 1]).then_inc(gla_in, 16)
                    pool.memset(z_cols[:, :], 1.0).then_inc(z_turned, 1)
                    pre_acc(b)
                    load_s0(0)
                    load_s0(1)
                if kind == "sgu":
                    j = layer // 2

                    def load_bias(i):
                        pool.dma_start(feat_rows[:, i % 2, 0, :], a["sgu_b_in"][j:j + 1, HALF + i * WIDE:
                                       HALF + (i + 1) * WIDE].to_broadcast([P, WIDE])).then_inc(rows_in[i % 2], 16)

                    pool.wait_ge(x_new, DK * b + 1)
                    load_bias(0)
                    load_bias(1)
                    pre_acc(b)
                    pool.memset(w_rows[:, 1], 0.0).then_inc(ws_zero, 1)
                    pool.dma_start(w_rows[:, 0], a["sgu_w_s"][j].rearrange("g t s -> t g s")).then_inc(ws_in, 16)
                    pool.dma_start(b_spatial[:, :, :].rearrange("p g t -> p (g t)"), a["sgu_b_s"][j:j + 1].rearrange(
                        "a g t -> a (g t)").to_broadcast([P, SPATIAL * P])).then_inc(ws_in, 16)
                    pool.wait_ge(ws_zero, 1)
                    for c in range(dec_batch):
                        at = slice(c * dec_seq, (c + 1) * dec_seq)
                        pool.dma_start(w_rows[at, 1, :, at], a["sgu_w_s"][j, :, 0:dec_seq, 0:dec_seq].rearrange(
                            "g t s -> t g s")).then_inc(ws_in, 16)
                if kind == "ffn":
                    pre_acc(b)
                    with pool.Fori(0, FF // WIDE) as it:
                        for j in range(2):
                            pool.wait_ge(h_hi, ff0[b] + 2 * it + j + 1)
                            at = bass.ds(2 * it + j, 1)
                            pool.tensor_tensor(hlo[:, at, :], h_up[:, j:j + 1, :], hhi[:, at, :].bitcast(F32),
                                               ALU.subtract).then_inc(h_lo, 1)
                if kind == "gla":
                    for h in range(HEADS):
                        pool.wait_ge(dec_done, dec_batch * (h + 1))
                        pool.wait_ge(s_done, seq // GCH * (h + 1))
                        pool.dma_start(outs["gla_state_prompt"][layer // 2, 0, h], s_prompt[:, seq // GCH - 1, :])\
                            .then_inc(sp_stored, 16)
                        pool.dma_start(outs["gla_state_sample"][layer // 2, :, h].rearrange("b p v -> p b v"),
                                       s0[:, h % 2]).then_inc(s0_stored[h % 2], 16)
                        if h + 2 < HEADS:
                            pool.wait_ge(s0_stored[h % 2], 16)
                            load_s0(h + 2)
                        power(stat0[b] + 1 + h, 1)
                    pool.wait_ge(sp_stored, 16 * HEADS)
                    for i in range(2):
                        pool.wait_ge(s0_stored[i], 16 * HEADS // 2)
                if kind == "sgu":
                    def load_ln(i):
                        for which_row, name in enumerate(("sgu_ln_g", "sgu_ln_b")):
                            pool.dma_start(feat_rows[:, i % 2, which_row, :], a[name][j:j + 1, i * WIDE:(i + 1) * WIDE]
                                           .to_broadcast([P, WIDE])).then_inc(rows_in[i % 2], 16)

                    def affine(i):
                        at = i % PER_SET * WIDE
                        v = v_set[i // PER_SET][:, :, at:at + WIDE]
                        pool.wait_ge(rows_in[i % 2], 16 * (V_CHUNKS // 2 + 2 * (i // 2 + 1)))
                        pool.wait_ge(ln_norm, NT * (i + 1))
                        pool.tensor_tensor(v, v, feat_rows[:, i % 2, 0:1, :].to_broadcast([P, NT, WIDE]), ALU.mult)\
                            .then_inc(ln_gain, 1)
                        pool.wait_ge(ln_gain, i + 1)
                        pool.tensor_tensor(v, v, feat_rows[:, i % 2, 1:2, :].to_broadcast([P, NT, WIDE]), ALU.add)\
                            .then_inc(ln_done, 1)
                        pool.wait_ge(ln_done, i + 1)
                        if i + 2 < V_CHUNKS:
                            load_ln(i + 2)
                        if i % PER_SET == PER_SET - 1:
                            at = i // PER_SET * KT * P
                            pool.dma_start(outs["sgu_v_sample"][j].rearrange("b l c -> (b l) c")[:, at:at + KT * P],
                                           v_set[i // PER_SET][:, NP, :]).then_inc(v_stored, 16)

                    for i in range(2, V_CHUNKS):
                        pool.wait_ge(tile_out, tile0[b] + NT * (i - 1))
                        load_bias(i)
                    for i in range(2):
                        pool.wait_ge(tile_out, tile0[b] + NT * (V_CHUNKS - 1 + i))
                        load_ln(i)
                    pool.wait_ge(ln_eps, 1)
                    pool.tensor_tensor(ln_rstd[:, :], ln_var[:, :], minus_half[:, :].to_broadcast([P, NT]), ALU.pow)\
                        .then_inc(ln_pow, 1)
                    affine(0)
                    for i in range(V_CHUNKS):
                        if i + 1 < V_CHUNKS:
                            affine(i + 1)
                        for c in (2 * i, 2 * i + 1):
                            if c == KT:
                                pool.wait_ge(mix_mm, PER_SET)
                                pool.wait_ge(v_stored, 16)
                            if c == 2 * KT:
                                pool.wait_ge(mix_mm, 2 * PER_SET)
                                pool.wait_ge(v_stored, 32)
                            pool.wait_ge(u_hi, c + 1)
                            pool.tensor_tensor(ulo[c // KT][:, c % KT, :], u_tile[:, c % 2, :],
                                               uhi[c // KT][:, c % KT, :].bitcast(F32), ALU.subtract)\
                                .then_inc(u_lo, 1)
                    pool.wait_ge(v_stored, 48)
                power(stat0[b + 1] - 1, 1)
                pool.wait_ge(post_read, b + 1)
                pool.wait_ge(tile_out, tile0[b + 1])
                for k in range(1, DK):
                    pool.tensor_tensor(yg[:, k, :], yg[:, k, :], acc[:, :], ALU.mult).then_inc(y_scaled_pool, 1)

        @block.tensor
        def _(pe):
            def multiply(out, slot, k, j, rhs_hi, rhs_lo, start, stop):
                cols = slice(j * P, (j + 1) * P)
                w_hi_part, w_lo_part = weights[slot]
                pe.matmul(out, w_hi_part[:, k, cols], rhs_hi, start=start, stop=False)
                pe.matmul(out, w_hi_part[:, k, cols], rhs_lo, start=False, stop=False)
                return pe.matmul(out, w_lo_part[:, k, cols], rhs_hi, start=False, stop=stop)

            def sums(*parts):
                for t in range(NT):
                    cols = slice(t * P, (t + 1) * P)
                    for i, part in enumerate(parts):
                        last = pe.matmul(stat[:, TOK + t:TOK + t + 1], part[:, cols], ones[:, 0:1], start=i == 0,
                                         stop=i == len(parts) - 1)
                last.then_inc(sums_ready, 1)

            def factors(s):
                pe.wait_ge(diag_ready, s + 1)
                pe.matmul(stat[:, 0:TOK], ones[:, :], diag[:, :], start=True, stop=True).then_inc(factor_ready, 1)

            def multiply_rows(out, slot, k, t, start, stop):
                cols = slice(t * P, (t + 1) * P)
                w_hi_part, w_lo_part = weights[slot]
                pe.matmul(out, xhi[:, k, cols], w_hi_part[:, k, :], start=start, stop=False)
                pe.matmul(out, xhi[:, k, cols], w_lo_part[:, k, :], start=False, stop=False)
                return pe.matmul(out, xlo[:, k, cols], w_hi_part[:, k, :], start=False, stop=stop)

            def first_chunk(b):
                pe.wait_ge(w_lo, chunk0[b] + 1)
                if b > 0:
                    pe.wait_ge(tile_out, tile0[b])
                for k in range(KT):
                    pe.wait_ge(x_lo, DK * b + k + 1)
                    if plan[b][0] == "sgu":
                        for t in range(NT):
                            mm = multiply_rows(proj[t][:, 0:WIDE], 0, k, t, k == 0, k == KT - 1)
                        continue
                    for j in range(2):
                        mm = multiply(proj[j][:, 0:TOK], 0, k, j, xhi[:, k, :], xlo[:, k, :], k == 0, k == KT - 1)
                mm.then_inc(w_used, 1)

            def pre_sums(b):
                pe.wait_ge(x_acc, 3 * (b + 1))
                if b > 0:
                    pe.wait_ge(post_read, b)
                sums(yg[:, 4, :])

            def tile(bank, slot, j, midway=None):
                for k in range(KT):
                    if midway and k == KT // 2:
                        midway()
                    mm = multiply(proj[bank][:, 0:TOK], slot, k, j, xhi[:, k, :], xlo[:, k, :], k == 0, k == KT - 1)
                return mm

            def output(b, n1, T1, steps, rhs, in_order=False):
                def group(q, parity):
                    if in_order and q == 0:
                        pe.wait_ge(tile_out, T1)
                        pe.wait_ge(w_lo, n1 + 1)
                        for k in range(KT):
                            pe.wait_ge(rhs(0)[2], k + 1)
                            for j in range(2):
                                mm = multiply(proj[j][:, 0:TOK], 0, k, j, rhs(0)[0][:, k, :], rhs(0)[1][:, k, :],
                                              k == 0, k == KT - 1)
                                if k == KT - 1:
                                    mm.then_inc((y_first, w_used)[j], 1)
                        return
                    pe.wait_ge(tile_out, T1 + 2 * q - 2)
                    for step in range(steps):
                        n = n1 + q * steps + step
                        pe.wait_ge(w_lo, n + 1)
                        ready, count = rhs(step)[2:]
                        if not in_order:
                            pe.wait_ge(ready, count)
                        for j in range(2):
                            for k in range(KT):
                                hi, lo = rhs(step)[:2]
                                mm = multiply(proj[2 * parity + j][:, 0:TOK], (steps * parity + step) % 2, k, j,
                                              hi[:, k, :], lo[:, k, :], step == k == 0,
                                              step == steps - 1 and k == KT - 1)
                            if j == 0 and step == steps - 1:
                                mm.then_inc(y_first, 1)
                        mm.then_inc(w_used, 1)
                pairs_of_groups(pe, group, in_order)
                pe.wait_ge(y_acc, DK * (b + 1))
                pe.wait_ge(y_sq, DK * (b + 1))
                pe.wait_ge(pre_read, b + 1)
                if kind == "gla":
                    pe.wait_ge(o_scaled, HEADS * VT)
                sums(acc, sq[:, 1, :])
                factors(stat0[b + 1] - 1)

            pe.wait_ge(const_in, 96)
            pe.wait_ge(x_in, 32)
            pe.wait_ge(consts_ready, 2)
            for k in range(DK):
                if k >= NPROJ:
                    pe.wait_ge(x_new, k - NPROJ + 1)
                for t in range(NT):
                    last = pe.transpose(proj[k % NPROJ][:, t * P:(t + 1) * P], x_rows[:, t, k * P:(k + 1) * P],
                                        ident)
                last.then_inc(xt_ready, 1)
            for b, (kind, layer, which) in enumerate(plan):
                n0, T0 = chunk0[b], tile0[b]
                first_chunk(b)
                if kind == "ffn":
                    pe.wait_ge(w_lo, n0 + 2)
                    tile(2, NEXT, 0)
                    pre_sums(b)
                    tile(3, NEXT, 1, lambda: factors(stat0[b])).then_inc(w_used, 1)
                    with pe.Fori(1, FF // WIDE) as it:
                        for slot in range(2):
                            pe.wait_ge(w_lo, n0 + 2 * it + slot + 1)
                            pe.wait_ge(tile_out, T0 + 4 * it + 2 * slot - 2)
                            tile(2 * slot, slot, 0)
                            tile(2 * slot + 1, slot, 1).then_inc(w_used, 1)
                    output(b, n0 + 2 * FF // WIDE, T0 + 2 * FK, DOWN_STEPS,
                           lambda step: (hhi[:, KT * step:KT * (step + 1), :], hlo[:, KT * step:KT * (step + 1), :],
                                         h_lo, ff0[b] + KT * (step + 1)))
                if kind == "gla":
                    pe.wait_ge(wz_split, 2)
                    for t in range(NT):
                        cols = slice(t * P, (t + 1) * P)
                        z = banks[7][:, t * RANK:(t + 1) * RANK]
                        for k in range(KT):
                            pe.matmul(z, xhi[:, k, cols], wz_hi[:, k, :], start=k == 0, stop=False)
                            pe.matmul(z, xhi[:, k, cols], wz_lo[:, k, :], start=False, stop=False)
                            mm = pe.matmul(z, xlo[:, k, cols], wz_hi[:, k, :], start=False, stop=k == KT - 1)
                    mm.then_inc(z_mm, 1)

                    def x_tile(i, j):
                        return tile(2 * (i % 2 if i < 2 * Q_CHUNKS else 0) + j, i % 2, j)

                    def v_chunk(h):
                        i = 2 * Q_CHUNKS + h
                        pe.wait_ge(w_lo, n0 + i + 1)
                        for t in range(NT):
                            T = T0 + V_TILE + NT * h + t
                            pe.wait_ge(tile_out, T - NPROJ + 1)
                            out = proj[(NT * h + t) % NPROJ][:, 0:DV]
                            for k in range(KT):
                                mm = multiply_rows(out, i % 2, k, t, k == 0, k == KT - 1)
                        mm.then_inc(w_used, 1)

                    pe.wait_ge(w_lo, n0 + 2)
                    tile(2, NEXT, 0)
                    pre_sums(b)
                    tile(3, NEXT, 1, lambda: factors(stat0[b])).then_inc(w_used, 1)
                    pe.wait_ge(z_evac, NT)
                    for t in range(NT):
                        mm = pe.matmul(banks[6][0:RANK, t * P:(t + 1) * P], z_rows[:, t, :], ident,
                                       start=True, stop=True)
                    mm.then_inc(z_mm, 1)
                    pe.wait_ge(w_lo, n0 + 3)
                    pe.wait_ge(tile_out, T0 + 2)
                    x_tile(2, 0)
                    pe.wait_ge(z_turned, 2)
                    pe.wait_ge(gla_in, 48)
                    for t in range(NT):
                        mm = pe.matmul(banks[5 + t][:, :], z_cols[0:RANK + 1, t * P:(t + 1) * P],
                                       w_gate2[:, :], start=True, stop=True)
                    mm.then_inc(z_mm, 1)
                    x_tile(2, 1).then_inc(w_used, 1)
                    pe.wait_ge(w_lo, n0 + 4)
                    pe.wait_ge(tile_out, T0 + 4)
                    x_tile(3, 0)
                    x_tile(3, 1).then_inc(w_used, 1)
                    v_chunk(0)
                    pe.wait_ge(g_done, NT)
                    for t in range(NT):
                        for h in range(HEADS):
                            mm = pe.matmul(banks[5 + t][:, h * P:(h + 1) * P], log_g_rows[:, t, h * P:(h + 1) * P],
                                           tri_tok[t], start=True, stop=True)
                    mm.then_inc(z_mm, 1)
                    for h in range(1, HEADS):
                        v_chunk(h)
                    pe.wait_ge(tile_out, T0 + R_TILE)
                    pe.wait_ge(b_copied, NT)
                    for h in range(HEADS):
                        s = stat0[b] + 1 + h
                        q_h, k_h, v_h = qk[:, h, 0, :], qk[:, h, 1, :], v_rows[:, :, h * DV:(h + 1) * DV]
                        pe.wait_ge(qk_ready, h + 1)
                        if h > 0:
                            pe.wait_ge(dec_done, dec_batch * h)
                        for t in range(NT):
                            cols = slice(t * P, (t + 1) * P)
                            mm = pe.matmul(banks[2][:, cols], k_h[:, cols], q_h[:, cols], start=True, stop=True)
                        mm.then_inc(scores_mm, 1)
                        pe.wait_ge(k_decayed, h + 1)
                        for t in range(NT):
                            mm = pe.transpose(banks[3][:, t * P:(t + 1) * P], k_dec[:, h, t * P:(t + 1) * P], ident)
                        mm.then_inc(k_turned, 1)
                        pe.wait_ge(w_lo, n0 + R_AT + h + 1)
                        pe.wait_ge(tile_out, T0 + R_TILE + VT * h)
                        x_tile(R_AT + h, 0)
                        if h > 0:
                            pe.wait_ge(o_acc, h)
                            if h > 1:
                                pe.wait_ge(o_scaled, VT * (h - 1))
                            sums(acc)
                        pe.wait_ge(k_out, h + 1)
                        pe.wait_ge(scores_out, 1 + NT * (h + 1))
                        for c in (0, 2, 1, 3):
                            rows, t = slice(c % 2 * GCH, (c % 2 + 1) * GCH), c // 2
                            mm = pe.matmul(banks[7 if c % 2 == 0 else 2][:, t * DV:(t + 1) * DV],
                                           k_rows[rows, t * P:(t + 1) * P], v_h[rows, t, :], start=True, stop=True)
                            if t == 1:
                                mm.then_inc(kv_mm, 1)
                        if h > 0:
                            pe.wait_ge(o_out, VT * h)
                        pe.wait_ge(s0_in[h % 2], 16 * (h // 2 + 1))
                        for i in range(VT):
                            o, vals = banks[5 + i], slice(i * P, (i + 1) * P)
                            for t in range(NT):
                                cols = slice(t * P, (t + 1) * P)
                                pe.matmul(o[:, cols], v_h[:, t, vals], scores[:, cols], start=t == 0, stop=False,
                                          skip_group_check=True)
                            for c in range(dec_batch):
                                cols = slice(seq + c * dec_seq, seq + (c + 1) * dec_seq)
                                mm = pe.matmul(o[:, cols], s0[:, h % 2, c, vals], q_h[:, cols], start=False,
                                               stop=False, skip_group_check=True)
                        mm.then_inc(inter_mm, 1)
                        x_tile(R_AT + h, 1).then_inc(w_used, 1)
                        if h > 0:
                            factors(s - 1)
                        for c in range(1, seq // GCH):
                            cols = slice(c * GCH, (c + 1) * GCH)
                            pe.wait_ge(s_done, seq // GCH * h + c)
                            for i in range(VT):
                                mm = pe.matmul(banks[5 + i][:, cols], s_prompt[:, c - 1, i * P:(i + 1) * P],
                                               q_h[:, cols], start=False, stop=c == seq // GCH - 1,
                                               skip_group_check=True)
                        mm.then_inc(o_mm, 1)
                        pe.wait_ge(vp_done, 2 * (h + 1))
                        pe.wait_ge(s_done, seq // GCH * (h + 1))
                        for j in range(dec_batch // 2):
                            rows = slice(j * 2 * dec_seq, (j + 1) * 2 * dec_seq)
                            if j == dec_batch // 2 - 1:
                                pe.wait_ge(dec_done, dec_batch * h + 2)
                            pe.matmul(banks[DEC_BANKS[j]][:, :], k_rows[rows, NP * P:TOK],
                                      v_pair[rows, :, :].rearrange("p i v -> p (i v)"), start=True, stop=True)\
                              .then_inc(dec_mm, 1)
                    s = stat0[b] + HEADS
                    pe.wait_ge(o_acc, HEADS)
                    pe.wait_ge(o_scaled, VT * (HEADS - 1))
                    sums(acc)
                    pe.wait_ge(w_lo, n0 + OUT_AT + 1)
                    factors(stat0[b] + HEADS)
                    output(b, n0 + OUT_AT, T0 + R_TILE + HEADS * VT, 1, lambda step: (ohi, olo, o_lo, 0), True)
                if kind == "sgu":
                    def v_tile(i, parity4, t):
                        second = isinstance(i, int) and i == 1
                        if not (second and t > 0):
                            pe.wait_ge(tile_out, NT * i + (T0 + t - NPROJ + 1))
                        out = banks[4 + t] if second and t > 0 else proj[(NT * parity4 + t) % NPROJ]
                        for k in range(KT):
                            mm = multiply_rows(out[:, 0:WIDE], NEXT if second else parity4 % 2, k, t,
                                               k == 0, k == KT - 1)
                        return mm

                    for i in range(1, 4):
                        pe.wait_ge(w_lo, n0 + i + 1)
                        for t in range(NT):
                            mm = v_tile(i, i, t)
                            if i == 1 and t == 0:
                                pre_sums(b)
                        mm.then_inc(w_used, 1)
                        if i == 1:
                            factors(stat0[b])
                        if i == 2:
                            pe.wait_ge(tile_out, T0 + 2 * NT)
                            pe.wait_ge(ws_in, 16 * (dec_batch + 2))
                            for which_w in range(2):
                                for g in range(SPATIAL):
                                    mm = pe.transpose(banks[5 + which_w][:, g * P:(g + 1) * P],
                                                      w_rows[:, which_w, g, :], ident)
                            mm.then_inc(ws_mm, 1)
                    with pe.Fori(1, V_CHUNKS // 4) as it:
                        for c in range(4):
                            pe.wait_ge(w_lo, n0 + 4 * it + c + 1)
                            for t in range(NT):
                                mm = v_tile(4 * it + c, c, t)
                            mm.then_inc(w_used, 1)
                    pe.wait_ge(ws_done, 2)
                    for i in range(V_CHUNKS):
                        pe.wait_ge(w_lo, n0 + V_CHUNKS + i + 1)
                        pe.wait_ge(tile_out, T0 + U_TILE + 2 * i - 2)
                        tile(2 * (i % 2), i % 2, 0)
                        if i == 0:
                            tile(1, 0, 1).then_inc(w_used, 1)
                        pe.wait_ge(ln_done, i + 1)
                        if i > 0:
                            pe.wait_ge(mix_out, 4 * i)
                        for j in range(2):
                            c = 2 * i + j
                            g = c * SPATIAL // (HALF // P)
                            for t in range(NT):
                                mm = pe.matmul(banks[5 + j][:, t * P:(t + 1) * P],
                                               v_at(i, t)[:, j * P:(j + 1) * P], w_turned[:, t // NP, g, :],
                                               start=True, stop=True)
                        mm.then_inc(mix_mm, 1)
                        if i > 0:
                            tile(2 * (i % 2) + 1, i % 2, 1).then_inc(w_used, 1)
                    output(b, n0 + 2 * V_CHUNKS, T0 + SGU_OUT_TILE, SGU_STEPS,
                           lambda step: (uhi[step], ulo[step], u_lo, KT * (step + 1)))
            for g in range(2 * NT):
                half, t = divmod(g, NT)
                pe.wait_ge(x_new, DK * len(plan) + (half + 1) * DK // 2)
                if g >= NPROJ:
                    pe.wait_ge(yt_out, g - NPROJ + 1)
                for k in range(DK // 2):
                    last = pe.transpose(proj[g % NPROJ][:, k * P:(k + 1) * P],
                                        x[:, half * DK // 2 + k, t * P:(t + 1) * P], ident)
                last.then_inc(yt_ready, 1)


def constants():
    import numpy as np

    s, t = np.arange(P)[:, None], np.arange(P)[None, :]
    upto = s <= t
    tri = np.stack([s == t, upto, upto & (s // 64 == t // 64), upto & (s // 16 == t // 16)], axis=1)
    odd = np.arange(P) // 16 % 2
    return {"ident_tri": tri.astype(np.float32), "pair_mask": np.stack([1 - odd, odd], axis=1).astype(np.float32)}


def laid_out(inputs):
    import numpy as np

    def columns(g):
        return np.ascontiguousarray(g.reshape(-1, P).T)

    return {"gain_pre": columns(inputs["norm_pre"]), "gain_post": columns(inputs["norm_post"]),
            "gain_head": columns(inputs["gla_norm"]), "u_bias": columns(inputs["sgu_b_in"])}


PLAN = [("ffn", 0, 0), ("gla", 0, 1), ("ffn", 0, 2), ("ffn", 1, 0), ("sgu", 1, 1), ("ffn", 1, 2)]


def kernel(**inputs):
    import numpy as np
    import concourse.bacc as bacc
    from concourse.bass_utils import run_bass_kernel_spmd

    nc = bacc.Bacc("TRN2", target_bir_lowering=False, num_devices=1)
    arrays = {name: np.ascontiguousarray(value) for name, value in inputs.items()}
    arrays.update(constants(), **laid_out(arrays))
    a = {name: nc.dram_tensor(name, value.shape, mybir.dt.from_np(value.dtype), kind="ExternalInput").ap()
         for name, value in arrays.items()}
    n_gla, dec_batch, heads, dk, dv = inputs["state_gla"].shape
    n_sgu, half = inputs["sgu_ln_g"].shape
    shapes = {"y_prompt": inputs["x_prompt"].shape, "y_sample": inputs["x_sample"].shape,
              "gla_state_prompt": (n_gla, inputs["x_prompt"].shape[0], heads, dk, dv),
              "gla_state_sample": inputs["state_gla"].shape,
              "sgu_v_sample": (n_sgu,) + inputs["x_sample"].shape[:2] + (half,)}
    outs = {name: nc.dram_tensor(name, shape, F32, kind="ExternalOutput").ap() for name, shape in shapes.items()}
    build_trunk(nc, a, outs, PLAN)
    result = run_bass_kernel_spmd(nc, [arrays], core_ids=[0])
    return tuple(result.results[0][name] for name in shapes)
```

```python
from contextlib import ExitStack

import concourse.bass as bass
from concourse import mybir

F32 = mybir.dt.float32
F32R = mybir.dt.float32r
U32 = mybir.dt.uint32
ALU = mybir.AluOpType
ACT = mybir.ActivationFunctionType

P = 128
WIDE = 256
KT = 8
BANK = 512
RMS_EPS = 1e-6


def build_trunk(nc, a, outs, plan):
    seq, D = a["x_prompt"].shape[1:]
    dec_batch, dec_seq = a["x_sample"].shape[:2]
    NP = seq // P
    NT = NP + 1
    TOK = NT * P
    DK = D // P
    FF = a["ffn_w_gate"].shape[-1]
    FK = FF // P
    assert dec_batch * dec_seq == P and dec_batch == DK == KT and TOK <= BANK

    FFN_CHUNKS = 2 * FF // WIDE + FF // (P * KT) * (D // WIDE)
    DOWN_STEPS = FK // KT
    QUARTERS = D // WIDE

    HEADS, DH, DV = a["state_gla"].shape[2:]
    VT = DV // P
    RANK = a["gla_w_gate2"].shape[1]
    GLA_TAU = 16.0
    GCH = 64
    assert DH == P and DV == WIDE and HEADS * DV == D and dec_seq <= GCH
    Q_CHUNKS = HEADS * DH // WIDE
    V_TILE = 4 * Q_CHUNKS
    R_TILE = V_TILE + HEADS * NT
    R_AT = 2 * Q_CHUNKS + HEADS
    OUT_AT = R_AT + HEADS
    DEC_BANKS = (3, 7, 2, 3)
    GLA_CHUNKS = OUT_AT + QUARTERS

    HALF = a["sgu_ln_g"].shape[1]
    SPATIAL = a["sgu_w_s"].shape[1]
    LN_EPS = 1e-5
    V_CHUNKS = HALF // WIDE
    SGU_STEPS = HALF // (P * KT)
    SGU_CHUNKS = 2 * V_CHUNKS + SGU_STEPS * QUARTERS
    U_TILE = NT * V_CHUNKS
    SGU_OUT_TILE = U_TILE + HALF // P
    PER_SET = KT * P // WIDE
    assert a["sgu_w_s"].shape[2] == P

    chunk0, tile0, stat0, ff0 = [0], [0], [0], [0]
    for kind, layer, which in plan:
        chunks, tiles, stats, ff = {
            "ffn": (FFN_CHUNKS, 2 * FK + DK, 2, FK),
            "sgu": (SGU_CHUNKS, SGU_OUT_TILE + DK, 2, 0),
            "gla": (GLA_CHUNKS, 2 * HEADS * 2 + NT * HEADS + DK, 2 + HEADS, 0),
        }[kind]
        for start, size in ((chunk0, chunks), (tile0, tiles), (stat0, stats), (ff0, ff)):
            start.append(start[-1] + size)
    CHUNKS = chunk0[-1]
    assert plan[0][0] == plan[-1][0] == "ffn"

    xp = a["x_prompt"].rearrange("b (t p) d -> p (b t) d", p=P)
    xs = a["x_sample"].rearrange("b l d -> (b l) d")
    yp = outs["y_prompt"].rearrange("b (t p) d -> p (b t) d", p=P)
    ys = outs["y_sample"].rearrange("b l d -> (b l) d")

    with ExitStack() as ctx:
        def sb(name, shape, dt=F32):
            return ctx.enter_context(nc.sbuf_tensor(name + "_sb", shape, dt))

        def shared(*wanted):
            with ExitStack() as scope:
                return [scope.enter_context(nc.sbuf_tensor(name + "_sb", shape, dt))
                        for name, shape, dt in wanted]

        def sem(name):
            return ctx.enter_context(nc.semaphore(name))

        ident_tri = sb("ident_tri", [P, 4, P])
        ident, tri_gla, tri_dec = ident_tri[:, 0, :], ident_tri[:, 2, :], ident_tri[:, 3, :]
        tri_tok = [tri_gla] * NP + [tri_dec]
        pair_mask = sb("pair_mask", [P, 2])
        ones = sb("ones", [P, P])
        g_pre = sb("g_pre", [P, 2 * 3 * DK])
        g_post = sb("g_post", [P, 2 * 3 * DK])
        g_head = sb("g_head", [P, VT])
        u_bias = sb("u_bias", [P, 2 * HALF // P])
        x = sb("x", [P, DK, TOK])
        xhi = sb("xhi", [P, DK, TOK], F32R)
        xlo = sb("xlo", [P, DK, TOK], F32R)
        yg = sb("yg", [P, DK, TOK])
        raw = sb("raw", [P, 2, KT, WIDE])
        whi = sb("whi", [P, 2, KT, WIDE], F32R)
        wlo = sb("wlo", [P, 2, KT, WIDE], F32R)
        sq = sb("sq", [P, 2, TOK])
        acc = sb("acc", [P, TOK])
        r_pre = sb("r_pre", [P, TOK])
        minus_half = sb("minus_half", [P, 1])
        mean_sq = sb("mean_sq", [P, NT])
        rstd = sb("rstd", [P, 2, NT])

        hhi, hlo, h_gate, h_up = shared(
            ("hhi", [P, FK, TOK], F32R), ("hlo", [P, FK, TOK], F32R),
            ("h_gate", [P, 2, TOK], F32), ("h_up", [P, 2, TOK], F32))
        (v_rows, qk, k_dec, s0, v_pair, log_g, e_neg, e_pos, olo, k_rows, scores, s_prompt, ot, z_cols,
         wz, w_gate2, wz_hi, wz_lo) = shared(
            ("v_rows", [P, NT, D], F32), ("qk", [P, HEADS, 2, TOK], F32), ("k_dec", [P, HEADS, TOK], F32),
            ("s0", [P, 2, dec_batch, DV], F32), ("v_pair", [P, 2, DV], F32),
            ("log_g", [P, HEADS * TOK], F32), ("e_neg", [P, HEADS, TOK], F32), ("e_pos", [P, HEADS, TOK], F32),
            ("olo", [P, HEADS * VT, TOK], F32R), ("k_rows", [P, TOK], F32),
            ("scores", [P, TOK], F32), ("s_prompt", [P, seq // GCH, DV], F32),
            ("ot", [P, VT, TOK], F32), ("z_cols", [32, TOK], F32),
            ("wz", [P, KT, RANK], F32), ("w_gate2", [RANK + 1, HEADS * DH], F32),
            ("wz_hi", [P, KT, RANK], F32R), ("wz_lo", [P, KT, RANK], F32R))
        log_g_rows = log_g[:, :].rearrange("p (t f) -> p t f", t=NT)
        b_cum = log_g[:, :].rearrange("p (h t) -> p h t", h=HEADS)
        _, ohi, _, r_silu = shared(
            ("under_v_rows", [P, NT, D], F32), ("ohi", [P, HEADS * VT, TOK], F32R),
            ("under_k_dec_s0_v_pair", [P, HEADS * TOK + 2 * (dec_batch + 1) * DV], F32),
            ("r_silu", [P, HEADS * VT, TOK], F32))
        set_rows = [P, NT, KT * P]
        (uhi0, v0, v1, v2, ulo0, uhi1, uhi2, feat_rows, w_turned, b_spatial, u_tile, mixed, ln_stats, ln_mean_var,
         ln_var, ln_rstd) = shared(
            ("uhi0", [P, KT, TOK], F32R), ("v0", set_rows, F32), ("v1", set_rows, F32), ("v2", set_rows, F32),
            ("ulo0", [P, KT, TOK], F32R), ("uhi1", [P, KT, TOK], F32R), ("uhi2", [P, KT, TOK], F32R),
            ("feat_rows", [P, 2, 2, WIDE], F32),
            ("w_turned", [P, 2, SPATIAL, P], F32), ("b_spatial", [P, SPATIAL, P], F32), ("u_tile", [P, 2, TOK], F32),
            ("mixed", [P, 2, TOK], F32), ("ln_stats", [P, NT, V_CHUNKS, 6], F32), ("ln_mean_var", [P, NT, 2], F32),
            ("ln_var", [P, NT], F32), ("ln_rstd", [P, NT], F32))
        _, ulo1, ulo2, w_rows = shared(("under_uhi0", [P, KT, TOK], F32), ("ulo1", [P, KT, TOK], F32R),
                                       ("ulo2", [P, KT, TOK], F32R), ("w_rows", [P, 2, SPATIAL, P], F32))
        v_set, uhi, ulo = [v0, v1, v2], [uhi0, uhi1, uhi2], [ulo0, ulo1, ulo2]
        assert SGU_STEPS == len(v_set)
        next_hi, _, next_lo = shared(
            ("next_hi", [P, KT, WIDE], F32R), ("next_between", [P, FK * TOK - KT * WIDE], F32),
            ("next_lo", [P, KT, WIDE], F32R))
        weights = [(whi[:, 0], wlo[:, 0]), (whi[:, 1], wlo[:, 1]), (next_hi, next_lo)]
        NEXT = 2
        y_rows, = shared(("y_rows", [P, NT, D], F32))
        x_rows = yg[:, :, :].rearrange("p k t -> p (k t)").rearrange("p (n d) -> p n d", n=NT)

        banks = [ctx.enter_context(nc.psum_tensor(f"bank{i}", [P, BANK], F32)) for i in range(8)]
        proj = banks[:4]
        NPROJ = len(proj)
        row_banks = banks[5:]
        free_banks = banks[2:]
        stat = banks[4]

        const_in = sem("const_in")
        small_in = sem("small_in")
        x_in = [sem(f"x_in{i}") for i in range(2)]
        landed = [sem(f"landed{i}") for i in range(2)]
        w_hi = sem("w_hi")
        w_lo = sem("w_lo")
        w_used = sem("w_used")
        y_first = sem("y_first")
        tile_out = sem("tile_out")
        consts_ready = sem("consts_ready")
        xt_ready = sem("xt_ready")
        x_new = sem("x_new")
        x_hi = sem("x_hi")
        x_lo = sem("x_lo")
        x_sq = sem("x_sq")
        x_acc = sem("x_acc")
        x_acc_pool = sem("x_acc_pool")
        y_sq = sem("y_sq")
        y_acc = sem("y_acc")
        y_scaled = sem("y_scaled")
        y_scaled_pool = sem("y_scaled_pool")
        sums_ready = sem("sums_ready")
        mean_ready = sem("mean_ready")
        rstd_ready = sem("rstd_ready")
        factor_ready = sem("factor_ready")
        pre_read = sem("pre_read")
        post_read = sem("post_read")
        silu_ready = sem("silu_ready")
        prod_ready = sem("prod_ready")
        h_hi = sem("h_hi")
        h_lo = sem("h_lo")
        gla_in = sem("gla_in")
        s0_in = [sem(f"s0_in{i}") for i in range(2)]
        s0_stored = [sem(f"s0_stored{i}") for i in range(2)]
        sp_stored = sem("sp_stored")
        wz_split = sem("wz_split")
        z_mm = sem("z_mm")
        z_out = sem("z_out")
        g_abs = sem("g_abs")
        g_exp = sem("g_exp")
        g_log = sem("g_log")
        g_done = sem("g_done")
        b_copied = sem("b_copied")
        b_exp = sem("b_exp")
        b_diff = sem("b_diff")
        d_exp = sem("d_exp")
        k_decayed = sem("k_decayed")
        qk_ready = sem("qk_ready")
        scores_mm = sem("scores_mm")
        k_turned = sem("k_turned")
        scores_out = sem("scores_out")
        k_out = sem("k_out")
        kv_mm = sem("kv_mm")
        s_done = sem("s_done")
        o_mm = sem("o_mm")
        dec_mm = sem("dec_mm")
        dec_done = sem("dec_done")
        vp_done = sem("vp_done")
        o_sq = sem("o_sq")
        o_out = sem("o_out")
        o_acc = sem("o_acc")
        o_scaled = sem("o_scaled")
        o_gated = sem("o_gated")
        o_hi = sem("o_hi")
        o_lo = sem("o_lo")
        r_silu_done = sem("r_silu_done")
        ws_zero = sem("ws_zero")
        ws_in = sem("ws_in")
        ws_mm = sem("ws_mm")
        ws_done = sem("ws_done")
        rows_in = [sem(f"rows_in{i}") for i in range(2)]
        v_act = sem("v_act")
        v_stat = sem("v_stat")
        ln_aggr = sem("ln_aggr")
        ln_eps = sem("ln_eps")
        ln_pow = sem("ln_pow")
        ln_norm = sem("ln_norm")
        ln_gain = sem("ln_gain")
        ln_done = sem("ln_done")
        v_stored = sem("v_stored")
        mix_mm = sem("mix_mm")
        mix_out = sem("mix_out")
        u_act = sem("u_act")
        u_prod = sem("u_prod")
        u_hi = sem("u_hi")
        u_lo = sem("u_lo")
        turned = sem("turned")
        x_rows_out = sem("x_rows_out")
        y_ready = sem("y_ready")
        stored = sem("stored")

        block = ctx.enter_context(nc.Block())

        def v_at(i, t):
            at = i % PER_SET * WIDE
            return v_set[i // PER_SET][:, t, at:at + WIDE]

        def gain(g, b, k):
            kind, layer, which = plan[b]
            return g[:, bass.ds((layer * 3 + which) * DK + k, 1)]

        @block.sync
        def _(sp):
            def by_k(w):
                return w.rearrange("(k p) c -> p k c", p=P)

            sp.dma_start(raw[:, 0], by_k(a["ffn_w_gate"][0, 0])[:, :, 0:WIDE]).then_inc(landed[0], 16)
            sp.dma_start(ident_tri[:, :, :], a["ident_tri"]).then_inc(const_in, 16)
            for i, half in enumerate((slice(0, D // 2), slice(D // 2, D))):
                sp.dma_start(x_rows[:, 0:NP, half], xp[:, :, half]).then_inc(x_in[i], 16)
                sp.dma_start(x_rows[:, NP, half], xs[:, half]).then_inc(x_in[i], 16)
                if i == 0:
                    sp.dma_start(g_pre[:, :], a["gain_pre"]).then_inc(const_in, 16)

            def load(n, src, slot, first=False):
                if not first:
                    sp.wait_ge(w_lo, n - 1)
                sp.dma_start(raw[:, slot], src).then_inc(landed[slot], 16)

            for b, (kind, layer, which) in enumerate(plan):
                n0 = chunk0[b]
                if kind == "ffn":
                    i = which // 2
                    gate, up = by_k(a["ffn_w_gate"][layer, i]), by_k(a["ffn_w_up"][layer, i])
                    down = by_k(a["ffn_w_down"][layer, i])
                    if b > 0:
                        load(n0, gate[:, :, 0:WIDE], 0)
                    load(n0 + 1, up[:, :, 0:WIDE], 1, b == 0)
                    if b == 0:
                        sp.dma_start(g_post[:, :], a["gain_post"]).then_inc(small_in, 16)
                        sp.dma_start(g_head[:, :], a["gain_head"]).then_inc(small_in, 16)
                        sp.dma_start(u_bias[:, :], a["u_bias"]).then_inc(small_in, 16)
                        sp.dma_start(pair_mask[:, :], a["pair_mask"]).then_inc(small_in, 16)
                    with sp.Fori(1, FF // WIDE) as it:
                        load(n0 + 2 * it, gate[:, :, bass.ds(it * WIDE, WIDE)], 0)
                        load(n0 + 2 * it + 1, up[:, :, bass.ds(it * WIDE, WIDE)], 1)
                    with sp.Fori(0, QUARTERS) as q:
                        for step in range(DOWN_STEPS):
                            load(n0 + 2 * FF // WIDE + DOWN_STEPS * q + step,
                                 down[:, KT * step:KT * step + KT, bass.ds(q * WIDE, WIDE)], step % 2)
                if kind == "gla":
                    w_in, w_out = by_k(a["gla_w_in"][layer // 2]), by_k(a["gla_w_out"][layer // 2])
                    with sp.Fori(0, OUT_AT // 2) as it:
                        for slot in range(2):
                            load(n0 + 2 * it + slot, w_in[:, :, bass.ds((2 * it + slot) * WIDE, WIDE)], slot)
                    with sp.Fori(0, QUARTERS // 2) as it:
                        for slot in range(2):
                            load(n0 + OUT_AT + 2 * it + slot, w_out[:, :, bass.ds((2 * it + slot) * WIDE, WIDE)], slot)
                if kind == "sgu":
                    w_in, w_out = by_k(a["sgu_w_in"][layer // 2]), by_k(a["sgu_w_out"][layer // 2])

                    def load_pairs(at, start, first):
                        with sp.Fori(first, V_CHUNKS // 2) as it:
                            for slot in range(2):
                                load(n0 + at + 2 * it + slot,
                                     w_in[:, :, bass.ds((2 * it + slot) * WIDE + start, WIDE)], slot)

                    for i in range(4):
                        load(n0 + i, w_in[:, :, HALF + i * WIDE:HALF + (i + 1) * WIDE], i % 2)
                    w_s, b_s = a["sgu_w_s"][layer // 2], a["sgu_b_s"][layer // 2:layer // 2 + 1]
                    sp.wait_ge(ws_zero, 1)
                    sp.dma_start(w_rows[:, 0], w_s.rearrange("g t s -> t g s")).then_inc(ws_in, 16)
                    sp.dma_start(b_spatial[:, :, :].rearrange("p g t -> p (g t)"), b_s.rearrange(
                        "a g t -> a (g t)").to_broadcast([P, SPATIAL * P])).then_inc(ws_in, 16)
                    for c in range(dec_batch):
                        at = slice(c * dec_seq, (c + 1) * dec_seq)
                        sp.dma_start(w_rows[at, 1, :, at], w_s[:, 0:dec_seq, 0:dec_seq].rearrange(
                            "g t s -> t g s")).then_inc(ws_in, 16)
                    load_pairs(0, HALF, 2)
                    load_pairs(V_CHUNKS, 0, 0)
                    with sp.Fori(0, QUARTERS // 2) as it:
                        for c in range(2 * SGU_STEPS):
                            q, step = 2 * it + c // SGU_STEPS, c % SGU_STEPS
                            load(n0 + 2 * V_CHUNKS + 2 * SGU_STEPS * it + c,
                                 w_out[:, KT * step:KT * step + KT, bass.ds(q * WIDE, WIDE)], c % 2)
            for half in range(2):
                for t in range(NT):
                    g = half * NT + t
                    sp.wait_ge(y_ready, g + 1)
                    dst = (yp[:, t, :] if t < NP else ys)[:, half * BANK:(half + 1) * BANK]
                    sp.dma_start(dst, y_rows[:, t, half * BANK:(half + 1) * BANK]).then_inc(stored, 16)
            sp.wait_ge(stored, 16 * 2 * NT)

        @block.scalar
        def _(act):
            def round_chunk(n, slot, first=False):
                act.wait_ge(landed[slot], 8 * (n - slot) + 16)
                if not first:
                    act.wait_ge(w_used, n - 1)
                act.activation(whi[:, slot], raw[:, slot], ACT.Copy).then_inc(w_hi, 1)

            def round_next(n):
                act.wait_ge(landed[1], 8 * (n - 1) + 16)
                act.activation(next_hi[:, :, :], raw[:, 1], ACT.Copy).then_inc(w_hi, 1)

            def hi_x(b, k):
                act.wait_ge(x_new, DK * b + k + 1)
                act.activation(xhi[:, k, :], x[:, k, :], ACT.Copy, scale=gain(g_pre, b, k)).then_inc(x_hi, 1)

            def square_x(k):
                act.activation(yg[:, k, :], x[:, k, :], ACT.Square).then_inc(x_sq, 1)

            def pre_factor(b):
                act.wait_ge(factor_ready, stat0[b] + 1)
                act.activation(r_pre[:, :], stat[:, 0:TOK], ACT.Copy).then_inc(pre_read, 1)

            def output(b, n1, steps, started=False):
                def group(q, parity):
                    for step in range(steps):
                        n = n1 + q * steps + step
                        if n + 1 >= CHUNKS or started and n == n1:
                            continue
                        round_chunk(n + 1, (steps * parity + step + 1) % 2)
                        if n + 1 == chunk0[b + 1]:
                            round_next(n + 2)
                        if (b, q) == (len(plan) - 1, QUARTERS - 1) and step > 0:
                            half = step - 1
                            act.wait_ge(turned, step)
                            for t in range(NT):
                                act.activation(y_rows[:, t, half * BANK:(half + 1) * BANK], row_banks[t][:, :],
                                               ACT.Copy).then_inc(x_rows_out, 1)
                    for j in range(2):
                        m = 2 * q + j
                        if j == 0:
                            act.wait_ge(y_first, QUARTERS * b + q + 1)
                        else:
                            act.wait_ge(w_used, n1 + (q + 1) * steps)
                        act.wait_ge(y_acc, DK * b + max(m, 1))
                        psum = proj[2 * parity + j][:, 0:TOK]
                        act.activation(sq[:, j, :], psum, ACT.Square).then_inc(y_sq, 1)
                        act.activation(yg[:, bass.ds(m, 1), :], psum, ACT.Copy,
                                       scale=gain(g_post, b, m)).then_inc(tile_out, 1)
                for q in range(QUARTERS):
                    group(q, q % 2)
                if b + 1 < len(plan):
                    act.wait_ge(factor_ready, stat0[b + 1])
                    act.wait_ge(y_scaled, 2 * b + 1)
                    act.activation(acc[:, :], stat[:, 0:TOK], ACT.Copy).then_inc(post_read, 1)

            round_chunk(0, 0, True)
            act.wait_ge(const_in, 32)
            for k in range(DK):
                hi_x(0, k)
                if k == 5:
                    round_next(1)
            act.wait_ge(small_in, 64)
            act.wait_ge(xt_ready, DK)
            for k in range(DK):
                square_x(k)
            for b, (kind, layer, which) in enumerate(plan):
                n0 = chunk0[b]
                if b > 0:
                    for k in range(DK):
                        hi_x(b, k)
                        square_x(k)
                if kind == "ffn":
                    f0 = ff0[b]

                    def silu(it):
                        for j in range(2):
                            act.wait_ge(tile_out, tile0[b] + 4 * it + j + 1)
                            act.activation(h_gate[:, j, :], h_gate[:, j, :], ACT.Silu).then_inc(silu_ready, 1)

                    def round_h(it):
                        for j in range(2):
                            act.wait_ge(prod_ready, f0 + 2 * it + j + 1)
                            act.activation(hhi[:, bass.ds(2 * it + j, 1), :], h_up[:, j:j + 1, :], ACT.Copy)\
                               .then_inc(h_hi, 1)

                    round_chunk(n0 + 2, 0)
                    pre_factor(b)
                    silu(0)
                    with act.Fori(1, FF // WIDE) as it:
                        round_chunk(n0 + 2 * it + 1, 1)
                        round_h(it - 1)
                        round_chunk(n0 + 2 * it + 2, 0)
                        silu(it)
                    round_h(FF // WIDE - 1)
                    output(b, n0 + 2 * FF // WIDE, DOWN_STEPS)
                if kind == "gla":
                    def tile_cols(buf, t):
                        return buf[:, :, t * P:(t + 1) * P]

                    act.wait_ge(gla_in, 48)
                    act.activation(wz_hi[:, :, :], wz[:, :, :], ACT.Copy).then_inc(wz_split, 1)
                    round_chunk(n0 + 2, 0)
                    pre_factor(b)
                    round_chunk(n0 + 3, 1)
                    act.wait_ge(z_mm, 2)
                    for t in range(NT):
                        act.activation(log_g_rows[:, t, :], banks[5 + t][:, :], ACT.Abs).then_inc(g_abs, 1)
                    round_chunk(n0 + 4, 0)
                    for t in range(NT):
                        act.wait_ge(g_abs, t + 1)
                        act.activation(log_g_rows[:, t, :], log_g_rows[:, t, :], ACT.Exp, scale=-1.0)\
                           .then_inc(g_exp, 1)
                    for t in range(NT):
                        act.wait_ge(g_exp, t + 1)
                        act.activation(log_g_rows[:, t, :], log_g_rows[:, t, :], ACT.Ln, bias=ones[:, 0:1])\
                           .then_inc(g_log, 1)
                    round_chunk(n0 + 5, 1)
                    round_chunk(n0 + 6, 0)
                    for t in range(NT):
                        act.wait_ge(b_copied, t + 1)
                        act.activation(tile_cols(e_pos, t), tile_cols(b_cum, t), ACT.Exp, scale=1 / GLA_TAU)\
                           .then_inc(b_exp, 1)
                        act.activation(tile_cols(e_neg, t), tile_cols(b_cum, t), ACT.Exp, scale=-1 / GLA_TAU)\
                           .then_inc(b_exp, 1)
                    act.wait_ge(b_diff, 2)
                    act.activation(k_dec[:, :, :], k_dec[:, :, :], ACT.Exp, scale=1 / GLA_TAU).then_inc(d_exp, 1)
                    round_chunk(n0 + 7, 1)
                    round_chunk(n0 + 8, 0)

                    def round_o(h):
                        for i in range(VT):
                            act.wait_ge(o_gated, VT * h + i + 1)
                            act.activation(ohi[:, VT * h + i, :], ot[:, i, :], ACT.Copy).then_inc(o_hi, 1)

                    for h in range(HEADS):
                        act.wait_ge(k_turned, h + 1)
                        act.activation(k_rows[:, :], banks[3][:, 0:TOK], ACT.Copy).then_inc(k_out, 1)
                        round_chunk(n0 + R_AT + h + 1, (h + 1) % 2)
                        if h > 0:
                            round_o(h - 1)
                        act.wait_ge(o_mm, h + 1)
                        if h > 0:
                            act.wait_ge(o_acc, h)
                            act.wait_ge(o_lo, VT * h)
                        for i in range(VT):
                            act.activation(sq[:, i, :], banks[5 + i][:, 0:TOK], ACT.Square).then_inc(o_sq, 1)
                        for i in range(VT):
                            act.activation(ot[:, i, :], banks[5 + i][:, 0:TOK], ACT.Copy,
                                           scale=g_head[:, i:i + 1]).then_inc(o_out, 1)
                        for i in range(VT):
                            act.wait_ge(tile_out, tile0[b] + R_TILE + VT * h + i + 1)
                            act.activation(r_silu[:, VT * h + i, :], r_silu[:, VT * h + i, :], ACT.Silu)\
                               .then_inc(r_silu_done, 1)
                    round_chunk(n0 + OUT_AT + 1, 1)
                    round_o(HEADS - 1)
                    output(b, n0 + OUT_AT, 1, started=True)
                if kind == "sgu":
                    def v_gelu(i):
                        for t in range(NT):
                            act.wait_ge(tile_out, tile0[b] + NT * i + t + 1)
                            act.activation(v_at(i, t), v_at(i, t), ACT.Gelu).then_inc(v_act, 1)

                    def round_u(i):
                        for j in range(2):
                            c = 2 * i + j
                            act.wait_ge(u_prod, c + 1)
                            act.activation(uhi[c // KT][:, c % KT, :], u_tile[:, j, :], ACT.Copy).then_inc(u_hi, 1)

                    round_chunk(n0 + 2, 0)
                    v_gelu(0)
                    pre_factor(b)
                    for i in range(1, V_CHUNKS):
                        if i > 1:
                            round_chunk(n0 + i + 1, (i + 1) % 2)
                        v_gelu(i)
                    for i in range(V_CHUNKS):
                        round_chunk(n0 + V_CHUNKS + i + 1, (i + 1) % 2)
                        if i > 0:
                            round_u(i - 1)
                        for j in range(2):
                            c = 2 * i + j
                            act.wait_ge(tile_out, tile0[b] + U_TILE + c + 1)
                            act.activation(u_tile[:, j, :], u_tile[:, j, :], ACT.Gelu, bias=u_bias[:, c:c + 1])\
                               .then_inc(u_act, 1)
                    round_u(V_CHUNKS - 1)
                    output(b, n0 + 2 * V_CHUNKS, SGU_STEPS)

        @block.vector
        def _(dve):
            def split_chunk(n, slot):
                dve.wait_ge(w_hi, n + 1)
                dve.tensor_tensor(wlo[:, slot], raw[:, slot], whi[:, slot].bitcast(F32), ALU.subtract)\
                   .then_inc(w_lo, 1)

            def lo_x(b, k):
                dve.wait_ge(x_hi, DK * b + k + 1)
                dve.scalar_tensor_tensor(xlo[:, k, :], x[:, k, :], gain(g_pre, b, k), xhi[:, k, :].bitcast(F32),
                                         ALU.mult, ALU.subtract).then_inc(x_lo, 1)

            def split_next(n):
                dve.wait_ge(w_hi, n + 1)
                dve.tensor_tensor(next_lo[:, :, :], raw[:, 1], next_hi[:, :, :].bitcast(F32), ALU.subtract)\
                   .then_inc(w_lo, 1)

            def mean(s, features, scale=1.0):
                dve.wait_ge(sums_ready, s + 1)
                dve.tensor_scalar(mean_sq[:, :], stat[:, TOK:TOK + NT], 1 / (features * scale ** 2),
                                  RMS_EPS / scale ** 2, ALU.mult, ALU.add).then_inc(mean_ready, 1)

            def pre_acc(b):
                dve.wait_ge(x_sq, DK * (b + 1))
                dve.tensor_tensor(yg[:, 4:6, :], yg[:, 4:6, :], yg[:, 6:8, :], ALU.add).then_inc(x_acc, 1)
                dve.wait_ge(x_acc_pool, 2 * (b + 1))
                dve.wait_ge(x_acc, 3 * b + 1)
                dve.tensor_tensor(yg[:, 4:6, :], yg[:, 4:6, :], yg[:, 0:3:2, :], ALU.add).then_inc(x_acc, 1)
                dve.wait_ge(x_acc, 3 * b + 2)
                dve.tensor_tensor(yg[:, 4, :], yg[:, 4, :], yg[:, 5, :], ALU.add).then_inc(x_acc, 1)

            def output(b, n1, steps, started=False):
                if b > 0:
                    dve.wait_ge(y_scaled_pool, (DK - 2) * b)
                dve.memset(acc[:, :], 0.0).then_inc(y_acc, 1)
                for q in range(QUARTERS):
                    for step in range(steps):
                        n = n1 + q * steps + step
                        if n + 1 >= CHUNKS or started and n == n1:
                            continue
                        split_chunk(n + 1, (n + 1) % 2)
                        if n + 1 == chunk0[b + 1]:
                            split_next(n + 2)
                    for j in range(2):
                        m = 2 * q + j
                        if m == DK - 1:
                            continue
                        dve.wait_ge(y_sq, DK * b + m + 1)
                        dve.wait_ge(y_acc, DK * b + 1 + m)
                        dve.tensor_tensor(acc[:, :], acc[:, :], sq[:, j, :], ALU.add).then_inc(y_acc, 1)

            dve.memset(ones[:, :], 1.0).then_inc(consts_ready, 1)
            split_chunk(0, 0)
            dve.wait_ge(const_in, 32)
            for k in range(DK):
                dve.wait_ge(xt_ready, k + 1)
                dve.tensor_copy(x[:, k, :], free_banks[k % len(free_banks)][:, 0:TOK]).then_inc(x_new, 1)
                if k > 0:
                    lo_x(0, k - 1)
            lo_x(0, DK - 1)
            split_next(1)
            for b, (kind, layer, which) in enumerate(plan):
                n0, T0, last = chunk0[b], tile0[b], b == len(plan) - 1
                if kind == "ffn":
                    f0 = ff0[b]

                    def gate(it, first):
                        dve.wait_ge(w_used, n0 + 2 * it + 1)
                        for j in range(2):
                            if not first:
                                dve.wait_ge(prod_ready, f0 + 2 * it + j - 1)
                            dve.tensor_tensor(h_gate[:, j, :], proj[j][:, 0:TOK], r_pre[:, :], ALU.mult)\
                               .then_inc(tile_out, 1)

                    def product(it, first):
                        T, f = T0 + 4 * it + 2, f0 + 2 * it
                        dve.wait_ge(w_used, n0 + 2 * it + 2)
                        for j in range(2):
                            if not first:
                                dve.wait_ge(h_lo, f + j - 1)
                            dve.tensor_tensor(h_up[:, j, :], proj[2 + j][:, 0:TOK], r_pre[:, :], ALU.mult)\
                               .then_inc(tile_out, 1)
                        for j in range(2):
                            dve.wait_ge(tile_out, T + j + 1)
                            dve.wait_ge(silu_ready, f + j + 1)
                            dve.tensor_tensor(h_up[:, j, :], h_up[:, j, :], h_gate[:, j, :], ALU.mult)\
                               .then_inc(prod_ready, 1)

                    pre_acc(b)
                    mean(stat0[b], D)
                    split_chunk(n0 + 2, 0)
                    dve.wait_ge(pre_read, b + 1)
                    gate(0, b == 0)
                    product(0, b == 0)
                    split_chunk(n0 + 3, 1)
                    gate(1, False)
                    split_chunk(n0 + 4, 0)
                    with dve.Fori(2, FF // WIDE) as it:
                        product(it - 1, False)
                        split_chunk(n0 + 2 * it + 1, 1)
                        gate(it, False)
                        split_chunk(n0 + 2 * it + 2, 0)
                    product(FF // WIDE - 1, False)
                    output(b, n0 + 2 * FF // WIDE, DOWN_STEPS)
                if kind == "gla":
                    dve.wait_ge(small_in, 64)
                    dve.memset(scores[:, :], 0.0).then_inc(scores_out, 1)
                    dve.wait_ge(wz_split, 1)
                    dve.tensor_tensor(wz_lo[:, :, :], wz[:, :, :], wz_hi[:, :, :].bitcast(F32), ALU.subtract)\
                       .then_inc(wz_split, 1)
                    pre_acc(b)
                    mean(stat0[b], D)
                    split_chunk(n0 + 2, 0)
                    dve.wait_ge(pre_read, b + 1)
                    dve.wait_ge(z_mm, 1)
                    dve.wait_ge(z_out, 1)
                    dve.tensor_tensor(z_cols[0:RANK, :], banks[7][0:RANK, 0:TOK], r_pre[0:RANK, :], ALU.mult)\
                       .then_inc(z_out, 1)
                    dve.wait_ge(rstd_ready, stat0[b] + 1)

                    def evac_qk(i):
                        dve.wait_ge(w_used, n0 + i + 1)
                        which_qk, at = divmod(i, Q_CHUNKS)
                        for j in range(2):
                            dve.scalar_tensor_tensor(qk[:, 2 * at + j, which_qk, :], proj[2 * (i % 2) + j][:, 0:TOK],
                                                     (DH ** -0.5, 1.0)[which_qk], r_pre[:, :], ALU.mult, ALU.mult)\
                               .then_inc(tile_out, 1)

                    def evac_v(h):
                        dve.wait_ge(w_used, n0 + 2 * Q_CHUNKS + h + 1)
                        for t in range(NT):
                            dve.tensor_scalar(v_rows[:, t, h * DV:(h + 1) * DV], proj[(NT * h + t) % NPROJ][:, 0:DV],
                                              rstd[:, 0, t:t + 1], None, ALU.mult).then_inc(tile_out, 1)

                    evac_qk(0)
                    split_chunk(n0 + 3, 1)
                    evac_qk(1)
                    split_chunk(n0 + 4, 0)
                    evac_qk(2)
                    for t in range(NT):
                        dve.wait_ge(g_log, t + 1)
                        dve.scalar_tensor_tensor(log_g_rows[:, t, :], banks[5 + t][:, :], 0.0, log_g_rows[:, t, :],
                                                 ALU.min, ALU.subtract).then_inc(g_done, 1)
                    split_chunk(n0 + 5, 1)
                    evac_qk(3)
                    evac_v(0)
                    split_chunk(n0 + 6, 0)
                    dve.wait_ge(z_mm, 3)
                    for t in range(NT):
                        dve.tensor_copy(b_cum[:, :, t * P:(t + 1) * P],
                                        banks[5 + t][:, :].rearrange("p (h t) -> p h t", h=HEADS))\
                           .then_inc(b_copied, 1)
                    dve.wait_ge(b_copied, NT)
                    for at, size, span in ((0, seq, GCH), (seq, P, dec_seq)):
                        cut = lambda buf: buf[:, :, at:at + size].rearrange("p h (c l) -> p h c l", l=span)
                        dve.tensor_tensor(cut(k_dec), cut(b_cum)[:, :, :, span - 1:span].to_broadcast(
                                              [P, HEADS, size // span, span]), cut(b_cum), ALU.subtract)\
                           .then_inc(b_diff, 1)
                    evac_v(1)
                    dve.wait_ge(d_exp, 1)
                    for h in range(HEADS):
                        dve.tensor_tensor(k_dec[:, h, :], k_dec[:, h, :], qk[:, h, 1, :], ALU.mult)\
                           .then_inc(k_decayed, 1)
                    split_chunk(n0 + 7, 1)
                    evac_v(2)
                    dve.wait_ge(b_exp, 2 * NT)
                    for h in range(HEADS):
                        dve.tensor_tensor(qk[:, h, 0, :], qk[:, h, 0, :], e_pos[:, h, :], ALU.mult)
                        dve.tensor_tensor(qk[:, h, 1, :], qk[:, h, 1, :], e_neg[:, h, :], ALU.mult)\
                           .then_inc(qk_ready, 1)
                    split_chunk(n0 + 8, 0)
                    evac_v(3)

                    def evac_r(h, i):
                        dve.tensor_tensor(r_silu[:, VT * h + i, :], proj[i][:, 0:TOK], r_pre[:, :], ALU.mult)\
                           .then_inc(tile_out, 1)

                    def gate_o(h):
                        dve.wait_ge(factor_ready, stat0[b] + 2 + h)
                        dve.wait_ge(o_out, VT * (h + 1))
                        dve.wait_ge(r_silu_done, VT * (h + 1))
                        for i in range(VT):
                            dve.tensor_tensor(ot[:, i, :], ot[:, i, :], stat[:, 0:TOK], ALU.mult)\
                               .then_inc(o_scaled, 1)
                        for i in range(VT):
                            dve.wait_ge(o_scaled, VT * h + i + 1)
                            dve.tensor_tensor(ot[:, i, :], ot[:, i, :], r_silu[:, VT * h + i, :], ALU.mult)\
                               .then_inc(o_gated, 1)
                        for i in range(VT):
                            dve.wait_ge(o_hi, VT * h + i + 1)
                            dve.tensor_tensor(olo[:, VT * h + i, :], ot[:, i, :], ohi[:, VT * h + i, :].bitcast(F32),
                                              ALU.subtract).then_inc(o_lo, 1)

                    for h in range(HEADS):
                        dve.wait_ge(scores_mm, h + 1)
                        if h == 0:
                            dve.wait_ge(scores_out, 1)
                        for t in range(NT):
                            cols = slice(t * P, (t + 1) * P)
                            dve.copy_predicated(scores[:, cols], tri_tok[t].bitcast(U32), banks[2][:, cols])\
                               .then_inc(scores_out, 1)
                        dve.wait_ge(tile_out, T0 + R_TILE)
                        for i in range(2):
                            dve.tensor_scalar(v_pair[:, i, :], v_rows[:, NP, h * DV:(h + 1) * DV],
                                              pair_mask[:, i:i + 1], None, ALU.mult).then_inc(vp_done, 1)
                        for c in range(seq // GCH):
                            product = banks[7 if c % 2 == 0 else 2][:, c // 2 * DV:(c // 2 + 1) * DV]
                            dve.wait_ge(kv_mm, 2 * h + 1 + c % 2)
                            if c == 0:
                                if h > 0:
                                    dve.wait_ge(sp_stored, 16 * h)
                                dve.tensor_copy(s_prompt[:, 0, :], product).then_inc(s_done, 1)
                            else:
                                dve.wait_ge(s_done, seq // GCH * h + c)
                                dve.scalar_tensor_tensor(s_prompt[:, c, :], s_prompt[:, c - 1, :],
                                                         e_pos[:, h, (c + 1) * GCH - 1:(c + 1) * GCH], product,
                                                         ALU.mult, ALU.add).then_inc(s_done, 1)
                        evac_r(h, 0)
                        split_chunk(n0 + R_AT + h + 1, (h + 1) % 2)
                        if h > 0:
                            gate_o(h - 1)
                        dve.wait_ge(o_sq, VT * (h + 1))
                        dve.tensor_tensor(acc[:, :], sq[:, 0, :], sq[:, 1, :], ALU.add).then_inc(o_acc, 1)
                        for c in range(dec_batch):
                            dve.wait_ge(dec_mm, dec_batch // 2 * h + c // 2 + 1)
                            last_token = seq + (c + 1) * dec_seq - 1
                            state = s0[:, h % 2, c, :]
                            dve.scalar_tensor_tensor(state, state, e_pos[:, h, last_token:last_token + 1],
                                                     banks[DEC_BANKS[c // 2]][:, c % 2 * DV:(c % 2 + 1) * DV],
                                                     ALU.mult, ALU.add).then_inc(dec_done, 1)
                        mean(stat0[b] + 1 + h, DV)
                        dve.wait_ge(w_used, n0 + R_AT + h + 1)
                        evac_r(h, 1)
                    split_chunk(n0 + OUT_AT + 1, 1)
                    gate_o(HEADS - 1)
                    output(b, n0 + OUT_AT, 1, started=True)
                if kind == "sgu":
                    def v_evac(i):
                        dve.wait_ge(rows_in[i % 2], 16 * (i // 2 + 1))
                        dve.wait_ge(w_used, n0 + i + 1)
                        for t in range(NT):
                            bank = banks[4 + t] if i == 1 and t > 0 else proj[(NT * i + t) % NPROJ]
                            dve.scalar_tensor_tensor(v_at(i, t), bank[:, 0:WIDE],
                                                     rstd[:, 0, t:t + 1], feat_rows[:, i % 2, 0, :],
                                                     ALU.mult, ALU.add).then_inc(tile_out, 1)

                    def v_stats(i):
                        for t in range(NT):
                            dve.wait_ge(v_act, NT * i + t + 1)
                            dve.bn_stats(ln_stats[:, t, i, :], v_at(i, t)).then_inc(v_stat, 1)

                    def normalise(i):
                        for t in range(NT):
                            dve.tensor_scalar(v_at(i, t), v_at(i, t), ln_mean_var[:, t, 0:1], ln_rstd[:, t:t + 1],
                                              ALU.subtract, ALU.mult).then_inc(ln_norm, 1)

                    def u_product(i):
                        for j in range(2):
                            dve.wait_ge(u_act, 2 * i + j + 1)
                            dve.wait_ge(mix_out, 4 * i + 2 * j + 2)
                            dve.tensor_tensor(u_tile[:, j, :], u_tile[:, j, :], mixed[:, j, :], ALU.mult)\
                               .then_inc(u_prod, 1)

                    pre_acc(b)
                    split_chunk(n0 + 2, 0)
                    mean(stat0[b], D)
                    dve.wait_ge(rstd_ready, stat0[b] + 1)
                    v_evac(0)
                    for i in range(1, V_CHUNKS):
                        if i > 1:
                            split_chunk(n0 + i + 1, (i + 1) % 2)
                        v_evac(i)
                        if i == 3:
                            dve.wait_ge(ws_mm, 1)
                            for w, mask in enumerate((ident_tri[:, 1:2, :], ident_tri[:, 3:4, :])):
                                product = banks[5 + w][:, :].rearrange("p (g t) -> p g t", g=SPATIAL)
                                dve.tensor_tensor(w_turned[:, w], product, mask.to_broadcast([P, SPATIAL, P]),
                                                  ALU.mult).then_inc(ws_done, 1)
                        v_stats(i - 1)
                    v_stats(V_CHUNKS - 1)
                    dve.wait_ge(v_stat, NT * V_CHUNKS)
                    for t in range(NT):
                        dve.bn_aggr(ln_mean_var[:, t, :], ln_stats[:, t].rearrange("p c s -> p (c s)"))\
                           .then_inc(ln_aggr, 1)
                    dve.wait_ge(ln_aggr, NT)
                    dve.tensor_scalar(ln_var[:, :], ln_mean_var[:, :, 1], LN_EPS, None, ALU.add).then_inc(ln_eps, 1)
                    dve.wait_ge(ln_pow, 1)
                    normalise(0)
                    dve.wait_ge(ws_in, 16 * (dec_batch + 2))
                    for i in range(V_CHUNKS):
                        if i > 0:
                            u_product(i - 1)
                        split_chunk(n0 + V_CHUNKS + i + 1, (i + 1) % 2)
                        if i + 1 < V_CHUNKS:
                            normalise(i + 1)
                        dve.wait_ge(mix_mm, i + 1)
                        if i > 0:
                            dve.wait_ge(u_prod, 2 * i)
                        for j in range(2):
                            g = (2 * i + j) * SPATIAL // (HALF // P)
                            for at, size, span in ((0, seq, P), (seq, P, dec_seq)):
                                cut = lambda buf: buf.rearrange("p (c l) -> p c l", l=span)
                                dve.tensor_tensor(cut(mixed[:, j, at:at + size]), cut(banks[5 + j][:, at:at + size]),
                                                  b_spatial[:, g:g + 1, 0:span].to_broadcast([P, size // span, span]),
                                                  ALU.add).then_inc(mix_out, 1)
                        dve.wait_ge(w_used, n0 + V_CHUNKS + i + 1)
                        for j in range(2):
                            if i > 0:
                                dve.wait_ge(u_lo, 2 * i + j - 1)
                            dve.tensor_tensor(u_tile[:, j, :], proj[2 * (i % 2) + j][:, 0:TOK], r_pre[:, :], ALU.mult)\
                               .then_inc(tile_out, 1)
                    u_product(V_CHUNKS - 1)
                    output(b, n0 + 2 * V_CHUNKS, SGU_STEPS)
                s = stat0[b + 1] - 1
                mean(s, D, 0.5 if kind == "ffn" else 1.0)
                if last:
                    dve.wait_ge(rstd_ready, s + 1)
                    dve.wait_ge(x_rows_out, 2 * NT)
                    for half in range(2):
                        dve.wait_ge(turned, 3 + half)
                        for t in range(NT):
                            rows = y_rows[:, t, half * BANK:(half + 1) * BANK]
                            dve.scalar_tensor_tensor(rows, (row_banks, proj)[half][t][:, :], rstd[:, 1, t:t + 1], rows,
                                                     ALU.mult, ALU.add).then_inc(y_ready, 1)
                    continue
                dve.wait_ge(factor_ready, s + 1)
                dve.tensor_tensor(yg[:, 0, :], yg[:, 0, :], stat[:, 0:TOK], ALU.mult).then_inc(y_scaled, 1)
                for k in range(DK):
                    if k < 2:
                        dve.wait_ge(y_scaled, 2 * b + k + 1)
                    else:
                        dve.wait_ge(y_scaled_pool, (DK - 2) * b + k - 1)
                    dve.tensor_tensor(x[:, k, :], x[:, k, :], yg[:, k, :], ALU.add).then_inc(x_new, 1)
                    if k == 0:
                        dve.wait_ge(post_read, b + 1)
                        dve.tensor_tensor(yg[:, 1, :], yg[:, 1, :], acc[:, :], ALU.mult).then_inc(y_scaled, 1)
                    if k != 1:
                        lo_x(b + 1, max(k - 1, 0))
                lo_x(b + 1, DK - 1)

        @block.gpsimd
        def _(pool):
            def power(s, buf):
                pool.wait_ge(mean_ready, s + 1)
                pool.tensor_tensor(rstd[:, buf, :], mean_sq[:, :], minus_half[:, :].to_broadcast([P, NT]), ALU.pow)\
                    .then_inc(rstd_ready, 1)

            def pre_acc(b):
                for k in (0, 2):
                    pool.wait_ge(x_sq, DK * b + k + 2)
                    pool.tensor_tensor(yg[:, k, :], yg[:, k, :], yg[:, k + 1, :], ALU.add).then_inc(x_acc_pool, 1)
                power(stat0[b], 0)

            pool.memset(minus_half[:, :], -0.5).then_inc(consts_ready, 1)
            pool.wait_ge(consts_ready, 2)

            for b, (kind, layer, which) in enumerate(plan):
                if kind == "gla":
                    def load_s0(h):
                        pool.dma_start(s0[:, h % 2], a["state_gla"][layer // 2, :, h].rearrange("b p v -> p b v"))\
                            .then_inc(s0_in[h % 2], 16)

                    j = layer // 2
                    pool.wait_ge(x_new, DK * b + 1)
                    with nc.allow_non_contiguous_dma(reason="16 columns of w_in"):
                        pool.dma_start(wz[:, :, :], a["gla_w_in"][j].rearrange("(k p) c -> p k c", p=P)[
                            :, :, OUT_AT * WIDE:OUT_AT * WIDE + RANK]).then_inc(gla_in, 16)
                    pool.dma_start(w_gate2[0:RANK, :], a["gla_w_gate2"][j]).then_inc(gla_in, 16)
                    pool.dma_start(w_gate2[RANK:RANK + 1, :], a["gla_b_gate"][j:j + 1]).then_inc(gla_in, 16)
                    pool.memset(z_cols[:, :], 1.0).then_inc(z_out, 1)
                    pre_acc(b)
                    load_s0(0)
                    load_s0(1)
                if kind == "sgu":
                    j = layer // 2

                    def load_bias(i):
                        pool.dma_start(feat_rows[:, i % 2, 0, :], a["sgu_b_in"][j:j + 1, HALF + i * WIDE:
                                       HALF + (i + 1) * WIDE].to_broadcast([P, WIDE])).then_inc(rows_in[i % 2], 16)

                    pool.wait_ge(x_new, DK * b + 1)
                    pool.memset(w_rows[:, 1], 0.0).then_inc(ws_zero, 1)
                    load_bias(0)
                    load_bias(1)
                    pre_acc(b)
                if kind == "ffn":
                    pre_acc(b)
                    with pool.Fori(0, FF // WIDE) as it:
                        for j in range(2):
                            pool.wait_ge(h_hi, ff0[b] + 2 * it + j + 1)
                            at = bass.ds(2 * it + j, 1)
                            pool.tensor_tensor(hlo[:, at, :], h_up[:, j:j + 1, :], hhi[:, at, :].bitcast(F32),
                                               ALU.subtract).then_inc(h_lo, 1)
                if kind == "gla":
                    for h in range(HEADS):
                        power(stat0[b] + 1 + h, 1)
                        pool.wait_ge(dec_done, dec_batch * (h + 1))
                        pool.wait_ge(s_done, seq // GCH * (h + 1))
                        pool.dma_start(outs["gla_state_prompt"][layer // 2, 0, h], s_prompt[:, seq // GCH - 1, :])\
                            .then_inc(sp_stored, 16)
                        pool.dma_start(outs["gla_state_sample"][layer // 2, :, h].rearrange("b p v -> p b v"),
                                       s0[:, h % 2]).then_inc(s0_stored[h % 2], 16)
                        if h + 2 < HEADS:
                            pool.wait_ge(s0_stored[h % 2], 16)
                            load_s0(h + 2)
                    pool.wait_ge(sp_stored, 16 * HEADS)
                    for i in range(2):
                        pool.wait_ge(s0_stored[i], 16 * HEADS // 2)
                if kind == "sgu":
                    def load_ln(i):
                        for which_row, name in enumerate(("sgu_ln_g", "sgu_ln_b")):
                            pool.dma_start(feat_rows[:, i % 2, which_row, :], a[name][j:j + 1, i * WIDE:(i + 1) * WIDE]
                                           .to_broadcast([P, WIDE])).then_inc(rows_in[i % 2], 16)

                    def affine(i):
                        at = i % PER_SET * WIDE
                        v = v_set[i // PER_SET][:, :, at:at + WIDE]
                        pool.wait_ge(rows_in[i % 2], 16 * (V_CHUNKS // 2 + 2 * (i // 2 + 1)))
                        pool.wait_ge(ln_norm, NT * (i + 1))
                        pool.tensor_tensor(v, v, feat_rows[:, i % 2, 0:1, :].to_broadcast([P, NT, WIDE]), ALU.mult)\
                            .then_inc(ln_gain, 1)
                        pool.wait_ge(ln_gain, i + 1)
                        pool.tensor_tensor(v, v, feat_rows[:, i % 2, 1:2, :].to_broadcast([P, NT, WIDE]), ALU.add)\
                            .then_inc(ln_done, 1)
                        pool.wait_ge(ln_done, i + 1)
                        if i == 1:
                            load_ln(2)
                            load_ln(3)
                        if 1 < i < V_CHUNKS - 2:
                            load_ln(i + 2)
                        if i % PER_SET == PER_SET - 1:
                            at = i // PER_SET * KT * P
                            pool.dma_start(outs["sgu_v_sample"][j].rearrange("b l c -> (b l) c")[:, at:at + KT * P],
                                           v_set[i // PER_SET][:, NP, :]).then_inc(v_stored, 16)

                    for i in range(2, V_CHUNKS):
                        pool.wait_ge(tile_out, tile0[b] + NT * (i - 1))
                        load_bias(i)
                    for i in range(2):
                        pool.wait_ge(tile_out, tile0[b] + NT * (V_CHUNKS - 1 + i))
                        load_ln(i)
                    pool.wait_ge(ln_eps, 1)
                    pool.tensor_tensor(ln_rstd[:, :], ln_var[:, :], minus_half[:, :].to_broadcast([P, NT]), ALU.pow)\
                        .then_inc(ln_pow, 1)
                    affine(0)
                    for i in range(V_CHUNKS):
                        if i + 1 < V_CHUNKS:
                            affine(i + 1)
                        for c in (2 * i, 2 * i + 1):
                            if c == KT:
                                pool.wait_ge(mix_mm, PER_SET)
                                pool.wait_ge(v_stored, 16)
                            if c == 2 * KT:
                                pool.wait_ge(mix_mm, 2 * PER_SET)
                                pool.wait_ge(v_stored, 32)
                            pool.wait_ge(u_hi, c + 1)
                            pool.tensor_tensor(ulo[c // KT][:, c % KT, :], u_tile[:, c % 2, :],
                                               uhi[c // KT][:, c % KT, :].bitcast(F32), ALU.subtract)\
                                .then_inc(u_lo, 1)
                    pool.wait_ge(v_stored, 48)
                power(stat0[b + 1] - 1, 1)
                if b + 1 == len(plan):
                    continue
                pool.wait_ge(post_read, b + 1)
                pool.wait_ge(tile_out, tile0[b + 1])
                for k in range(2, DK):
                    pool.tensor_tensor(yg[:, k, :], yg[:, k, :], acc[:, :], ALU.mult).then_inc(y_scaled_pool, 1)

        @block.tensor
        def _(pe):
            def multiply(out, slot, k, j, rhs_hi, rhs_lo, start, stop):
                cols = slice(j * P, (j + 1) * P)
                w_hi_part, w_lo_part = weights[slot]
                pe.matmul(out, w_hi_part[:, k, cols], rhs_hi, start=start, stop=False)
                pe.matmul(out, w_hi_part[:, k, cols], rhs_lo, start=False, stop=False)
                return pe.matmul(out, w_lo_part[:, k, cols], rhs_hi, start=False, stop=stop)

            def sums(part, last=None, ready=0):
                for t in range(NT):
                    mm = pe.matmul(stat[:, TOK + t:TOK + t + 1], part[:, t * P:(t + 1) * P], ones[:, 0:1],
                                   start=t == 0, stop=last is None, skip_group_check=True)
                if last is not None:
                    pe.wait_ge(y_sq, ready)
                    for t in range(NT):
                        mm = pe.matmul(stat[:, TOK + t:TOK + t + 1], last[:, t * P:(t + 1) * P], ones[:, 0:1],
                                       start=False, stop=t == NT - 1, skip_group_check=True)
                mm.then_inc(sums_ready, 1)

            def factors(s, buf):
                pe.wait_ge(rstd_ready, s + 1)
                for t in range(NT):
                    mm = pe.transpose(stat[:, t * P:(t + 1) * P], rstd[:, buf, t:t + 1].to_broadcast([P, P]), ident)
                mm.then_inc(factor_ready, 1)

            def multiply_rows(out, slot, k, t, start, stop):
                cols = slice(t * P, (t + 1) * P)
                w_hi_part, w_lo_part = weights[slot]
                pe.matmul(out, xhi[:, k, cols], w_hi_part[:, k, :], start=start, stop=False)
                pe.matmul(out, xhi[:, k, cols], w_lo_part[:, k, :], start=False, stop=False)
                return pe.matmul(out, xlo[:, k, cols], w_hi_part[:, k, :], start=False, stop=stop)

            def first_chunk(b):
                pe.wait_ge(w_lo, chunk0[b] + 1)
                if b > 0:
                    pe.wait_ge(tile_out, tile0[b])
                for k in range(KT):
                    pe.wait_ge(x_hi, DK * b + k + 1)
                    for lo_ready in (False, True):
                        if lo_ready:
                            pe.wait_ge(x_lo, DK * b + k + 1)
                        for j in range(NT if plan[b][0] == "sgu" else 2):
                            cols = slice(j * P, (j + 1) * P)
                            if plan[b][0] == "sgu":
                                if lo_ready:
                                    passes = [(xlo[:, k, cols], whi[:, 0, k, :])]
                                else:
                                    passes = [(xhi[:, k, cols], w[:, 0, k, :]) for w in (whi, wlo)]
                                out = proj[j][:, 0:WIDE]
                            else:
                                if lo_ready:
                                    passes = [(whi[:, 0, k, cols], xlo[:, k, :])]
                                else:
                                    passes = [(w[:, 0, k, cols], xhi[:, k, :]) for w in (whi, wlo)]
                                out = proj[j][:, 0:TOK]
                            for i, (stationary, moving) in enumerate(passes):
                                mm = pe.matmul(out, stationary, moving, start=k == 0 and not lo_ready and i == 0,
                                               stop=k == KT - 1 and lo_ready)
                mm.then_inc(w_used, 1)

            def keep_busy(products):
                for _ in range(products):
                    pe.matmul(banks[5][:, 0:P], ones[:, :], ones[:, :], start=True, stop=True)

            def pre_sums(b):
                pe.wait_ge(x_acc, 3 * (b + 1))
                if b > 0:
                    pe.wait_ge(post_read, b)
                sums(yg[:, 4, :])

            def tile(bank, slot, j, midway=None, before=lambda k: None):
                for k in range(KT):
                    if midway and k == KT // 2:
                        midway()
                    before(k)
                    mm = multiply(proj[bank][:, 0:TOK], slot, k, j, xhi[:, k, :], xlo[:, k, :], k == 0, k == KT - 1)
                return mm

            def turn(src, half, out):
                for t in range(NT):
                    for k in range(DK // 2):
                        mm = pe.transpose(out[t][:, k * P:(k + 1) * P],
                                          src[:, half * DK // 2 + k, t * P:(t + 1) * P], ident)
                mm.then_inc(turned, 1)

            def output(b, n1, T1, steps, rhs, in_order=False):
                def group(q, parity):
                    if in_order and q == 0:
                        pe.wait_ge(tile_out, T1)
                        pe.wait_ge(w_lo, n1 + 1)
                        for k in range(KT):
                            if k == KT // 2:
                                factors(stat0[b] + HEADS, 1)
                            pe.wait_ge(rhs(0)[2], k + 1)
                            for j in range(2):
                                mm = multiply(proj[j][:, 0:TOK], 0, k, j, rhs(0)[0][:, k, :], rhs(0)[1][:, k, :],
                                              k == 0, k == KT - 1)
                                if k == KT - 1:
                                    mm.then_inc((y_first, w_used)[j], 1)
                        return
                    pe.wait_ge(tile_out, T1 + 2 * q - 2)
                    for step in range(steps):
                        n = n1 + q * steps + step
                        pe.wait_ge(w_lo, n + 1)
                        ready, count = rhs(step)[2:]
                        if not in_order:
                            pe.wait_ge(ready, count)
                        for j in range(2):
                            for k in range(KT):
                                hi, lo = rhs(step)[:2]
                                mm = multiply(proj[2 * parity + j][:, 0:TOK], (steps * parity + step) % 2, k, j,
                                              hi[:, k, :], lo[:, k, :], step == k == 0,
                                              step == steps - 1 and k == KT - 1)
                            if j == 0 and step == steps - 1:
                                mm.then_inc(y_first, 1)
                        mm.then_inc(w_used, 1)
                        if (b, q) == (len(plan) - 1, QUARTERS - 1) and step < 3:
                            if step > 0:
                                pe.wait_ge(x_rows_out, NT * step)
                            turn((x, x, yg)[step], step % 2, row_banks)
                if in_order or b == len(plan) - 1:
                    for q in range(QUARTERS):
                        group(q, q % 2)
                else:
                    with pe.Fori(0, QUARTERS // 2) as it:
                        for parity in range(2):
                            group(2 * it + parity, parity)
                pe.wait_ge(y_acc, DK * (b + 1))
                pe.wait_ge(pre_read, b + 1)
                if kind == "gla":
                    pe.wait_ge(o_scaled, HEADS * VT)
                sums(acc, sq[:, 1, :], DK * (b + 1))
                if b + 1 < len(plan):
                    keep_busy(5)
                    factors(stat0[b + 1] - 1, 1)
                    keep_busy(8)
                else:
                    pe.wait_ge(tile_out, tile0[b + 1])
                    turn(yg, 1, proj)

            pe.wait_ge(consts_ready, 2)
            pe.wait_ge(const_in, 32)
            for k in range(DK):
                if k % (DK // 2) == 0:
                    pe.wait_ge(x_in[2 * k // DK], 32)
                if k >= len(free_banks):
                    pe.wait_ge(x_new, k - len(free_banks) + 1)
                out = free_banks[k % len(free_banks)]
                for t in range(NT):
                    last = pe.transpose(out[:, t * P:(t + 1) * P], x_rows[:, t, k * P:(k + 1) * P], ident)
                last.then_inc(xt_ready, 1)
            for b, (kind, layer, which) in enumerate(plan):
                n0, T0 = chunk0[b], tile0[b]
                first_chunk(b)
                if kind == "ffn":
                    pe.wait_ge(w_lo, n0 + 2)
                    tile(2, NEXT, 0)
                    pre_sums(b)
                    tile(3, NEXT, 1, lambda: factors(stat0[b], 0)).then_inc(w_used, 1)
                    with pe.Fori(1, FF // WIDE) as it:
                        for slot in range(2):
                            pe.wait_ge(w_lo, n0 + 2 * it + slot + 1)
                            pe.wait_ge(tile_out, T0 + 4 * it + 2 * slot - 2)
                            tile(2 * slot, slot, 0)
                            tile(2 * slot + 1, slot, 1).then_inc(w_used, 1)
                    output(b, n0 + 2 * FF // WIDE, T0 + 2 * FK, DOWN_STEPS,
                           lambda step: (hhi[:, KT * step:KT * (step + 1), :], hlo[:, KT * step:KT * (step + 1), :],
                                         h_lo, ff0[b] + KT * (step + 1)))
                if kind == "gla":
                    def x_tile(i, j, *amid):
                        return tile(2 * (i % 2 if i < 2 * Q_CHUNKS else 0) + j, i % 2, j, *amid)

                    def v_chunk(h, after_first=None):
                        i = 2 * Q_CHUNKS + h
                        pe.wait_ge(w_lo, n0 + i + 1)
                        for t in range(NT):
                            T = T0 + V_TILE + NT * h + t
                            pe.wait_ge(tile_out, T - NPROJ + 1)
                            out = proj[(NT * h + t) % NPROJ][:, 0:DV]
                            for k in range(KT):
                                mm = multiply_rows(out, i % 2, k, t, k == 0, k == KT - 1)
                            if t == 0 and after_first:
                                after_first()
                        mm.then_inc(w_used, 1)

                    pe.wait_ge(w_lo, n0 + 2)
                    tile(2, NEXT, 0)
                    pe.wait_ge(wz_split, 2)
                    z = banks[7][0:RANK, 0:TOK]
                    for k in range(KT):
                        pe.matmul(z, wz_hi[:, k, :], xhi[:, k, :], start=k == 0, stop=False)
                        pe.matmul(z, wz_hi[:, k, :], xlo[:, k, :], start=False, stop=False)
                        mm = pe.matmul(z, wz_lo[:, k, :], xhi[:, k, :], start=False, stop=k == KT - 1)
                    mm.then_inc(z_mm, 1)
                    pre_sums(b)
                    tile(3, NEXT, 1, lambda: factors(stat0[b], 0)).then_inc(w_used, 1)
                    pe.wait_ge(w_lo, n0 + 3)
                    pe.wait_ge(tile_out, T0 + 2)
                    x_tile(2, 0)
                    pe.wait_ge(z_out, 2)
                    pe.wait_ge(gla_in, 48)
                    for t in range(NT):
                        mm = pe.matmul(banks[5 + t][:, :], z_cols[0:RANK + 1, t * P:(t + 1) * P],
                                       w_gate2[:, :], start=True, stop=True)
                    mm.then_inc(z_mm, 1)
                    x_tile(2, 1).then_inc(w_used, 1)
                    pe.wait_ge(w_lo, n0 + 4)
                    pe.wait_ge(tile_out, T0 + 4)
                    x_tile(3, 0)
                    x_tile(3, 1).then_inc(w_used, 1)
                    v_chunk(0)

                    def cumulate():
                        pe.wait_ge(g_done, NT)
                        for t in range(NT):
                            for h in range(HEADS):
                                mm = pe.matmul(banks[5 + t][:, h * P:(h + 1) * P],
                                               log_g_rows[:, t, h * P:(h + 1) * P], tri_tok[t], start=True, stop=True)
                        mm.then_inc(z_mm, 1)

                    for h in range(1, HEADS):
                        v_chunk(h, cumulate if h == 1 else None)
                    pe.wait_ge(b_copied, NT)
                    for h in range(HEADS):
                        s = stat0[b] + 1 + h
                        q_h, k_h, v_h = qk[:, h, 0, :], qk[:, h, 1, :], v_rows[:, :, h * DV:(h + 1) * DV]

                        def scores_and_keys():
                            pe.wait_ge(qk_ready, h + 1)
                            pe.wait_ge(tile_out, T0 + R_TILE + VT * h)
                            if h > 0:
                                pe.wait_ge(dec_done, dec_batch * h)
                            for t in range(NT):
                                cols = slice(t * P, (t + 1) * P)
                                mm = pe.matmul(banks[2][:, cols], k_h[:, cols], q_h[:, cols], start=True, stop=True)
                            mm.then_inc(scores_mm, 1)
                            pe.wait_ge(k_decayed, h + 1)
                            for t in range(NT):
                                cols = slice(t * P, (t + 1) * P)
                                mm = pe.transpose(banks[3][:, cols], k_dec[:, h, cols], ident)
                            mm.then_inc(k_turned, 1)

                        pe.wait_ge(w_lo, n0 + R_AT + h + 1)
                        pe.wait_ge(tile_out, T0 + R_TILE + VT * h - (1 if h > 0 else NT))
                        x_tile(R_AT + h, 0, scores_and_keys)
                        if h > 0:
                            factors(s - 1, 1)
                        pe.wait_ge(k_out, h + 1)
                        pe.wait_ge(scores_out, 1 + NT * (h + 1))
                        for c in (0, 2, 1, 3):
                            rows, t = slice(c % 2 * GCH, (c % 2 + 1) * GCH), c // 2
                            mm = pe.matmul(banks[7 if c % 2 == 0 else 2][:, t * DV:(t + 1) * DV],
                                           k_rows[rows, t * P:(t + 1) * P], v_h[rows, t, :], start=True, stop=True)
                            if t == 1:
                                mm.then_inc(kv_mm, 1)
                        if h > 0:
                            pe.wait_ge(o_out, VT * h)
                        pe.wait_ge(s0_in[h % 2], 16 * (h // 2 + 1))
                        for i in range(VT):
                            for t in range(NT):
                                cols = slice(t * P, (t + 1) * P)
                                pe.matmul(banks[5 + i][:, cols], v_h[:, t, i * P:(i + 1) * P], scores[:, cols],
                                          start=t == 0, stop=False, skip_group_check=True)

                        def amid(k):
                            if k < KT // 2:
                                for c in (2 * k, 2 * k + 1):
                                    cols = slice(seq + c * dec_seq, seq + (c + 1) * dec_seq)
                                    for i in range(VT):
                                        pe.matmul(banks[5 + i][:, cols], s0[:, h % 2, c, i * P:(i + 1) * P],
                                                  q_h[:, cols], start=False, stop=False, skip_group_check=True)
                                return
                            j = k - KT // 2
                            if j == 0:
                                for c in range(1, seq // GCH):
                                    cols = slice(c * GCH, (c + 1) * GCH)
                                    pe.wait_ge(s_done, seq // GCH * h + c)
                                    for i in range(VT):
                                        mm = pe.matmul(banks[5 + i][:, cols], s_prompt[:, c - 1, i * P:(i + 1) * P],
                                                       q_h[:, cols], start=False, stop=c == seq // GCH - 1,
                                                       skip_group_check=True)
                                mm.then_inc(o_mm, 1)
                                pe.wait_ge(vp_done, 2 * (h + 1))
                                pe.wait_ge(s_done, seq // GCH * (h + 1))
                            if j == dec_batch // 2 - 1:
                                pe.wait_ge(dec_done, dec_batch * h + 2)
                            rows = slice(j * 2 * dec_seq, (j + 1) * 2 * dec_seq)
                            pe.matmul(banks[DEC_BANKS[j]][:, :], k_rows[rows, NP * P:TOK],
                                      v_pair[rows, :, :].rearrange("p i v -> p (i v)"), start=True, stop=True)\
                              .then_inc(dec_mm, 1)
                            if k == KT - 1:
                                pe.wait_ge(o_acc, h + 1)
                                if h > 0:
                                    pe.wait_ge(o_scaled, VT * h)
                                sums(acc)

                        x_tile(R_AT + h, 1, None, amid).then_inc(w_used, 1)
                    output(b, n0 + OUT_AT, T0 + R_TILE + HEADS * VT, 1, lambda step: (ohi, olo, o_lo, 0), True)
                if kind == "sgu":
                    def v_tile(i, parity4, t):
                        second = isinstance(i, int) and i == 1
                        if not (second and t > 0):
                            pe.wait_ge(tile_out, NT * i + (T0 + t - NPROJ + 1))
                        out = banks[4 + t] if second and t > 0 else proj[(NT * parity4 + t) % NPROJ]
                        for k in range(KT):
                            mm = multiply_rows(out[:, 0:WIDE], NEXT if second else parity4 % 2, k, t,
                                               k == 0, k == KT - 1)
                        return mm

                    for i in range(1, 4):
                        pe.wait_ge(w_lo, n0 + i + 1)
                        for t in range(NT):
                            mm = v_tile(i, i, t)
                            if i == 1 and t == 0:
                                pre_sums(b)
                        mm.then_inc(w_used, 1)
                        if i == 1:
                            factors(stat0[b], 0)
                        if i == 3:
                            pe.wait_ge(tile_out, T0 + 2 * NT)
                            pe.wait_ge(ws_in, 16 * (dec_batch + 2))
                            for which_w in range(2):
                                for g in range(SPATIAL):
                                    mm = pe.transpose(banks[5 + which_w][:, g * P:(g + 1) * P],
                                                      w_rows[:, which_w, g, :], ident)
                            mm.then_inc(ws_mm, 1)
                    with pe.Fori(1, V_CHUNKS // 4) as it:
                        for c in range(4):
                            pe.wait_ge(w_lo, n0 + 4 * it + c + 1)
                            for t in range(NT):
                                mm = v_tile(4 * it + c, c, t)
                            mm.then_inc(w_used, 1)
                    pe.wait_ge(ws_done, 2)

                    def mix(i):
                        pe.wait_ge(ln_done, i + 1)
                        if i > 0:
                            pe.wait_ge(mix_out, 4 * i)
                        for j in range(2):
                            g = (2 * i + j) * SPATIAL // (HALF // P)
                            for t in range(NT):
                                mm = pe.matmul(banks[5 + j][:, t * P:(t + 1) * P],
                                               v_at(i, t)[:, j * P:(j + 1) * P], w_turned[:, t // NP, g, :],
                                               start=True, stop=True)
                        mm.then_inc(mix_mm, 1)

                    for i in range(V_CHUNKS):
                        pe.wait_ge(w_lo, n0 + V_CHUNKS + i + 1)
                        pe.wait_ge(tile_out, T0 + U_TILE + 2 * i - 2)
                        tile(2 * (i % 2), i % 2, 0, (lambda: mix(0)) if i == 1 else None)
                        if i > 0:
                            mix(i)
                        tile(2 * (i % 2) + 1, i % 2, 1).then_inc(w_used, 1)
                    output(b, n0 + 2 * V_CHUNKS, T0 + SGU_OUT_TILE, SGU_STEPS,
                           lambda step: (uhi[step], ulo[step], u_lo, KT * (step + 1)))


def constants():
    import numpy as np

    s, t = np.arange(P)[:, None], np.arange(P)[None, :]
    upto = s <= t
    tri = np.stack([s == t, upto, upto & (s // 64 == t // 64), upto & (s // 16 == t // 16)], axis=1)
    odd = np.arange(P) // 16 % 2
    return {"ident_tri": tri.astype(np.float32), "pair_mask": np.stack([1 - odd, odd], axis=1).astype(np.float32)}


def laid_out(inputs):
    import numpy as np

    def columns(g):
        return np.ascontiguousarray(g.reshape(-1, P).T)

    return {"gain_pre": columns(inputs["norm_pre"]), "gain_post": columns(inputs["norm_post"]),
            "gain_head": columns(inputs["gla_norm"]), "u_bias": columns(inputs["sgu_b_in"])}


PLAN = [("ffn", 0, 0), ("gla", 0, 1), ("ffn", 0, 2), ("ffn", 1, 0), ("sgu", 1, 1), ("ffn", 1, 2)]


def kernel(**inputs):
    import numpy as np
    import concourse.bacc as bacc
    from concourse.bass_utils import run_bass_kernel_spmd

    nc = bacc.Bacc("TRN2", target_bir_lowering=False, num_devices=1)
    arrays = {name: np.ascontiguousarray(value) for name, value in inputs.items()}
    arrays.update(constants(), **laid_out(arrays))
    a = {name: nc.dram_tensor(name, value.shape, mybir.dt.from_np(value.dtype), kind="ExternalInput").ap()
         for name, value in arrays.items()}
    n_gla, dec_batch, heads, dk, dv = inputs["state_gla"].shape
    n_sgu, half = inputs["sgu_ln_g"].shape
    shapes = {"y_prompt": inputs["x_prompt"].shape, "y_sample": inputs["x_sample"].shape,
              "gla_state_prompt": (n_gla, inputs["x_prompt"].shape[0], heads, dk, dv),
              "gla_state_sample": inputs["state_gla"].shape,
              "sgu_v_sample": (n_sgu,) + inputs["x_sample"].shape[:2] + (half,)}
    outs = {name: nc.dram_tensor(name, shape, F32, kind="ExternalOutput").ap() for name, shape in shapes.items()}
    build_trunk(nc, a, outs, PLAN)
    result = run_bass_kernel_spmd(nc, [arrays], core_ids=[0])
    return tuple(result.results[0][name] for name in shapes)
```
